# Optimizing a Trainium2 kernel written in Bass

```python
import jax, jax.numpy as jnp
from jax import lax
import numpy as np
import jax
import jax.numpy as jnp

D_MODEL = 1024
BATCH = 1
SEQ = 1024
DEPTH = 1

CHUNK = 64
HEAD_DIM = 64
N_HEADS_A = 8
N_HEADS_B = 8
D_A = N_HEADS_A * HEAD_DIM
D_B = N_HEADS_B * HEAD_DIM
D_MIX = D_A + D_B
N_LEFT_CHUNKS = 8
BAND_CHUNKS = N_LEFT_CHUNKS + 1
REL_CLIP = 128
Q_BLOCK = 128
D_FF = 2816
CONV_WIDTH = 3
LN_EPS = 1e-5
DEEPNORM_ALPHA = (2.0 * DEPTH) ** 0.25
DEEPNORM_BETA = (8.0 * DEPTH) ** -0.25
PROJ_COLS = 3 * D_A + N_HEADS_A + 3 * D_B
SPLITS = (D_A, 2 * D_A, 3 * D_A, 3 * D_A + N_HEADS_A,
          3 * D_A + N_HEADS_A + D_B, 3 * D_A + N_HEADS_A + 2 * D_B)


def layer_norm(x, g, b):
    xf = x.astype(jnp.float32)
    mu = jnp.mean(xf, axis=-1, keepdims=True)
    var = jnp.mean(jnp.square(xf - mu), axis=-1, keepdims=True)
    y = (xf - mu) * lax.rsqrt(var + LN_EPS)
    return (y * g.astype(jnp.float32) + b.astype(jnp.float32)).astype(x.dtype)

def split_heads(t, n_heads):
    b, s, _ = t.shape
    return t.reshape(b, s, n_heads, HEAD_DIM).transpose(0, 2, 1, 3)

def forgetting_attention(q, k, v, log_f):
    b, h, s, d = q.shape
    n_blk = s // Q_BLOCK
    cum = jnp.cumsum(log_f.astype(jnp.float32), axis=-1)
    q_blocks = q.reshape(b, h, n_blk, Q_BLOCK, d).transpose(2, 0, 1, 3, 4)
    c_blocks = cum.reshape(b, h, n_blk, Q_BLOCK).transpose(2, 0, 1, 3)
    starts = jnp.arange(n_blk, dtype=jnp.int32) * Q_BLOCK
    k_pos = jnp.arange(s, dtype=jnp.int32)
    scale = d ** -0.5

    def one_block(args):
        qb, cb, start = args
        logits = jnp.einsum('bhqd,bhkd->bhqk', qb, k).astype(jnp.float32) * scale
        logits = logits + cb[..., :, None] - cum[..., None, :]
        q_pos = start + jnp.arange(Q_BLOCK, dtype=jnp.int32)
        causal = k_pos[None, :] <= q_pos[:, None]
        logits = jnp.where(causal, logits, -jnp.inf)
        p = jax.nn.softmax(logits, axis=-1)
        return jnp.einsum('bhqk,bhkd->bhqd', p.astype(v.dtype), v)

    out = lax.map(one_block, (q_blocks, c_blocks, starts))
    return out.transpose(1, 2, 0, 3, 4).reshape(b, h, s, d)

def chunked_band_attention(q, k, v, rel_bias):
    b, h, s, d = q.shape
    n_c = s // CHUNK
    band = BAND_CHUNKS * CHUNK
    qc = q.reshape(b, h, n_c, CHUNK, d)
    pad = ((0, 0), (0, 0), (N_LEFT_CHUNKS, 0), (0, 0), (0, 0))
    kp = jnp.pad(k.reshape(b, h, n_c, CHUNK, d), pad)
    vp = jnp.pad(v.reshape(b, h, n_c, CHUNK, d), pad)
    band_idx = np.arange(n_c)[:, None] + np.arange(BAND_CHUNKS)[None, :]
    k_band = kp[:, :, band_idx].reshape(b, h, n_c, band, d)
    v_band = vp[:, :, band_idx].reshape(b, h, n_c, band, d)
    dist = (N_LEFT_CHUNKS * CHUNK + np.arange(CHUNK)[:, None]) - np.arange(band)[None, :]
    rel_idx = np.clip(dist, -REL_CLIP, REL_CLIP) + REL_CLIP
    bias = rel_bias.astype(jnp.float32)[:, rel_idx]
    valid = (np.arange(n_c)[:, None] + np.arange(band)[None, :] // CHUNK) >= N_LEFT_CHUNKS
    logits = jnp.einsum('bhcqd,bhckd->bhcqk', qc, k_band).astype(jnp.float32) * (d ** -0.5)
    logits = logits + bias[None, :, None, :, :]
    logits = jnp.where(valid[None, None, :, None, :], logits, -jnp.inf)
    p = jax.nn.softmax(logits, axis=-1)
    out = jnp.einsum('bhcqk,bhckd->bhcqd', p.astype(v.dtype), v_band)
    return out.reshape(b, h, s, d)

def token_mixer(x, w_in, b_forget, rel_bias, w_out):
    b, s, _ = x.shape
    proj = x @ w_in
    q_a, k_a, v_a, f_a, q_b, k_b, v_b = jnp.split(proj, SPLITS, axis=-1)
    log_f = jax.nn.log_sigmoid((f_a + b_forget).astype(jnp.float32)).transpose(0, 2, 1)
    y_a = forgetting_attention(split_heads(q_a, N_HEADS_A), split_heads(k_a, N_HEADS_A),
                               split_heads(v_a, N_HEADS_A), log_f)
    y_b = chunked_band_attention(split_heads(q_b, N_HEADS_B), split_heads(k_b, N_HEADS_B),
                                 split_heads(v_b, N_HEADS_B), rel_bias)
    y = jnp.concatenate([y_a, y_b], axis=1)
    y = y.transpose(0, 2, 1, 3).reshape(b, s, D_MIX)
    return y @ w_out

def conv_ffn(x, w_up, conv_w, conv_b, w_down):
    s = x.shape[1]
    u = x @ w_up
    u_pad = jnp.pad(u, ((0, 0), (CONV_WIDTH - 1, 0), (0, 0)))
    u = sum(u_pad[:, j:j + s, :] * conv_w[j] for j in range(CONV_WIDTH)) + conv_b
    value, gate = jnp.split(u, 2, axis=-1)
    return (value * jax.nn.gelu(gate)) @ w_down

def first_inputs(seed: int = 0) -> dict:
    key = jax.random.key(seed)
    ks = jax.random.split(key, 16)
    f32 = jnp.float32
    x = jax.random.normal(ks[0], (BATCH, SEQ, D_MODEL), f32)
    col_scale = np.ones((PROJ_COLS,), np.float32)
    col_scale[2 * D_A:3 * D_A] = DEEPNORM_BETA
    col_scale[SPLITS[5]:] = DEEPNORM_BETA
    w_in = jax.random.normal(ks[1], (DEPTH, D_MODEL, PROJ_COLS), f32) * (D_MODEL ** -0.5) * jnp.asarray(col_scale)
    b_forget = jax.random.uniform(ks[2], (DEPTH, N_HEADS_A), f32, 2.0, 5.0)
    rel_bias = jax.random.normal(ks[3], (DEPTH, N_HEADS_B, 2 * REL_CLIP + 1), f32) * 0.5
    w_out = jax.random.normal(ks[4], (DEPTH, D_MIX, D_MODEL), f32) * (D_MIX ** -0.5) * DEEPNORM_BETA
    ln1_g = 1.0 + 0.05 * jax.random.normal(ks[5], (DEPTH, D_MODEL), f32)
    ln1_b = 0.02 * jax.random.normal(ks[6], (DEPTH, D_MODEL), f32)
    w_up = jax.random.normal(ks[7], (DEPTH, D_MODEL, 2 * D_FF), f32) * (D_MODEL ** -0.5)
    conv_w = jax.random.normal(ks[8], (DEPTH, CONV_WIDTH, 2 * D_FF), f32) * (CONV_WIDTH ** -0.5)
    conv_b = 0.02 * jax.random.normal(ks[9], (DEPTH, 2 * D_FF), f32)
    w_down = jax.random.normal(ks[10], (DEPTH, D_FF, D_MODEL), f32) * (D_FF ** -0.5) * DEEPNORM_BETA
    ln2_g = 1.0 + 0.05 * jax.random.normal(ks[11], (DEPTH, D_MODEL), f32)
    ln2_b = 0.02 * jax.random.normal(ks[12], (DEPTH, D_MODEL), f32)
    return {"x": x, "w_in": w_in, "b_forget": b_forget, "rel_bias": rel_bias, "w_out": w_out,
            "ln1_g": ln1_g, "ln1_b": ln1_b, "w_up": w_up, "conv_w": conv_w, "conv_b": conv_b,
            "w_down": w_down, "ln2_g": ln2_g, "ln2_b": ln2_b}

def first_block(x, w_in, b_forget, rel_bias, w_out, ln1_g, ln1_b, w_up, conv_w, conv_b,
              w_down, ln2_g, ln2_b):
    for l in range(DEPTH):
        mix = token_mixer(x, w_in[l], b_forget[l], rel_bias[l], w_out[l])
        x = layer_norm(DEEPNORM_ALPHA * x + mix, ln1_g[l], ln1_b[l])
        ffn = conv_ffn(x, w_up[l], conv_w[l], conv_b[l], w_down[l])
        x = layer_norm(DEEPNORM_ALPHA * x + ffn, ln2_g[l], ln2_b[l])
    return x


GRID_W = 64
CTX_LEN = 256
N_MIXERS = 3
EPS = 1e-6
D_FF_2 = 4 * D_MODEL
N_DIRS = 2

GLA_HEADS = 4
GLA_DK = D_MODEL // 2
GLA_DV = D_MODEL
GLA_HK = GLA_DK // GLA_HEADS
GLA_HV = GLA_DV // GLA_HEADS
GLA_IN = 2 * GLA_DK + 2 * GLA_DV
GLA_GATE_RANK = 16
GLA_TAU = 16.0
GLA_CHUNK = 64

MLSTM_HEADS = 4
MLSTM_INNER = 2 * D_MODEL
MLSTM_HD = MLSTM_INNER // MLSTM_HEADS
MLSTM_QKV_BLOCK = 4
MLSTM_N_BLOCKS = MLSTM_INNER // MLSTM_QKV_BLOCK
MLSTM_CONV = 4
MLSTM_CHUNK = 64

POOL_WINDOWS = (2, 4, 8, 16)
POOL_GROUP = D_MODEL // len(POOL_WINDOWS)


def rmsnorm(x, g):
    xf = x.astype(jnp.float32)
    y = xf * lax.rsqrt(jnp.mean(xf * xf, axis=-1, keepdims=True) + EPS)
    return (y * g.astype(jnp.float32)).astype(x.dtype)

def modulate(h, shift, scale):
    return h * (1 + scale) + shift

def head_rmsnorm(o, g):
    return o * lax.rsqrt(jnp.mean(o * o, axis=-1, keepdims=True) + EPS) * g.astype(jnp.float32)

def head_layernorm(o, g):
    mu = jnp.mean(o, axis=-1, keepdims=True)
    oc = o - mu
    return oc * lax.rsqrt(jnp.mean(oc * oc, axis=-1, keepdims=True) + EPS) * g.astype(jnp.float32)

def to_chunks(t, size):
    b, n = t.shape[0], t.shape[1] // size
    t = t.reshape((b, n, size) + t.shape[2:])
    return t.transpose((1, 0, 3, 2) + tuple(range(4, t.ndim)))

def from_chunks(t):
    n, b, h, c, d = t.shape
    return t.transpose(1, 0, 3, 2, 4).reshape(b, n * c, h, d)

def gla_chunk_scan(q, k, v, log_a, s0):
    f32 = jnp.float32
    qc, kc, vc, gc = (to_chunks(t.astype(f32), GLA_CHUNK) for t in (q, k, v, log_a))
    tri = jnp.tril(jnp.ones((GLA_CHUNK, GLA_CHUNK), dtype=bool))

    def step(s, blk):
        qb, kb, vb, gb = blk
        b = jnp.cumsum(gb, axis=2)
        b_last = b[:, :, -1:, :]
        q_dec = qb * jnp.exp(b)
        att = jnp.where(tri, jnp.einsum('bhtd,bhsd->bhts', q_dec, kb * jnp.exp(-b)), 0.0)
        o = jnp.einsum('bhts,bhsv->bhtv', att, vb) + jnp.einsum('bhtd,bhdv->bhtv', q_dec, s)
        s_new = (jnp.exp(b_last[:, :, 0, :])[..., None] * s
                 + jnp.einsum('bhsd,bhsv->bhdv', kb * jnp.exp(b_last - b), vb))
        return s_new, o

    s_fin, o = lax.scan(step, s0, (qc, kc, vc, gc))
    return from_chunks(o), s_fin

def mlstm_chunk_scan(q, k, v, log_i, log_f, state):
    f32 = jnp.float32
    qc, kc, vc = (to_chunks(t.astype(f32), MLSTM_CHUNK) for t in (q, k, v))
    ic, fc = (to_chunks(t.astype(f32), MLSTM_CHUNK) for t in (log_i, log_f))
    tri = jnp.tril(jnp.ones((MLSTM_CHUNK, MLSTM_CHUNK), dtype=bool))

    def step(carry, blk):
        c_bar, n_bar, m_prev = carry
        qb, kb, vb, ib, fb = blk
        b = jnp.cumsum(fb, axis=-1)
        d_mat = jnp.where(tri, b[..., :, None] - b[..., None, :] + ib[..., None, :], -jnp.inf)
        inter = b + m_prev[..., None]
        m_row = jnp.maximum(jnp.max(d_mat, axis=-1), inter)
        w_qk = jnp.einsum('bhtd,bhsd->bhts', qb, kb) * jnp.exp(d_mat - m_row[..., None])
        w_inter = jnp.exp(inter - m_row)
        num = (jnp.einsum('bhts,bhsv->bhtv', w_qk, vb)
               + w_inter[..., None] * jnp.einsum('bhtd,bhdv->bhtv', qb, c_bar))
        den = jnp.sum(w_qk, axis=-1) + w_inter * jnp.einsum('bhtd,bhd->bht', qb, n_bar)
        h = num / jnp.maximum(jnp.abs(den), jnp.exp(-m_row))[..., None]
        carry_log = b[..., -1] + m_prev
        tok_log = b[..., -1:] - b + ib
        m_new = jnp.maximum(carry_log, jnp.max(tok_log, axis=-1))
        w_tok = jnp.exp(tok_log - m_new[..., None])
        w_carry = jnp.exp(carry_log - m_new)
        k_w = kb * w_tok[..., None]
        c_new = w_carry[..., None, None] * c_bar + jnp.einsum('bhsd,bhsv->bhdv', k_w, vb)
        n_new = w_carry[..., None] * n_bar + jnp.sum(k_w, axis=2)
        return (c_new, n_new, m_new), h

    state_fin, h = lax.scan(step, state, (qc, kc, vc, ic, fc))
    return from_chunks(h), state_fin

def bidirectional_scan(scan_fn, ctx_dirs, lat_dirs, init):
    rev = lambda t: jnp.flip(t, axis=1)
    out_ctx, out_lat = [], []
    for direction in range(N_DIRS):
        ca, la = ctx_dirs[direction], lat_dirs[direction]
        if direction == 1:
            ca = tuple(rev(t) for t in ca)
            la = tuple(rev(t) for t in la)
        o_c, state = scan_fn(*ca, init)
        o_l, _ = scan_fn(*la, state)
        if direction == 1:
            o_c, o_l = rev(o_c), rev(o_l)
        out_ctx.append(o_c)
        out_lat.append(o_l)
    return out_ctx[0] + out_ctx[1], out_lat[0] + out_lat[1]

def gla_mixer(a_ctx, a_lat, w_in, w_a1, w_a2, b_a, g_head, w_o, need_ctx):
    def project(a):
        B, T, _ = a.shape
        q, k, v, r = jnp.split(a @ w_in, [GLA_DK, 2 * GLA_DK, 2 * GLA_DK + GLA_DV], axis=-1)
        q = q.reshape(B, T, GLA_HEADS, GLA_HK) * GLA_HK ** -0.5
        k = k.reshape(B, T, GLA_HEADS, GLA_HK)
        v = v.reshape(B, T, GLA_HEADS, GLA_HV)
        dirs = []
        for d in range(N_DIRS):
            z = (a @ w_a1[d]) @ w_a2[d] + b_a[d]
            log_a = jax.nn.log_sigmoid(z.astype(jnp.float32)) / GLA_TAU
            dirs.append((q, k, v, log_a.reshape(B, T, GLA_HEADS, GLA_HK)))
        return dirs, r

    def finish(o, r):
        B, T = o.shape[:2]
        o = head_rmsnorm(o, g_head).reshape(B, T, GLA_DV).astype(r.dtype)
        return (o * jax.nn.silu(r)) @ w_o

    ctx_dirs, r_ctx = project(a_ctx)
    lat_dirs, r_lat = project(a_lat)
    s0 = jnp.zeros((a_lat.shape[0], GLA_HEADS, GLA_HK, GLA_HV), jnp.float32)
    o_ctx, o_lat = bidirectional_scan(gla_chunk_scan, ctx_dirs, lat_dirs, s0)
    out_ctx = finish(o_ctx, r_ctx) if need_ctx else None
    return out_ctx, finish(o_lat, r_lat)

def centred_conv(x, w, b):
    K = w.shape[0]
    y = lax.conv_general_dilated(x, w[:, None, :], window_strides=(1,),
                                 padding=[(K // 2, K - 1 - K // 2)],
                                 dimension_numbers=('NWC', 'WIO', 'NWC'),
                                 feature_group_count=x.shape[-1])
    return y + b

def headwise(t, w):
    B, T, _ = t.shape
    t = t.reshape(B, T, MLSTM_N_BLOCKS, MLSTM_QKV_BLOCK)
    return jnp.einsum('btni,nij->btnj', t, w).reshape(B, T, MLSTM_INNER)

def mlstm_mixer(a_ctx, a_lat, w_up, conv_w, conv_b, w_qkv, w_gate, b_gate, g_norm, skip, w_down, need_ctx):
    H = MLSTM_HEADS

    def project(a):
        B, T, _ = a.shape
        xm, z = jnp.split(a @ w_up, 2, axis=-1)
        xc = jax.nn.silu(centred_conv(xm, conv_w, conv_b))
        q = headwise(xc, w_qkv[0])
        k = headwise(xc, w_qkv[1])
        v = headwise(xm, w_qkv[2])
        gin = jnp.concatenate([q, k, v], axis=-1)
        heads = lambda t: t.reshape(B, T, H, MLSTM_HD)
        qh, kh, vh = heads(q), heads(k) * MLSTM_HD ** -0.5, heads(v)
        dirs = []
        for d in range(N_DIRS):
            g = (gin @ w_gate[d] + b_gate[d]).astype(jnp.float32)
            dirs.append((qh, kh, vh, g[..., :H], jax.nn.log_sigmoid(g[..., H:])))
        return dirs, xc, z

    def finish(h, xc, z):
        B, T = h.shape[:2]
        hn = head_layernorm(h, g_norm).reshape(B, T, MLSTM_INNER).astype(xc.dtype)
        return ((hn + skip * xc) * jax.nn.silu(z)) @ w_down

    ctx_dirs, xc_ctx, z_ctx = project(a_ctx)
    lat_dirs, xc_lat, z_lat = project(a_lat)
    B = a_lat.shape[0]
    init = (jnp.zeros((B, H, MLSTM_HD, MLSTM_HD), jnp.float32),
            jnp.zeros((B, H, MLSTM_HD), jnp.float32),
            jnp.zeros((B, H), jnp.float32))
    h_ctx, h_lat = bidirectional_scan(mlstm_chunk_scan, ctx_dirs, lat_dirs, init)
    out_ctx = finish(h_ctx, xc_ctx, z_ctx) if need_ctx else None
    return out_ctx, finish(h_lat, xc_lat, z_lat)

def box_mean(x, axis, window):
    length = x.shape[axis]
    pad = [(0, 0)] * x.ndim
    pad[axis] = (1, 0)
    cs = jnp.pad(jnp.cumsum(x.astype(jnp.float32), axis=axis), pad)
    pos = jnp.arange(length)
    lo = jnp.maximum(pos - window // 2, 0)
    hi = jnp.minimum(pos + (window - window // 2), length)
    total = jnp.take(cs, hi, axis=axis) - jnp.take(cs, lo, axis=axis)
    shape = [1] * x.ndim
    shape[axis] = length
    return total / (hi - lo).astype(jnp.float32).reshape(shape)

def pool_mixer(a_ctx, a_lat, w_pool, b_pool, scale, need_ctx):
    B, T, D = a_lat.shape
    rows = T // GRID_W
    grid = a_lat.reshape(B, rows, GRID_W, D)
    lat_parts, ctx_parts = [], []
    for g, win in enumerate(POOL_WINDOWS):
        sl = slice(g * POOL_GROUP, (g + 1) * POOL_GROUP)
        hg = grid[..., sl]
        pooled = box_mean(box_mean(hg, 2, win), 1, win).astype(hg.dtype) - hg
        lat_parts.append(pooled.reshape(B, T, POOL_GROUP) @ w_pool[g] + b_pool[g])
        if need_ctx:
            cg = a_ctx[..., sl]
            pooled_c = box_mean(cg, 1, win).astype(cg.dtype) - cg
            ctx_parts.append(pooled_c @ w_pool[g] + b_pool[g])
    out_lat = jnp.concatenate(lat_parts, axis=-1) * scale
    out_ctx = jnp.concatenate(ctx_parts, axis=-1) * scale if need_ctx else None
    return out_ctx, out_lat

def sqrelu_mlp(h, w1, w2):
    return jnp.square(jax.nn.relu(h @ w1)) @ w2

def second_inputs(seed: int = 0) -> dict:
    key = jax.random.key(seed)
    keys = iter(jax.random.split(key, 48))

    def normal(shape, scale):
        return jax.random.normal(next(keys), shape, jnp.float32) * scale

    def gain(shape):
        return 1.0 + normal(shape, 0.02)

    n_gla = sum(1 for i in range(DEPTH) if i % N_MIXERS == 0)
    n_mlstm = sum(1 for i in range(DEPTH) if i % N_MIXERS == 1)
    n_pool = sum(1 for i in range(DEPTH) if i % N_MIXERS == 2)
    d = D_MODEL
    gate_i = normal((n_mlstm, N_DIRS, MLSTM_HEADS), 0.1)
    gate_f = jnp.linspace(3.0, 6.0, MLSTM_HEADS, dtype=jnp.float32) + normal((n_mlstm, N_DIRS, MLSTM_HEADS), 0.1)
    return {
        'x': normal((BATCH, SEQ, d), 1.0),
        'c': normal((BATCH, d), 1.0),
        'ctx': normal((BATCH, CTX_LEN, d), 1.0),
        'c_ctx': normal((d,), 1.0),
        'ada_w': normal((DEPTH, d, 6 * d), 0.5 * d ** -0.5),
        'ada_b': normal((DEPTH, 6 * d), 0.01),
        'norm1_g': gain((DEPTH, d)),
        'norm2_g': gain((DEPTH, d)),
        'mlp_w1': normal((DEPTH, d, D_FF_2), d ** -0.5),
        'mlp_w2': normal((DEPTH, D_FF_2, d), D_FF_2 ** -0.5),
        'gla_w_in': normal((n_gla, d, GLA_IN), d ** -0.5),
        'gla_w_a1': normal((n_gla, N_DIRS, d, GLA_GATE_RANK), d ** -0.5),
        'gla_w_a2': normal((n_gla, N_DIRS, GLA_GATE_RANK, GLA_DK), GLA_GATE_RANK ** -0.5),
        'gla_b_a': normal((n_gla, N_DIRS, GLA_DK), 0.1),
        'gla_g_head': gain((n_gla, GLA_HEADS, GLA_HV)),
        'gla_w_o': normal((n_gla, GLA_DV, d), GLA_DV ** -0.5),
        'mlstm_w_up': normal((n_mlstm, d, 2 * MLSTM_INNER), d ** -0.5),
        'mlstm_conv_w': normal((n_mlstm, MLSTM_CONV, MLSTM_INNER), MLSTM_CONV ** -0.5),
        'mlstm_conv_b': normal((n_mlstm, MLSTM_INNER), 0.01),
        'mlstm_w_qkv': normal((n_mlstm, 3, MLSTM_N_BLOCKS, MLSTM_QKV_BLOCK, MLSTM_QKV_BLOCK), MLSTM_QKV_BLOCK ** -0.5),
        'mlstm_w_gate': normal((n_mlstm, N_DIRS, 3 * MLSTM_INNER, 2 * MLSTM_HEADS), (3 * MLSTM_INNER) ** -0.5),
        'mlstm_b_gate': jnp.concatenate([gate_i, gate_f], axis=-1),
        'mlstm_g_norm': gain((n_mlstm, MLSTM_HEADS, MLSTM_HD)),
        'mlstm_skip': gain((n_mlstm, MLSTM_INNER)),
        'mlstm_w_down': normal((n_mlstm, MLSTM_INNER, d), MLSTM_INNER ** -0.5),
        'pool_w': normal((n_pool, len(POOL_WINDOWS), POOL_GROUP, POOL_GROUP), POOL_GROUP ** -0.5),
        'pool_b': normal((n_pool, len(POOL_WINDOWS), POOL_GROUP), 0.01),
        'pool_scale': gain((n_pool, d)),
        'final_g': gain((d,)),
    }

def second_block(x, c, ctx, c_ctx, ada_w, ada_b, norm1_g, norm2_g, mlp_w1, mlp_w2,
              gla_w_in, gla_w_a1, gla_w_a2, gla_b_a, gla_g_head, gla_w_o,
              mlstm_w_up, mlstm_conv_w, mlstm_conv_b, mlstm_w_qkv, mlstm_w_gate, mlstm_b_gate,
              mlstm_g_norm, mlstm_skip, mlstm_w_down,
              pool_w, pool_b, pool_scale, final_g):
    silu_c = jax.nn.silu(c)
    silu_cc = jax.nn.silu(c_ctx)
    h_lat, h_ctx = x, ctx
    for i in range(DEPTH):
        kind, j = i % N_MIXERS, i // N_MIXERS
        need_ctx = i < DEPTH - 1
        mod_l = jnp.split((silu_c @ ada_w[i] + ada_b[i])[:, None, :], 6, axis=-1)
        mod_c = jnp.split((silu_cc @ ada_w[i] + ada_b[i])[None, None, :], 6, axis=-1)
        a_lat = modulate(rmsnorm(h_lat, norm1_g[i]), mod_l[0], mod_l[1])
        a_ctx = modulate(rmsnorm(h_ctx, norm1_g[i]), mod_c[0], mod_c[1])
        if kind == 0:
            o_ctx, o_lat = gla_mixer(a_ctx, a_lat, gla_w_in[j], gla_w_a1[j], gla_w_a2[j], gla_b_a[j],
                                     gla_g_head[j], gla_w_o[j], need_ctx)
        elif kind == 1:
            o_ctx, o_lat = mlstm_mixer(a_ctx, a_lat, mlstm_w_up[j], mlstm_conv_w[j], mlstm_conv_b[j],
                                       mlstm_w_qkv[j], mlstm_w_gate[j], mlstm_b_gate[j],
                                       mlstm_g_norm[j], mlstm_skip[j], mlstm_w_down[j], need_ctx)
        else:
            o_ctx, o_lat = pool_mixer(a_ctx, a_lat, pool_w[j], pool_b[j], pool_scale[j], need_ctx)
        h_lat = h_lat + mod_l[2] * o_lat
        h_lat = h_lat + mod_l[5] * sqrelu_mlp(modulate(rmsnorm(h_lat, norm2_g[i]), mod_l[3], mod_l[4]),
                                              mlp_w1[i], mlp_w2[i])
        if need_ctx:
            h_ctx = h_ctx + mod_c[2] * o_ctx
            h_ctx = h_ctx + mod_c[5] * sqrelu_mlp(modulate(rmsnorm(h_ctx, norm2_g[i]), mod_c[3], mod_c[4]),
                                                  mlp_w1[i], mlp_w2[i])
    return rmsnorm(h_lat, final_g)


def setup_inputs(seed=0):
    out = dict(first_inputs(seed))
    for name, value in second_inputs(seed + 1).items():
        if name != "x":
            out[name + "_2"] = value
    return out


def reference(
    x, w_in, b_forget, rel_bias, w_out, ln1_g, ln1_b, w_up, conv_w, conv_b, w_down, ln2_g,
    ln2_b, c_2, ctx_2, c_ctx_2, ada_w_2, ada_b_2, norm1_g_2, norm2_g_2, mlp_w1_2, mlp_w2_2,
    gla_w_in_2, gla_w_a1_2, gla_w_a2_2, gla_b_a_2, gla_g_head_2, gla_w_o_2, mlstm_w_up_2,
    mlstm_conv_w_2, mlstm_conv_b_2, mlstm_w_qkv_2, mlstm_w_gate_2, mlstm_b_gate_2,
    mlstm_g_norm_2, mlstm_skip_2, mlstm_w_down_2, pool_w_2, pool_b_2, pool_scale_2, final_g_2,
):
    x = first_block(
        x, w_in, b_forget, rel_bias, w_out, ln1_g, ln1_b, w_up, conv_w, conv_b, w_down, ln2_g,
        ln2_b,
    )
    return second_block(
        x, c_2, ctx_2, c_ctx_2, ada_w_2, ada_b_2, norm1_g_2, norm2_g_2, mlp_w1_2, mlp_w2_2,
        gla_w_in_2, gla_w_a1_2, gla_w_a2_2, gla_b_a_2, gla_g_head_2, gla_w_o_2, mlstm_w_up_2,
        mlstm_conv_w_2, mlstm_conv_b_2, mlstm_w_qkv_2, mlstm_w_gate_2, mlstm_b_gate_2,
        mlstm_g_norm_2, mlstm_skip_2, mlstm_w_down_2, pool_w_2, pool_b_2, pool_scale_2,
        final_g_2,
    )


_drawn_inputs = setup_inputs


def setup_inputs(seed=0):
    import zlib

    import numpy as np

    out = dict(_drawn_inputs(seed))
    spreads = {}
    factors = {'rel_bias': 5.62,
     'conv_b': 5.966,
     'ctx_2': 3.249,
     'c_ctx_2': 5.108,
     'ada_b_2': 3.26,
     'norm1_g_2': 7.005,
     'norm2_g_2': 19.476,
     'gla_b_a_2': 5.903,
     'gla_g_head_2': 8.0,
     'final_g_2': 7.728}
    for name, (base, spread) in spreads.items():
        noise = np.random.default_rng([zlib.crc32(name.encode()), seed]).standard_normal(out[name].shape)
        drawn = base * np.exp(spread * noise) if base else spread * noise
        out[name] = jnp.asarray(drawn.astype(out[name].dtype))
    for name, factor in factors.items():
        out[name] = (out[name] * factor).astype(out[name].dtype)
    return out
```

```python
from contextlib import ExitStack

import concourse.bass as bass
from concourse import mybir

F32 = mybir.dt.float32
F32R = mybir.dt.float32r
BF16 = mybir.dt.bfloat16
U8 = mybir.dt.uint8
ALU = mybir.AluOpType
ACT = mybir.ActivationFunctionType
AX_X = mybir.AxisListType.X
ds = bass.ds

P = 128
SEQ = 1024
CTX = 256
TOK = SEQ + CTX
D = 1024
KC = D // P
TB = SEQ // P
HD = 64
NHEAD = 8
PAIRS = NHEAD // 2
D_A = NHEAD * HD
DFF = 2816
FCH = DFF // P
FFN_GROUPS = [(0, 8), (8, 8), (16, 6)]
REL = 128
NREL = 2 * REL + 1
LEFT = 4
ALPHA = 2.0 ** 0.25
LN_EPS = 1e-5
RMS_EPS = 1e-6
NEG = -1.0e30
QK_SCALE = HD ** -0.5

ADA_STEP = 12

GH = 4
GDK = 128
GDV = 256
GCH = 64
NCH_CTX = CTX // GCH
NCH = TOK // GCH
NPAIR = TOK // P
LPAIR0 = CTX // P
RANK = 16
TAU = 16.0
MLP_GROUPS = 4

C_ATT = 0
C_WOUT = C_ATT + 6 * PAIRS
C_FFN = C_WOUT + KC
C_GLA = C_FFN + sum(2 * g for _, g in FFN_GROUPS) + KC * len(FFN_GROUPS)
C_WO = C_GLA + 6 * GH
C_MLP = C_WO + KC
C_END = C_MLP + 2 * KC * MLP_GROUPS


def program(nc, x, w_in, b_forget, rel_bias, w_out, ln1_g, ln1_b, w_up, conv_w, conv_b, w_down, ln2_g, ln2_b,
            c_2, ctx_2, c_ctx_2, ada_w, ada_b, norm1_g, norm2_g, mlp_w1, mlp_w2, gla_w_in, gla_w_a1, gla_w_a2,
            gla_b_a, gla_g_head, gla_w_o, final_g, out):
    with ExitStack() as ctx:
        sem = lambda name: ctx.enter_context(nc.semaphore(name))
        base0 = (nc.sbuf_base + 31) // 32 * 32

        def at(name, kb, shape, dt):
            return nc.alloc_sbuf_tensor_at(name, shape, dt, offset=base0 + int(kb * 1024))

        whi = at("whi", 0, [P, 2, KC * P], F32R)
        wlo = at("wlo", 8, [P, 2, KC * P], F32R)
        wraw = at("wraw", 16, [P, 2, KC * P], F32)
        const0 = 24
        ident = at("ident", const0, [P, P], F32)
        ones = at("ones", const0 + .5, [P, P], F32)
        vecs = at("vecs", const0 + 1, [P, 4 * 96], F32)
        mods = at("mods", const0 + 2.5, [P, 96], F32)
        small = at("small", const0 + 2.875, [P, 32], F32)
        x0 = 27
        xres = at("xres", x0, [P, KC * SEQ], F32)
        a0 = x0 + 32
        ahi = at("ahi", a0, [P, KC * SEQ], F32R)
        alo = at("alo", a0 + 32, [P, KC * SEQ], F32R)
        r0 = a0 + 64

        q2 = at("q2", r0, [P, 2 * SEQ], F32R)
        khh = at("khh", r0 + 8, [P, 2 * SEQ], F32R)
        kll = at("kll", r0 + 16, [P, 2 * SEQ], F32R)
        vstage = at("vstage", r0 + 24, [P, SEQ], F32)
        vtok = at("vtok", r0 + 28, [P, TB * P], F32)
        prob = at("prob", r0 + 32, [P, 2 * SEQ], F32)
        probT = at("probT", r0 + 40, [P, 2 * SEQ], F32)
        relT = at("relT", r0 + 48, [P, NHEAD * 256], F32)
        cumL = at("cumL", r0 + 56, [6, 2 * SEQ], BF16)
        cumR = at("cumR", r0 + 60, [6, 2 * SEQ], BF16)
        identb = at("identb", r0 + 64, [P, P], BF16)
        maskb = at("maskb", r0 + 64.25, [P, P], BF16)
        mstat = at("mstat", r0 + 64.5, [P, 64], F32)
        rdiag = at("rdiag", r0 + 82, [P, 2 * P], F32)
        xin = at("xin", r0, [P, TB * D], F32)
        vrow = at("vrow", r0 + 32, [P, 4 * P], F32)
        wf = at("wf", r0 + 34, [P, KC * NHEAD], F32)
        flip = at("flip", r0 + 34.5, [P, P], F32)
        adaring = at("adaring", r0 + 65, [P, 4 * KC * P], F32)
        csil = at("csil", r0 + 81, [P, 2 * KC], F32)
        lf = at("lf", r0, [NHEAD, 4 * SEQ], F32)
        cumLs = at("cumLs", r0 + 16, [NHEAD, 6 * SEQ], BF16)
        cumRs = at("cumRs", r0 + 36, [NHEAD, 6 * SEQ], BF16)
        relx = at("relx", r0 + 28, [NHEAD, 512], F32)
        hank = at("hank", r0 + 48, [P, NHEAD * 256], F32)

        hhi = at("hhi", r0, [P, 8 * SEQ], F32R)
        hlo = at("hlo", r0 + 32, [P, 8 * SEQ], F32R)
        conv_v = at("conv_v", r0 + 64, [P, SEQ], F32)
        conv_g = at("conv_g", r0 + 68, [P, SEQ], F32)
        gelu_g = at("gelu_g", r0 + 72, [P, SEQ], F32)
        hidden = at("hidden", r0 + 76, [P, SEQ], F32)
        xs = at("xs", r0 + 64, [P, SEQ], F32)
        sums = at("sums", r0 + 72, [P, SEQ], F32)
        sumq = at("sumq", r0 + 76, [P, SEQ], F32)
        sqt = at("sqt", r0 + 80, [P, SEQ], F32)
        mean = at("mean", r0 + 16, [P, SEQ], F32)
        rstd = at("rstd", r0 + 20, [P, SEQ], F32)
        msq = at("msq", r0 + 24, [P, SEQ], F32)
        var = at("var", r0 + 28, [P, SEQ], F32)
        cent = at("cent", r0 + 32, [P, 2 * SEQ], F32)
        aff = at("aff", r0 + 40, [P, 2 * SEQ], F32)
        gahi = at("gahi", a0, [P, KC * TOK], F32R)
        galo = at("galo", a0 + 40, [P, KC * TOK], F32R)
        cin = at("cin", r0 + 48, [P, 2 * D], F32)
        cxT = at("cxT", r0 + 56, [P, KC * CTX], F32)
        csq = at("csq", r0 + 64, [P, KC * CTX], F32)
        crs = at("crs", r0 + 16, [P, CTX], F32)
        cvar = at("cvar", r0 + 17, [P, CTX], F32)
        csd = at("csd", r0 + 18, [P, CTX], F32)
        ccent = at("ccent", r0 + 48, [P, 2 * CTX], F32)
        caff = at("caff", r0 + 50, [P, 2 * CTX], F32)
        gains = small[:, 8:32]
        gT = at("gT", x0, [P, TOK], F32)
        qT = at("qT", x0 + 5, [P, SEQ], F32)
        kT = at("kT", x0 + 9, [P, TOK], F32)
        vst = at("vst", x0 + 14, [P, TOK], F32)
        rT = at("rT", x0 + 19, [P, 2 * SEQ], F32)
        state = at("state", x0 + 27, [P, 4 * GDV], F32)
        tot = at("tot", x0 + 31, [P, 2 * NCH], F32)
        etot = at("etot", x0 + 31.25, [P, 2 * NCH], F32)
        ossq = at("ossq", x0 + 31.5, [P, 3 * TB], F32)
        wa2 = at("wa2", x0 + 14, [P, P], F32)
        g0_ = r0 + 16
        g_v = at("g_v", g0_, [P, NPAIR * GDV], F32)
        gcum = at("gcum", g0_ + 10, [P, 2 * TOK], F32)
        gex = at("gex", g0_ + 20, [P, 2 * TOK], F32)
        qd = at("qd", g0_ + 30, [P, 2 * SEQ], F32)
        kn = at("kn", g0_ + 38, [P, 2 * SEQ], F32)
        kd = at("kd", g0_ + 46, [P, 2 * TOK], F32)
        kdt = at("kdt", g0_ + 56, [P, 2 * TOK], F32)
        mask_f = at("mask_f", g0_ + 66, [P, 512], U8)
        mask_b = at("mask_b", g0_ + 66.5, [P, 512], U8)
        restart = at("restart", g0_ + 67, [P, TOK], U8)
        o_tok = at("o_tok", g0_ + 10, [P, TB * GDV], F32)
        att_f = at("att_f", g0_ + 20, [P, TB * P], F32)
        att_b = at("att_b", g0_ + 24, [P, TB * P], F32)
        osq = at("osq", g0_ + 28, [P, GDV], F32)
        wa1raw = at("wa1raw", g0_, [P, KC * P], F32)
        wa1hi = at("wa1hi", g0_ + 4, [P, KC * P], F32R)
        wa1lo = at("wa1lo", g0_ + 8, [P, KC * P], F32R)
        mtmp = at("mtmp", g0_ + 12, [P, TOK], F32)
        relu = at("relu", r0 + 64, [P, SEQ], F32)
        sqr = at("sqr", r0 + 68, [P, SEQ], F32)
        ostage = at("ostage", r0 + 48, [P, 2 * SEQ], F32)

        psum = ctx.enter_context(nc.psum_tensor("ps", [P, 8 * 512], F32))
        G = [psum[:, 0:1024], psum[:, 1024:2048]]
        AUX = [psum[:, 2048:2560], psum[:, 2560:3072]]
        YP = psum[:, 3072:4096]
        AUXW = psum[:, 2048:3072]
        GS = [psum[:, 0:1536], psum[:, 1536:3072]]
        BANK = [psum[:, b * 512:(b + 1) * 512] for b in range(8)]

        xT_d = nc.dram_tensor("xT_scratch", [P, KC * SEQ], F32, kind="Internal").ap()
        cumL_d = nc.dram_tensor("cumL_scratch", [NHEAD, 6 * SEQ], BF16, kind="Internal").ap()
        cumR_d = nc.dram_tensor("cumR_scratch", [NHEAD, 6 * SEQ], BF16, kind="Internal").ap()
        x2_d = nc.dram_tensor("x2_scratch", [P, KC * SEQ], F32, kind="Internal").ap()
        oT_d = nc.dram_tensor("oT_scratch", [P, KC * SEQ], F32, kind="Internal").ap()
        rel_d = nc.dram_tensor("rel_scratch", [NHEAD, 512], F32, kind="Internal").ap()

        raw_loaded = [sem("raw_loaded0"), sem("raw_loaded1")]
        w_hi, w_lo = sem("w_hi"), sem("w_lo")
        gemm_done = sem("gemm_done")
        act_read, dve_read = sem("act_read"), sem("dve_read")
        a_hi, a_lo = sem("a_hi"), sem("a_lo")
        x_loaded = sem("x_loaded")
        consts_ready = sem("consts_ready")
        vec_loaded, vec_zero, vec_T, vec_cols = sem("vec_loaded"), sem("vec_zero"), sem("vec_T"), sem("vec_cols")
        xT_full = sem("xT_full")
        xT_copied, xT_spilled = sem("xT_copied"), sem("xT_spilled")
        small_loaded = sem("small_loaded")
        f_full, f_act, f_dve = sem("f_full"), sem("f_act"), sem("f_dve")
        cum_ready, cum_stored = sem("cum_ready"), sem("cum_stored")
        rel_ready, rel_stored, hank_loaded, rel_full, rel_done = (
            sem("rel_ready"), sem("rel_stored"), sem("hank_loaded"), sem("rel_full"), sem("rel_done"))
        cum_loaded = sem("cum_loaded")
        c_silu, ada_loaded, ada_used, mods_ready = (
            sem("c_silu"), [sem(f"ada_loaded{i}") for i in range(4)], sem("ada_used"), sem("mods_ready"))
        qk_hi, qk_lo = sem("qk_hi"), sem("qk_lo")
        v_staged, v_T, v_tok = sem("v_staged"), sem("v_T"), sem("v_tok")
        s_full, max_ready, exp_done, p_ready = sem("s_full"), sem("max_ready"), sem("exp_done"), sem("p_ready")
        bias_in = sem("bias_in")
        rinv_ready = sem("rinv_ready")
        pt_full, pt_act, pt_dve = sem("pt_full"), sem("pt_act"), sem("pt_dve")
        pv_done, y_out = sem("pv_done"), sem("y_out")
        xs_loaded = sem("xs_loaded")
        x_out, sq_ready, s_added, q_added, sums_zero = (
            sem("x_out"), sem("sq_ready"), sem("s_added"), sem("q_added"), sem("sums_zero"))
        stat_full, stat_act, stat_dve = sem("stat_full"), sem("stat_act"), sem("stat_dve")
        n_cent, n_mul, n_aff = sem("n_cent"), sem("n_mul"), sem("n_aff")
        h_hi, h_lo = sem("h_hi"), sem("h_lo")
        ga_hi, ga_lo = sem("ga_hi"), sem("ga_lo")
        conv_act, conv_dve, gelu_done, h_mul = sem("conv_act"), sem("conv_dve"), sem("gelu_done"), sem("h_mul")
        gains_ready = sem("gains_ready")
        x2_spilled, ctx_loaded, wa1_loaded = sem("x2_spilled"), sem("ctx_loaded"), sem("wa1_loaded")
        ctx_T, ctx_sq, ctx_full, ctx_st, ctx_sd = (
            sem("ctx_T"), sem("ctx_sq"), sem("ctx_full"), sem("ctx_st"), sem("ctx_sd"))
        cc_mul, cc_aff = sem("cc_mul"), sem("cc_aff")
        masks_ready, mask_step = sem("masks_ready"), sem("mask_step")
        wa1_hi, wa1_lo, low_full, low_out = sem("wa1_hi"), sem("wa1_lo"), sem("low_full"), sem("low_out")
        wa2_loaded, z_full, z_act, z_dve = sem("wa2_loaded"), sem("z_full"), sem("z_act"), sem("z_dve")
        g_out, gexp, gmul, tots = sem("g_out"), sem("gexp"), sem("gmul"), sem("tots")
        tr_full, tr_act, tr_dve = sem("tr_full"), sem("tr_act"), sem("tr_dve")
        att_zero, att_full, att_set, att_sum = sem("att_zero"), sem("att_full"), sem("att_set"), sem("att_sum")
        u_full, s_new, o_full, o_act, o_dve = sem("u_full"), sem("s_new"), sem("o_full"), sem("o_act"), sem("o_dve")
        o_sq, o_stat, o_sd, o_norm, oT_full, o_gated, o_spilled = (
            sem("o_sq"), sem("o_stat"), sem("o_sd"), sem("o_norm"), sem("oT_full"), sem("o_gated"), sem("o_spilled"))
        o_left = sem("o_left")
        oT_loaded, gcum_ex, o_rec = sem("oT_loaded"), sem("gcum_ex"), sem("o_rec")
        relu_done, sq_done, m_hi, m_lo = sem("relu_done"), sem("sq_done"), sem("m_hi"), sem("m_lo")
        out_T, out_copied, out_stored = sem("out_T"), sem("out_copied"), [sem("out_stored0"), sem("out_stored1")]

        w_cols = {
            "in": w_in[0].rearrange("(k p) n -> p k n", p=P),
            "out": w_out[0].rearrange("(k p) n -> p k n", p=P),
            "up": w_up[0].rearrange("(k p) n -> p k n", p=P),
            "gla": gla_w_in[0].rearrange("(k p) n -> p k n", p=P),
            "o": gla_w_o[0].rearrange("(k p) n -> p k n", p=P),
            "m1": mlp_w1[0].rearrange("(k p) n -> p k n", p=P),
            "m2": mlp_w2[0].rearrange("(k p) n -> p k n", p=P),
            "down": w_down[0].rearrange("(k p) n -> p k n", p=P),
        }

        def raw3(u):
            return wraw[:, u, :].rearrange("p (k n) -> p k n", n=P)

        QA, KA, VA = 0, D_A, 2 * D_A
        QB, KB, VB = 3 * D_A + NHEAD, 4 * D_A + NHEAD, 5 * D_A + NHEAD
        ATT_COLS = [QA, KA, VA, QB, KB, VB]

        def split_hi(n, half):
            u = half[0]
            act = nc.scalar
            act.wait_ge(raw_loaded[u], half[1])
            act.wait_ge(gemm_done, n + 1)
            act.copy(whi[:, u, :], wraw[:, u, :]).then_inc(w_hi, 1)

        def split_lo(n, u):
            dve = nc.vector
            dve.wait_ge(w_hi, n + 3)
            dve.tensor_tensor(wlo[:, u, :], wraw[:, u, :], whi[:, u, :].bitcast(F32), ALU.subtract).then_inc(w_lo, 1)

        def load_chunk(n, u, src):
            sp = nc.sync
            sp.wait_ge(w_hi, n + 1)
            sp.wait_ge(w_lo, n + 1)
            k = src.shape[1]
            sp.dma_start(raw3(u)[:, 0:k, :], src).then_inc(raw_loaded[u], 16)

        def product(n, u, kc, hi, lo, width, ready):
            pe = nc.tensor
            pe.wait_ge(w_hi, n + 3)
            pe.wait_ge(w_lo, n + 3)
            pe.wait_ge(act_read, n + 1)
            pe.wait_ge(dve_read, n + 1)
            dst = G[u]
            for k in range(kc):
                if ready is not None:
                    pe.wait_ge(ready[0], ready[2] + k + 1 + (ready[3] if len(ready) > 3 else 0))
                    pe.wait_ge(ready[1], ready[2] + k + 1 + (ready[4] if len(ready) > 4 else 0))
                wh, wl = whi[:, u, k * P:(k + 1) * P], wlo[:, u, k * P:(k + 1) * P]
                for w, a in ((wh, hi), (wh, lo), (wl, hi)):
                    for t in range(0, width, 512):
                        e = min(512, width - t)
                        last = pe.matmul(dst[:, t:t + e], w, a[:, k * width + t:k * width + t + e],
                                         start=(k == 0 and w is wh and a is hi),
                                         stop=(k == kc - 1 and w is wl))
            last.then_inc(gemm_done, 1)

        UNITS = [(e, b) for e in range(2) for b in range(TB)]

        def blocks(kind, b):
            return list(range(b + 1)) if kind == "A" else list(range(max(0, b - LEFT), b + 1))

        def pe_attention(pe, kind, half, i):
            un = i * 32 + half * 16
            nv = i * 2 + half
            pe.wait_ge(v_staged, nv + 1)
            pe.wait_ge(mods_ready, nv + 1)
            for b in range(TB):
                last = pe.transpose(AUX[b // 4][:, (b % 4) * P:(b % 4 + 1) * P], vstage[:, b * P:(b + 1) * P],
                                    ident[:, :])
                if b % 4 == 3:
                    last.then_inc(v_T, 1)

            def qk(u):
                e, b = UNITS[u]
                kb = blocks(kind, b)
                slot = G[u % 2]
                if u == 0:
                    pe.wait_ge(qk_hi, (nv + 1) * 6)
                    pe.wait_ge(qk_lo, (nv + 1) * 6)
                    pe.wait_ge(act_read, i * 6 + half * 3 + 3 + 2)
                    pe.wait_ge(dve_read, i * 6 + half * 3 + 3 + 2)
                    if kind == "A":
                        pe.wait_ge(cum_loaded, (i + 1) * 64)
                pe.wait_ge(exp_done, un + u + 1)
                n0, n = kb[0] * P, len(kb) * P
                qs = q2[:, e * SEQ + b * P:e * SEQ + (b + 1) * P]
                for t in range(0, n, 512):
                    w = min(512, n - t)
                    o = slot[:, t:t + w]
                    c = e * SEQ + n0 + t
                    final = kind == "B"
                    pe.matmul(o, qs, khh[:, c:c + w], start=True, stop=False)
                    last = pe.matmul(o, qs, kll[:, c:c + w], start=False, stop=final)
                    if kind == "A":
                        diag = t + w == n
                        last = pe.matmul(o, cumL[:, e * SEQ + b * P:e * SEQ + (b + 1) * P], cumR[:, c:c + w],
                                         start=False, stop=not diag)
                        if diag:
                            last = pe.matmul(slot[:, n - P:n], identb[:, :], maskb[:, :], start=False, stop=True)
                last.then_inc(s_full, 1)

            def turn(u):
                e, b = UNITS[u]
                kb = blocks(kind, b)
                pe.wait_ge(p_ready, un + u + 1)
                for hf in range(2):
                    js = [j for j in range(len(kb)) if j // 4 == hf]
                    done = (pt_act, pt_dve)[hf]
                    if u == 0:
                        pe.wait_ge(v_tok, (nv + 1) * 2)
                    else:
                        pe.wait_ge(done, un + u + 1)
                    if not js:
                        continue
                    for j in js:
                        last = pe.matmul(AUX[hf][:, (j % 4) * P:(j % 4 + 1) * P],
                                         prob[:, (u % 2) * SEQ + j * P:(u % 2) * SEQ + (j + 1) * P],
                                         rdiag[:, (u % 2) * P:(u % 2 + 1) * P], start=True, stop=True)
                last.then_inc(pt_full, 1)

            def pv(u):
                e, b = UNITS[u]
                kb = blocks(kind, b)
                pe.wait_ge(pt_act, un + u + 2)
                pe.wait_ge(pt_dve, un + u + 2)
                if u == 0:
                    pe.wait_ge(v_tok, (nv + 1) * 2)
                    pe.wait_ge(y_out, nv + 1)
                for j, k in enumerate(kb):
                    last = pe.matmul(YP[e * HD:(e + 1) * HD, b * P:(b + 1) * P],
                                     vtok[:, k * P + e * HD:k * P + (e + 1) * HD],
                                     probT[:, (u % 2) * SEQ + j * P:(u % 2) * SEQ + (j + 1) * P],
                                     start=(j == 0), stop=(j == len(kb) - 1))
                last.then_inc(pv_done, 1)

            qk(0)
            qk(1)
            for u in range(16):
                if u + 2 < 16:
                    qk(u + 2)
                turn(u)
                if u >= 1:
                    pv(u - 1)
            pv(15)

        def act_attention(act, kind, half, i):
            un = i * 32 + half * 16
            nv = i * 2 + half

            def evac(u):
                e, b = UNITS[u]
                n = min(4, len(blocks(kind, b))) * P
                act.wait_ge(pt_full, un + u + 3)
                act.wait_ge(pv_done, un + u + 1)
                act.copy(probT[:, (u % 2) * SEQ:(u % 2) * SEQ + n], AUX[0][:, 0:n]).then_inc(pt_act, 1)

            for u in range(16):
                e, b = UNITS[u]
                n = len(blocks(kind, b)) * P
                act.wait_ge(max_ready, un + u + 1)
                act.wait_ge(pt_full, un + u + 1)
                s = 3 * (u % 2)
                act.activation(prob[:, (u % 2) * SEQ:(u % 2) * SEQ + n], G[u % 2][:, 0:n], ACT.Exp,
                               bias=mstat[:, s:s + 1], accum_out=mstat[:, s + 1:s + 2]).then_inc(exp_done, 1)
                if u >= 1:
                    evac(u - 1)
            evac(15)
            act.wait_ge(pv_done, un + 18)
            act.wait_ge(xT_spilled, 16)
            act.copy(xres[:, ds(i * SEQ + half * PAIRS * SEQ, SEQ)], YP).then_inc(y_out, 1)

        def dve_attention(dve, kind, half, i):
            un = i * 32 + half * 16
            nv = i * 2 + half
            for hf in range(2):
                dve.wait_ge(v_T, nv * 2 + hf + 1)
                dve.wait_ge(pv_done, un + 2)
                dve.tensor_copy(vtok[:, hf * 512:(hf + 1) * 512], AUX[hf]).then_inc(v_tok, 1)

            def norm(u):
                e, b = UNITS[u]
                s = 3 * (u % 2)
                dve.wait_ge(exp_done, un + u + 3)
                dve.reciprocal(mstat[:, s + 2:s + 3], mstat[:, s + 1:s + 2]).then_inc(rinv_ready, 1)
                dve.wait_ge(rinv_ready, un + u + 1)
                dve.tensor_scalar(rdiag[:, (u % 2) * P:(u % 2 + 1) * P], ident[:, :], mstat[:, s + 2:s + 3], None,
                                  ALU.mult).then_inc(p_ready, 1)

            def evac(u):
                e, b = UNITS[u]
                n = max(0, len(blocks(kind, b)) - 4) * P
                dve.wait_ge(pt_full, un + u + 3)
                if n == 0:
                    dve.wait_ge(pt_dve, un + u + 1)
                    dve.sem_inc(pt_dve, 1)
                    return
                dve.wait_ge(pv_done, un + u + 1)
                dve.tensor_copy(probT[:, (u % 2) * SEQ + 512:(u % 2) * SEQ + 512 + n], AUX[1][:, 0:n]
                                ).then_inc(pt_dve, 1)

            nb = 0
            for u in range(16):
                e, b = UNITS[u]
                n = len(blocks(kind, b)) * P
                s = 3 * (u % 2)
                slot = G[u % 2]
                dve.wait_ge(s_full, un + u + 1)
                if kind == "B":
                    w = min(n, 256)
                    nb += 1
                    dve.tensor_tensor(slot[:, n - w:n], slot[:, n - w:n],
                                      relT[:, ds(i * 512 + e * 256 + 256 - w, w)], ALU.add).then_inc(bias_in, 1)
                    if n == (LEFT + 1) * P:
                        nb += 1
                        dve.memset(slot[64:128, 0:64], NEG).then_inc(bias_in, 1)
                    dve.wait_ge(bias_in, i * NB_B + nb)
                dve.wait_ge(exp_done, un + u + 1)
                dve.reduce_max(mstat[:, s:s + 1], slot[:, 0:n], AX_X, negate=True).then_inc(max_ready, 1)
                if u >= 1:
                    norm(u - 1)
                if u >= 2:
                    evac(u - 2)
            norm(15)
            evac(14)
            evac(15)

        NB_B = 16 + sum(1 for _, b in UNITS if len(blocks("B", b)) == LEFT + 1)

        NORMS = {
            "ln1": dict(sq=0, s=0, st=0, sa=0, sd=0, ce=0, mu=0, af=0),
            "ln2": dict(sq=8, s=8, st=1, sa=3, sd=2, ce=8, mu=8, af=8),
            "rms1": dict(sq=16, st=2, sa=6, sd=4, mu=16, af=16),
            "rms2": dict(sq=24, st=3, sa=7, sd=6, mu=24, af=24),
            "rmsf": dict(sq=32, st=4, sa=8, sd=8, mu=32, af=32),
        }
        LNV = {"ln1": 0, "ln2": 16}

        def vcol(t, row):
            return vecs[:, ds(row + t * 96, 1)]

        def act_square(act, j, sq, src):
            act.wait_ge(q_added, j + sq + 1)
            act.activation(sqt[:, :], src, ACT.Square).then_inc(sq_ready, 1)

        zeroed = [0]

        def pool_zero(pool):
            pool.memset(sums[:, :], 0.0).then_inc(sums_zero, 1)
            pool.memset(sumq[:, :], 0.0).then_inc(sums_zero, 1)
            zeroed[0] += 2
            pool.wait_ge(sums_zero, zeroed[0])

        def pool_sum(pool, j, xo, s, sq):
            if s is not None:
                pool.wait_ge(x_out, j + xo + 1)
                pool.tensor_tensor(sums[:, :], sums[:, :], xres[:, ds(j * SEQ, SEQ)], ALU.add).then_inc(s_added, 1)
                pool.wait_ge(s_added, j + s + 1)
            pool.wait_ge(sq_ready, j + sq + 1)
            pool.tensor_tensor(sumq[:, :], sumq[:, :], sqt[:, :], ALU.add).then_inc(q_added, 1)
            pool.wait_ge(q_added, j + sq + 2)

        def pe_stats(pe, name):
            c = NORMS[name]
            pe.wait_ge(q_added, c["sq"] + KC + 1)
            if "ce" in c:
                for t in range(0, SEQ, 512):
                    pe.matmul(YP[:, t:t + 512], ones[:, :], sums[:, t:t + 512], start=True, stop=True)
            for t in range(0, SEQ, 512):
                last = pe.matmul(AUXW[:, t:t + 512], ones[:, :], sumq[:, t:t + 512], start=True, stop=True)
            last.then_inc(stat_full, 1)

        def act_stats(act, name):
            c = NORMS[name]
            sa = c["sa"]
            act.wait_ge(stat_full, c["st"] + 1)
            if "ce" in c:
                act.copy(mean[:, :], YP).then_inc(stat_act, 1)
                act.activation(msq[:, :], YP, ACT.Square).then_inc(stat_act, 1)
                sa += 2
                act.wait_ge(stat_act, sa)
            act.wait_ge(stat_dve, c["sd"] + 1)
            act.activation(msq[:, :], var[:, :], ACT.Sqrt).then_inc(stat_act, 1)

        def dve_stats(dve, name):
            c = NORMS[name]
            dve.wait_ge(stat_full, c["st"] + 1)
            if "ce" in c:
                dve.wait_ge(stat_act, c["sa"] + 2)
                dve.scalar_tensor_tensor(out=var[:, :], in0=AUXW, scalar=LN_EPS, in1=msq[:, :], op0=ALU.add,
                                         op1=ALU.subtract).then_inc(stat_dve, 1)
                dve.wait_ge(stat_act, c["sa"] + 3)
            else:
                dve.tensor_scalar(var[:, :], AUXW, RMS_EPS, None, ALU.add).then_inc(stat_dve, 1)
                dve.wait_ge(stat_act, c["sa"] + 1)
            dve.reciprocal(rstd[:, :], msq[:, :]).then_inc(stat_dve, 1)
            dve.wait_ge(stat_dve, c["sd"] + 2)

        def pool_centre(pool, name):
            c = NORMS[name]
            pool.wait_ge(stat_act, c["sa"] + 2)
            with pool.Fori(0, KC // 2) as i:
                for u in range(2):
                    pool_centre_one(pool, name, i * 2 + u, u)

        def pool_centre_one(pool, name, k, u):
            pool.wait_ge(n_aff, k + NORMS[name]["af"] + 1)
            pool.tensor_tensor(cent[:, u * SEQ:(u + 1) * SEQ], xres[:, ds(k * SEQ, SEQ)], mean[:, :],
                               ALU.subtract).then_inc(n_cent, 1)

        def dve_scale(dve, name, k, u):
            c = NORMS[name]
            cu = cent[:, u * SEQ:(u + 1) * SEQ]
            if "ce" in c:
                dve.wait_ge(n_cent, k + c["ce"] + 1)
                src = cu
            else:
                dve.wait_ge(n_aff, k + c["af"] + 1)
                src = xres[:, ds(k * SEQ, SEQ)]
            dve.tensor_tensor(cu, src, rstd[:, :], ALU.mult).then_inc(n_mul, 1)

        def act_layer_norm(act, name, k, u):
            c = NORMS[name]
            act.wait_ge(n_mul, k + c["mu"] + 1)
            act.activation(xres[:, ds(k * SEQ, SEQ)], cent[:, u * SEQ:(u + 1) * SEQ], ACT.Identity,
                           scale=vcol(2, k + LNV[name]), bias=vcol(2, k + LNV[name] + KC)).then_inc(n_aff, 1)
            act.wait_ge(n_aff, k + c["af"] + 3)

        GLA_COLS = [(0, P), (GH * GDK, P), (2048, GDV), (2048 + P, GDV), (1024, GDV), (1024 + P, GDV)]
        STEPS = NCH

        def chunk_of(d, j):
            return j if d == 0 else (NCH_CTX - 1 - j if j < NCH_CTX else NCH + NCH_CTX - 1 - j)

        def first_visit(d, b):
            return (b < TB // 2) == (d == 0)

        GROUPS = [range(0, 4), range(4, 8), range(8, 10)]

        def act_rms(act, name, dst, w, off, gain, shift, done, base):
            c = NORMS[name]
            for k in range(KC):
                u = k % 2
                act.wait_ge(n_mul, c["mu"] + k + 1)
                act.wait_ge(done, base + k - 1 + 2)
                act.activation(aff[:, u * SEQ:(u + 1) * SEQ], cent[:, u * SEQ:(u + 1) * SEQ], ACT.Identity,
                               scale=gain(k), bias=shift(k)).then_inc(n_aff, 1)
                act.wait_ge(n_aff, c["af"] + k + 3)
                act.copy(dst[:, k * w + off:k * w + off + SEQ], aff[:, u * SEQ:(u + 1) * SEQ]).then_inc(
                    {"rms1": ga_hi, "rms2": a_hi}[name], 1)

        def dve_rms(dve, name, dhi, dlo, w, off, hi_sem, hi_base, lo_sem):
            for k in range(KC + 1):
                if k < KC:
                    dve_scale(dve, name, k, k % 2)
                if k >= 1:
                    q = k - 1
                    dve.wait_ge(hi_sem, hi_base + q + 1)
                    dve.tensor_tensor(dlo[:, q * w + off:q * w + off + SEQ], aff[:, (q % 2) * SEQ:(q % 2 + 1) * SEQ],
                                      dhi[:, q * w + off:q * w + off + SEQ].bitcast(F32), ALU.subtract
                                      ).then_inc(lo_sem, 1)

        def gla_product(n, u, lat_only):
            pe = nc.tensor
            pe.wait_ge(w_hi, n + 3)
            pe.wait_ge(w_lo, n + 3)
            pe.wait_ge(act_read, n + 1)
            pe.wait_ge(dve_read, n + 1)
            t0, width = (CTX, SEQ) if lat_only else (0, TOK)
            for k in range(KC):
                wh, wl = whi[:, u, k * P:(k + 1) * P], wlo[:, u, k * P:(k + 1) * P]
                for w, a in ((wh, gahi), (wh, galo), (wl, gahi)):
                    for t in range(0, width, 512):
                        e = min(512, width - t)
                        c = k * TOK + t0 + t
                        last = pe.matmul(GS[u][:, t:t + e], w, a[:, c:c + e],
                                         start=(k == 0 and w is wh and a is gahi), stop=(k == KC - 1 and w is wl))
            last.then_inc(gemm_done, 1)

        def pe_turn(pe, i, g0, src, ready):
            pe.wait_ge(*ready)
            for q, blks in enumerate(GROUPS):
                g = g0 + q
                if g < 2:
                    pe.wait_ge(o_dve, i * 8 + 2)
                    pe.wait_ge(o_act, i * 8 + 2)
                elif g - 2 < 6:
                    pe.wait_ge(tr_act, i * 6 + g - 1)
                else:
                    pe.wait_ge(tr_dve, i * 6 + g - 7)
                for y, b in enumerate(blks):
                    last = pe.transpose(BANK[6 + g % 2][:, y * P:(y + 1) * P], src[:, b * P:(b + 1) * P], ident[:, :])
                last.then_inc(tr_full, 1)

        def o_bank(d, v):
            return BANK[(6, 0)[v % 2] + d]

        def visits():
            return [(j, d, (chunk_of(d, j) - NCH_CTX) // 2, (j - NCH_CTX) // 2)
                    for j in range(NCH_CTX + 1, STEPS, 2) for d in range(2)]

        def evac_count(d, v):
            seen = {True: 0, False: 0}
            for _, dd, b, vv in visits():
                fv = first_visit(dd, b)
                seen[fv] += 1
                if (dd, vv) == (d, v):
                    return fv, seen[fv]

        def pe_gla_core(pe, i):
            pe.wait_ge(tr_act, i * 6 + 6)
            pe.wait_ge(tr_dve, i * 6 + 6)
            pe.wait_ge(gmul, i * 6 + 6)
            pe.wait_ge(act_read, i * 6 + C_GLA + 8)
            for h in range(2):
                if h == 1:
                    pe.wait_ge(att_set, i * 4 + 2)
                for d in range(2):
                    for y in range(4):
                        b = h * 4 + y
                        last = pe.matmul(BANK[d][:, y * P:(y + 1) * P], kn[:, d * SEQ + b * P:d * SEQ + (b + 1) * P],
                                         qd[:, d * SEQ + b * P:d * SEQ + (b + 1) * P], start=True, stop=True)
                last.then_inc(att_full, 1)
            for j in range(STEPS):
                for d in range(2):
                    c = chunk_of(d, j)
                    b, r = c // 2, (c % 2) * 64
                    if j < STEPS - 1:
                        if j >= 2:
                            pe.wait_ge(s_new, i * 38 + 2 * (j - 2) + d + 1)
                        pe.matmul(BANK[2 + 2 * d + j % 2][:, 0:GDV], kdt[r:r + 64, d * TOK + b * P:d * TOK + (b + 1) * P],
                                  g_v[r:r + 64, b * GDV:(b + 1) * GDV], start=True, stop=True).then_inc(u_full, 1)
                    if j >= NCH_CTX:
                        v = (j - NCH_CTX) // 2
                        lb = b - LPAIR0
                        bank = o_bank(d, v)[:, 0:GDV]
                        if (j - NCH_CTX) % 2 == 0:
                            if v >= 2:
                                fv, cnt = evac_count(d, v - 2)
                                pe.wait_ge(o_act if fv else o_dve, i * 8 + cnt + 2)
                            if v == 1:
                                pe.wait_ge(att_set, i * 4 + 4)
                            if d == 0:
                                if v == 0:
                                    pe.wait_ge(att_sum, i + 1)
                                pe.matmul(bank, att_f[:, lb * P:(lb + 1) * P], g_v[:, b * GDV:(b + 1) * GDV],
                                          start=True, stop=False, skip_group_check=True)
                        pe.wait_ge(s_new, i * 38 + 2 * (j - 1) + d + 1)
                        qo = d * SEQ + (c - NCH_CTX) * GCH
                        last = pe.matmul(bank[r:r + 64, :], qd[:, qo:qo + GCH],
                                         state[:, (d * 2 + j % 2) * GDV:(d * 2 + j % 2 + 1) * GDV],
                                         start=(d == 1), stop=True, skip_group_check=True)
                        if (j - NCH_CTX) % 2 == 1:
                            last.then_inc(o_full, 1)
            pe.wait_ge(o_norm, i + 1)
            for f in range(2):
                for b in range(TB):
                    last = pe.transpose(psum[:, f * SEQ + b * P:f * SEQ + (b + 1) * P],
                                        o_tok[:, b * GDV + f * P:b * GDV + (f + 1) * P], ident[:, :])
                last.then_inc(oT_full, 1)

        def dve_second(dve, i, v_no, d, b, v):
            dve.wait_ge(o_full, i * 16 + v_no + 1)
            fv, cnt = evac_count(1 - d, [w for _, dd, bb, w in visits() if dd == 1 - d and bb == b][0])
            dve.wait_ge(o_act, i * 8 + cnt + 2)
            ob = o_tok[:, b * GDV:(b + 1) * GDV]
            dve.tensor_tensor(ob, ob, o_bank(d, v)[:, 0:GDV], ALU.add).then_inc(o_dve, 1)

        DECAYS = [(0, 1, False, 3), (0, -1, False, 3), (0, 1, True, 7),
                  (1, 1, True, 6), (1, 1, False, 8), (1, -1, False, 8)]
        SECOND = [b for _, d, b, _ in visits() if not first_visit(d, b)]

        def peeled(eng, last, body):
            with eng.Fori(0, KC // 2 - (1 if last else 0)) as i:
                for u in range(2):
                    body(i, u)
            if last:
                for u in range(2):
                    body(KC // 2 - 1, u)

        block = ctx.enter_context(nc.Block())

        @block.sync
        def _(sp):
            xv = x[0].rearrange("(b p) d -> b p d", p=P)
            for b in range(TB):
                sp.dma_start(xin[:, b * D:(b + 1) * D], xv[b]).then_inc(x_loaded, 16)
            ada_v = ada_w[0].rearrange("(k p) n -> p k n", p=P)
            with sp.Fori(0, PAIRS) as i:
                for j in range(6):
                    load_chunk(i * 6 + C_ATT + j, j % 2, w_cols["in"][:, :, ds(i * P + ATT_COLS[j], P)])
                    for c in (2 * j, 2 * j + 1):
                        s = c % 4
                        sp.wait_ge(ada_used, i * ADA_STEP + c + 1)
                        sp.dma_start(adaring[:, s * D:(s + 1) * D].rearrange("p (k n) -> p k n", n=P),
                                     ada_v[:, :, ds(i * ADA_STEP * P + c * P, P)]).then_inc(ada_loaded[s], 16)
            with sp.Fori(0, KC // 2) as i:
                for u in range(2):
                    load_chunk(i * 2 + C_WOUT + u, u, w_cols["out"][:, :, ds(i * 2 * P + u * P, P)])
            n = C_FFN
            for g0, gc in FFN_GROUPS:
                with sp.Fori(0, gc) as i:
                    load_chunk(i * 2 + n, 0, w_cols["up"][:, :, ds(i * P + g0 * P, P)])
                    load_chunk(i * 2 + n + 1, 1, w_cols["up"][:, :, ds(i * P + (g0 + FCH) * P, P)])
                n += 2 * gc
                with sp.Fori(0, KC // 2) as i:
                    for u in range(2):
                        load_chunk(i * 2 + n + u, u, w_cols["down"][:, g0:g0 + gc, ds(i * 2 * P + u * P, P)])
                n += KC
            with sp.Fori(0, GH) as i:
                for j, (c0, step) in enumerate(GLA_COLS):
                    load_chunk(i * 6 + C_GLA + j, j % 2, w_cols["gla"][:, :, ds(i * step + c0, P)])
            with sp.Fori(0, KC // 2) as i:
                for u in range(2):
                    load_chunk(i * 2 + C_WO + u, u, w_cols["o"][:, :, ds(i * 2 * P + u * P, P)])
            n = C_MLP
            for g in range(MLP_GROUPS):
                with sp.Fori(0, KC // 2) as i:
                    for u in range(2):
                        load_chunk(i * 2 + n + u, u, w_cols["m1"][:, :, ds(i * 2 * P + (g * KC + u) * P, P)])
                n += KC
                with sp.Fori(0, KC // 2) as i:
                    for u in range(2):
                        load_chunk(i * 2 + n + u, u, w_cols["m2"][:, g * KC:(g + 1) * KC, ds(i * 2 * P + u * P, P)])
                n += KC

        @block.gpsimd
        def _(pool):
            pool.memset(ident[:, :], 0.0).then_inc(vec_zero, 1)
            pool.memset(flip[:, :], 0.0).then_inc(vec_zero, 1)
            pool.memset(maskb[:, :], 0.0).then_inc(vec_zero, 1)
            pool.memset(vrow[:, :], 0.0).then_inc(vec_zero, 1)
            pool.memset(ones[:, :], 1.0 / D).then_inc(consts_ready, 1)
            pool.wait_ge(vec_zero, 4)
            pool.affine_select(out=ident[:, :], in_=ident[:, :], compare_op=ALU.not_equal, fill=1.0, base=0,
                               pattern=[[-1, P]], channel_multiplier=1).then_inc(consts_ready, 1)
            pool.affine_select(out=flip[:, :], in_=flip[:, :], compare_op=ALU.not_equal, fill=1.0, base=1 - P,
                               pattern=[[1, P]], channel_multiplier=1).then_inc(consts_ready, 1)
            pool.affine_select(out=maskb[:, :], in_=maskb[:, :], compare_op=ALU.is_ge, fill=NEG, base=0,
                               pattern=[[-1, P]], channel_multiplier=1).then_inc(consts_ready, 1)
            pool.wait_ge(consts_ready, 4)
            pool.tensor_copy(identb[:, :], ident[:, :]).then_inc(consts_ready, 1)
            rows = [
                [conv_w[0, 0:2].rearrange("j (n p) -> (j n) p", p=P)],
                [conv_w[0, 2:3].rearrange("j (n p) -> (j n) p", p=P), conv_b.rearrange("j (n p) -> (j n) p", p=P)],
                [v.rearrange("j (n p) -> (j n) p", p=P) for v in (ln1_g, ln1_b, ln2_g, ln2_b, norm1_g, norm2_g)]
                + [final_g.rearrange("(n p) -> n p", p=P), gla_g_head[0].rearrange("h (n p) -> (h n) p", p=P),
                   c_2.rearrange("j (n p) -> (j n) p", p=P), c_ctx_2.rearrange("(n p) -> n p", p=P)],
                [ada_b.rearrange("j (n p) -> (j n) p", p=P), gla_b_a[0].rearrange("d (n p) -> (d n) p", p=P)],
            ]
            for t, vs in enumerate(rows):
                r = 0
                for v in vs:
                    pool.dma_start(vrow[r:r + v.shape[0], t * P:(t + 1) * P], v).then_inc(vec_loaded, 16)
                    r += v.shape[0]
            pool.dma_start(wf[:, :].rearrange("p (k n) -> p k n", n=NHEAD),
                           w_cols["in"][:, :, 3 * D_A:3 * D_A + NHEAD]).then_inc(small_loaded, 16)
            pool.dma_start(small[0:NHEAD, 0:1], b_forget.rearrange("j h -> h j")).then_inc(small_loaded, 16)
            pool.wait_ge(xT_full, KC)
            pool.dma_start(relx[:, 0:NREL], rel_bias[0]).then_inc(small_loaded, 16)
            pool.wait_ge(xT_copied, KC)
            pool.dma_start(xT_d, xres[:, :]).then_inc(xT_spilled, 16)
            pool.wait_ge(rel_ready, 3)
            pool.dma_start(rel_d, relx[:, :]).then_inc(rel_stored, 16)
            pool.wait_ge(cum_ready, 10)
            pool.dma_start(cumL_d, cumLs[:, :]).then_inc(cum_stored, 16)
            pool.dma_start(cumR_d, cumRs[:, :]).then_inc(cum_stored, 16)
            pool.wait_ge(rel_stored, 16)
            for h in range(NHEAD):
                for jj in range(2):
                    src = bass.AP(tensor=rel_d.tensor, offset=h * 512 + 129 - 128 * jj, ap=[[1, P], [1, P]])
                    pool.dma_start(hank[:, h * 256 + jj * P:h * 256 + (jj + 1) * P], src).then_inc(hank_loaded, 16)
            pool.wait_ge(cum_stored, 32)
            with pool.Fori(0, PAIRS) as i:
                pool.wait_ge(pv_done, i * 32 + 2)
                for e in range(2):
                    for dst, src in ((cumL, cumL_d), (cumR, cumR_d)):
                        pool.dma_start(dst[:, e * SEQ:(e + 1) * SEQ],
                                       src[ds(i * 2 + e, 1), :].rearrange("h (r t) -> (h r) t", r=6)
                                       ).then_inc(cum_loaded, 16)
            pool.wait_ge(cum_loaded, 16 * 4 * PAIRS)
            pool.wait_ge(y_out, 2 * PAIRS + 1)
            pool_zero(pool)
            pool.sem_inc(q_added, 1)
            pool.wait_ge(xT_spilled, 16)
            with pool.Fori(0, KC) as j:
                pool.dma_start(xs[:, :], xT_d[:, ds(j * SEQ, SEQ)]).then_inc(xs_loaded, 16)
                pool_sum(pool, j, 0, 0, 0)
            pool_centre(pool, "ln1")
            pool.wait_ge(h_lo, FCH)
            pool_zero(pool)
            with pool.Fori(0, KC) as j:
                pool_sum(pool, j, 24, 8, 8)
            pool.wait_ge(stat_full, 2)
            pool.memset(sumq[:, :], 0.0).then_inc(sums_zero, 1)
            zeroed[0] += 1
            pool.wait_ge(sums_zero, zeroed[0])
            pool.dma_start(cin[:, :].rearrange("p (b d) -> p b d", d=D), ctx_2[0].rearrange("(b p) d -> p b d", p=P)
                           ).then_inc(ctx_loaded, 16)
            pool.wait_ge(stat_act, NORMS["ln2"]["sa"] + 2)
            pool_centre_one(pool, "ln2", 0, 0)
            pool_centre_one(pool, "ln2", 1, 1)
            for k in range(KC):
                pool_sum(pool, k, 0, None, 16)
                if k + 2 < KC:
                    pool_centre_one(pool, "ln2", k + 2, k % 2)
            pool.dma_start(x2_d, xres[:, :]).then_inc(x2_spilled, 16)
            pool.wait_ge(q_added, 25)
            pool.wait_ge(ga_lo, KC + 2)
            ms = 0

            def step(ins):
                ins.then_inc(mask_step, 1)
                pool.wait_ge(mask_step, ms + 1)
                return ms + 1

            m3 = mtmp[:, 0:512].rearrange("p (b t) -> p b t", t=P)
            for mask, sign, rows, cols in ((mask_f, 1, slice(0, 64), slice(64, 128)),
                                           (mask_b, -1, slice(64, 128), slice(0, 64))):
                ms = step(pool.memset(mtmp[:, 0:512], 1.0))
                ms = step(pool.affine_select(out=m3, in_=m3, compare_op=ALU.is_ge, fill=0.0, base=0,
                                             pattern=[[0, 4], [sign, P]], channel_multiplier=-sign))
                ms = step(pool.memset(m3[rows, :, cols], 0.0))
                ms = step(pool.tensor_copy(mask[:, :], mtmp[:, 0:512]))
            ms = step(pool.memset(mtmp[:, :], 1.0))
            ms = step(pool.memset(mtmp[:, :].rearrange("p (c t) -> p c t", t=GCH)[:, :, 0:1], 0.0))
            ms = step(pool.tensor_copy(restart[:, :], mtmp[:, :]))
            pool.sem_inc(masks_ready, 1)
            pool.wait_ge(cc_mul, KC)
            pool.wait_ge(ga_lo, 2 * KC + 2)
            ms = step(pool.memset(wa1raw[:, :], 0.0))
            for d in range(2):
                pool.dma_start(wa1raw[:, :].rearrange("p (k n) -> p k n", n=P)[:, :, 32 * d:32 * d + RANK],
                               gla_w_a1[0, d].rearrange("(k p) n -> p k n", p=P)).then_inc(wa1_loaded, 16)
            pool.wait_ge(x2_spilled, 16)
            pool.wait_ge(low_out, 1)
            pool.sem_inc(o_left, 1)
            with pool.Fori(0, GH) as i:
                pool.wait_ge(tr_full, i * 12 + 1)
                for d in range(2):
                    pool.dma_start(wa2[32 * d:32 * d + RANK, :], gla_w_a2[0, d][:, ds(i * P, P)]
                                   ).then_inc(wa2_loaded, 16)
                pool.wait_ge(o_gated, i * 2 + 4)
                pool.dma_start(oT_d[:, ds(i * 2 * SEQ, 2 * SEQ)], rT[:, :]).then_inc(o_spilled, 16)
                pool.wait_ge(o_spilled, i * 16 + 16)
                pool.sem_inc(o_left, 1)
            pool.dma_start(xres[:, :], oT_d).then_inc(oT_loaded, 16)
            pool_zero(pool)
            with pool.Fori(0, KC) as j:
                pool.dma_start(xs[:, :], x2_d[:, ds(j * SEQ, SEQ)]).then_inc(xs_loaded, 16)
                pool.wait_ge(x_out, j + 33)
                pool_sum(pool, j, 0, None, 24)
            pool.wait_ge(m_lo, 4 * KC + 1)
            pool_zero(pool)
            with pool.Fori(0, KC) as j:
                pool_sum(pool, j, 0, None, 32)
            ov = out[0].rearrange("(b t) f -> t b f", t=P)
            with pool.Fori(0, KC // 2) as i:
                for u in range(2):
                    pool.wait_ge(out_copied, i * 2 + u + 1)
                    pool.dma_start(ov[:, :, ds(i * 2 * P + u * P, P)],
                                   ostage[:, u * SEQ:(u + 1) * SEQ].rearrange("p (b f) -> p b f", f=P)
                                   ).then_inc(out_stored[u], 16)
            for u in range(2):
                pool.wait_ge(out_stored[u], 16 * KC // 2)

        @block.tensor
        def _(pe):
            pe.sem_inc(gemm_done, 2)
            pe.sem_inc(ada_used, 4)
            pe.sem_inc(pv_done, 2)
            pe.sem_inc(pt_full, 2)
            pe.wait_ge(consts_ready, 5)
            pe.wait_ge(vec_loaded, 16 * 15)
            for t in range(4):
                last = pe.transpose(AUX[0][:, t * P:(t + 1) * P], vrow[:, t * P:(t + 1) * P], ident[:, :])
            last.then_inc(vec_T, 1)
            for k in range(KC):
                if k >= 2:
                    pe.wait_ge(xT_copied, k - 1)
                for b in range(TB):
                    if k == 0:
                        pe.wait_ge(x_loaded, 16 * TB)
                    last = pe.transpose(G[k % 2][:, b * P:(b + 1) * P], xin[:, b * D + k * P:b * D + (k + 1) * P],
                                        ident[:, :])
                last.then_inc(xT_full, 1)
            pe.wait_ge(small_loaded, 16 * 3)
            pe.wait_ge(xT_copied, KC)
            for t in range(2):
                for k in range(KC):
                    last = pe.matmul(YP[0:NHEAD, t * 512:(t + 1) * 512], wf[:, k * NHEAD:(k + 1) * NHEAD],
                                     xres[:, k * SEQ + t * 512:k * SEQ + (t + 1) * 512],
                                     start=(k == 0), stop=(k == KC - 1))
            last.then_inc(f_full, 1)
            pe.wait_ge(hank_loaded, 16 * 16)
            pe.wait_ge(xT_copied, KC)
            for h in range(NHEAD):
                slot = G[h // 4][:, (h % 4) * 256:(h % 4 + 1) * 256]
                for jj in range(2):
                    last = pe.matmul(slot[:, jj * P:(jj + 1) * P],
                                     hank[:, h * 256 + jj * P:h * 256 + (jj + 1) * P], flip[:, :], start=True, stop=True)
            last.then_inc(rel_full, 1)
            pe.wait_ge(rel_done, 3)
            pe.wait_ge(c_silu, 2)
            pe.wait_ge(vec_cols, 1)
            with pe.Fori(0, PAIRS) as i:
                for half, kind in enumerate("AB"):
                    n = i * 6 + half * 3
                    pe.wait_ge(exp_done, i * 32 + half * 16 + 2)
                    pe.wait_ge(pt_act, i * 32 + half * 16 + 1)
                    pe.wait_ge(pt_dve, i * 32 + half * 16 + 1)
                    for j in range(3):
                        product(n + j, (half * 3 + j) % 2, KC, ahi, alo, SEQ, (a_hi, a_lo, 0))
                        for c in (half * 6 + 2 * j, half * 6 + 2 * j + 1):
                            s = c % 4
                            pe.wait_ge(ada_loaded[s], i * (16 * ADA_STEP // 4) + (c // 4 + 1) * 16)
                            for k in range(KC):
                                last = pe.matmul(AUX[0][:, 2 * (c % 6):2 * (c % 6) + 2],
                                                 adaring[:, s * D + k * P:s * D + (k + 1) * P],
                                                 csil[:, 2 * k:2 * k + 2], start=(k == 0), stop=(k == KC - 1))
                            last.then_inc(ada_used, 1)
                    pe_attention(pe, kind, half, i)
            pe.wait_ge(exp_done, PAIRS * 32 + 2)
            with pe.Fori(0, KC // 2) as i:
                for u in range(2):
                    product(i * 2 + C_WOUT + u, u, KC, ahi, alo, SEQ, (a_hi, a_lo, 8))
            pe_stats(pe, "ln1")
            n = C_FFN
            for g0, gc in FFN_GROUPS:
                with pe.Fori(0, gc) as i:
                    for u in range(2):
                        product(i * 2 + n + u, u, KC, ahi, alo, SEQ, (a_hi, a_lo, 16))
                n += 2 * gc
                with pe.Fori(0, KC // 2) as i:
                    for u in range(2):
                        product(i * 2 + n + u, u, gc, hhi, hlo, SEQ, (h_hi, h_lo, g0, 1))
                n += KC
            pe_stats(pe, "ln2")
            pe.wait_ge(ctx_loaded, 16)
            for k in range(KC):
                for b in range(2):
                    last = pe.transpose(G[k // 4][:, (k % 4) * CTX + b * P:(k % 4) * CTX + (b + 1) * P],
                                        cin[:, b * D + k * P:b * D + (k + 1) * P], ident[:, :])
            last.then_inc(ctx_T, 1)
            pe_stats(pe, "rms1")
            pe.wait_ge(ctx_sq, 2)
            for k in range(KC):
                last = pe.matmul(BANK[6][:, 0:CTX], ones[:, :], csq[:, k * CTX:(k + 1) * CTX],
                                 start=(k == 0), stop=(k == KC - 1))
            last.then_inc(ctx_full, 1)
            pe.wait_ge(wa1_hi, 1)
            pe.wait_ge(wa1_lo, 1)
            pe.wait_ge(ga_lo, 2 * KC + 2)
            for k in range(KC):
                wh, wl = wa1hi[:, k * P:(k + 1) * P], wa1lo[:, k * P:(k + 1) * P]
                for w, a in ((wh, gahi), (wh, galo), (wl, gahi)):
                    for t in range(0, TOK, 512):
                        e = min(512, TOK - t)
                        last = pe.matmul(GS[0][:, t:t + e], w, a[:, k * TOK + t:k * TOK + t + e],
                                         start=(k == 0 and w is wh and a is gahi), stop=(k == KC - 1 and w is wl))
            last.then_inc(low_full, 1)
            pe.sem_inc(tr_full, 1)
            with pe.Fori(0, GH) as i:
                pe.wait_ge(wa2_loaded, i * 32 + 32)
                pe.wait_ge(low_out, 1)
                pe.wait_ge(o_gated, i * 2 + 2)
                for d in range(2):
                    for t in range(0, TOK, 512):
                        e = min(512, TOK - t)
                        last = pe.matmul(GS[d][:, t:t + e], wa2[32 * d:32 * d + RANK, :],
                                         gT[32 * d:32 * d + RANK, t:t + e], start=True, stop=True)
                    last.then_inc(z_full, 1)
                for j in range(6):
                    n = i * 6 + C_GLA + j
                    if j < 2:
                        pe.wait_ge(z_dve, i * 8 + j * 3 + 1)
                    lat_only = j in (0, 2, 3)
                    gla_product(n, j % 2, lat_only)
                    if j == 3:
                        for d in range(2):
                            pe_turn(pe, i, d * 3, kd[:, d * TOK:(d + 1) * TOK], (gmul, i * 6 + (3, 4)[d]))
                pe_turn(pe, i, 6, vst[:, :], (g_out, i * 6 + 5))
                pe_turn(pe, i, 9, vst[:, :], (g_out, i * 6 + 6))
                pe_gla_core(pe, i)
            pe.wait_ge(o_gated, GH * 2 + 2)
            with pe.Fori(0, KC // 2) as i:
                for u in range(2):
                    product(i * 2 + C_WO + u, u, KC, ahi, alo, SEQ, (a_hi, a_lo, 24))
            pe_stats(pe, "rms2")
            n = C_MLP
            for g in range(MLP_GROUPS):
                with pe.Fori(0, KC // 2) as i:
                    for u in range(2):
                        product(i * 2 + n + u, u, KC, ahi, alo, SEQ, (a_hi, a_lo, 32, 0, 2))
                n += KC
                with pe.Fori(0, KC // 2) as i:
                    for u in range(2):
                        product(i * 2 + n + u, u, KC, hhi, hlo, SEQ, (m_hi, m_lo, g * KC, 0, 1))
                n += KC
            pe_stats(pe, "rmsf")
            pe.wait_ge(act_read, C_END + 2)
            pe.wait_ge(dve_read, C_END + 2)
            for k in range(KC):
                pe.wait_ge(n_aff, NORMS["rmsf"]["af"] + k + 3)
                if k >= 2:
                    pe.wait_ge(out_copied, k - 1)
                for b in range(TB):
                    last = pe.transpose(G[k % 2][:, b * P:(b + 1) * P],
                                        aff[:, (k % 2) * SEQ + b * P:(k % 2) * SEQ + (b + 1) * P], ident[:, :])
                last.then_inc(out_T, 1)

        @block.scalar
        def _(act):
            act.sem_inc(w_hi, 2)
            act.sem_inc(act_read, 2)
            act.sem_inc(exp_done, 2)
            act.sem_inc(y_out, 1)
            act.sem_inc(pt_act, 1)
            act.wait_ge(vec_T, 1)
            act.copy(vecs[:, :].rearrange("p (t n) -> p t n", n=96),
                     AUX[0].rearrange("p (t n) -> p t n", n=P)[:, :, 0:96]).then_inc(vec_cols, 1)
            for k in range(KC):
                act.wait_ge(xT_full, k + 1)
                act.copy(ahi[:, k * SEQ:(k + 1) * SEQ], G[k % 2]).then_inc(a_hi, 1)
                act.copy(xres[:, k * SEQ:(k + 1) * SEQ], G[k % 2]).then_inc(xT_copied, 1)
            act.wait_ge(vec_cols, 1)
            cs = csil[:, :].rearrange("p (k two) -> p two k", two=2)
            act.activation(cs[:, 0, :], vecs[:, 2 * 96 + 64:2 * 96 + 72], ACT.Silu).then_inc(c_silu, 1)
            act.activation(cs[:, 1, :], vecs[:, 2 * 96 + 72:2 * 96 + 80], ACT.Silu).then_inc(c_silu, 1)
            act.wait_ge(f_full, 1)
            L = lambda s: lf[:, s * SEQ:(s + 1) * SEQ]
            act.activation(L(0), YP[0:NHEAD, :], ACT.Abs, bias=small[0:NHEAD, 0:1]).then_inc(f_act, 1)
            act.wait_ge(f_act, 1)
            act.activation(L(1), L(0), ACT.Exp, scale=-1.0).then_inc(f_act, 1)
            act.wait_ge(f_act, 2)
            act.activation(L(0), L(1), ACT.Ln, bias=1.0).then_inc(f_act, 1)
            act.wait_ge(rel_full, 1)
            act.copy(relT[:, 0:1024], G[0]).then_inc(rel_done, 1)
            act.copy(relT[:, 1024:2048], G[1]).then_inc(rel_done, 1)

            split_hi(0, (0, 16))
            with act.Fori(0, PAIRS) as i:
                for half, kind in enumerate("AB"):
                    n = i * 6 + half * 3
                    for j in range(3):
                        c = half * 3 + j
                        u = c % 2
                        split_hi(n + j + 1, ((c + 1) % 2, i * 48 + ((c + 1) // 2 + 1) * 16))
                        act.wait_ge(gemm_done, n + j + 3)
                        if j == 0:
                            act.mul(q2[0:64, 0:SEQ], G[u][0:64, :], QK_SCALE).then_inc(qk_hi, 1)
                            act.mul(q2[0:64, SEQ:2 * SEQ], G[u][64:128, :], QK_SCALE).then_inc(qk_hi, 1)
                        elif j == 1:
                            for e in range(2):
                                for r in range(2):
                                    act.copy(khh[r * 64:(r + 1) * 64, e * SEQ:(e + 1) * SEQ],
                                             G[u][e * 64:(e + 1) * 64, :]).then_inc(qk_hi, 1)
                        else:
                            act.copy(vstage[:, :], G[u]).then_inc(v_staged, 1)
                        if j < 2:
                            act.wait_ge(qk_hi, (i * 2 + half) * 6 + (2, 6)[j])
                        else:
                            act.wait_ge(v_staged, i * 2 + half + 1)
                        act.sem_inc(act_read, 1)
                    act_attention(act, kind, half, i)
            act.wait_ge(gemm_done, C_WOUT + 2)
            for k in range(KC):
                if k == 0:
                    act.wait_ge(y_out, 2 * PAIRS + 1)
                act.copy(ahi[:, k * SEQ:(k + 1) * SEQ], xres[:, k * SEQ:(k + 1) * SEQ]).then_inc(a_hi, 1)
            act.sem_inc(n_aff, 2)
            with act.Fori(0, KC // 2) as i:
                for u in range(2):
                    j = i * 2 + u
                    split_hi(j + C_WOUT + 1, (1 - u, i * 16 + (C_WOUT // 2 + 1 + u) * 16))
                    act.wait_ge(x_out, j + 1)
                    act_square(act, j, 0, xres[:, ds(j * SEQ, SEQ)])
                    act.sem_inc(act_read, 1)
            act_stats(act, "ln1")
            with act.Fori(0, KC // 2) as i:
                for u in range(2):
                    k = i * 2 + u
                    act_layer_norm(act, "ln1", k, u)
                    act.copy(ahi[:, ds(k * SEQ, SEQ)], xres[:, ds(k * SEQ, SEQ)]).then_inc(a_hi, 1)
            n = C_FFN
            act.sem_inc(h_mul, 1)
            act.sem_inc(h_hi, 1)
            for gi, (g0, gc) in enumerate(FFN_GROUPS):
                with act.Fori(0, gc) as i:
                    for u, cv in enumerate((conv_v, conv_g)):
                        split_hi(i * 2 + n + u + 1, (1 - u, i * 16 + (n // 2 + 1 + u) * 16))
                        act.wait_ge(gemm_done, i * 2 + n + u + 3)
                        act.wait_ge(h_mul, i + g0 + 1)
                        f = i + g0 + u * FCH
                        act.activation(cv[:, :], G[u], ACT.Identity, scale=vcol(1, f), bias=vcol(1, f + 44)
                                       ).then_inc(conv_act, 1)
                        act.wait_ge(conv_act, i * 2 + g0 * 2 + u + 1)
                        act.sem_inc(act_read, 1)
                    act.wait_ge(conv_dve, i * 4 + g0 * 4 + 4)
                    act.activation(gelu_g[:, :], conv_g[:, :], ACT.Gelu_apprx_tanh).then_inc(gelu_done, 1)
                    act.wait_ge(h_mul, i + g0 + 2)
                    act.copy(hhi[:, ds(i * SEQ, SEQ)], hidden[:, :]).then_inc(h_hi, 1)
                n += 2 * gc
                with act.Fori(0, KC // 2) as i:
                    for u in range(2):
                        j = i * 2 + u
                        split_hi(j + n + 1, (1 - u, i * 16 + (n // 2 + 1 + u) * 16))
                        if gi == len(FFN_GROUPS) - 1:
                            act.wait_ge(x_out, j + 25)
                            act_square(act, j, 8, xres[:, ds(j * SEQ, SEQ)])
                        act.sem_inc(act_read, 1)
                n += KC
            act_stats(act, "ln2")
            for k in range(KC):
                act_layer_norm(act, "ln2", k, k % 2)
                act_square(act, k, 16, xres[:, k * SEQ:(k + 1) * SEQ])
            act.wait_ge(ctx_T, 1)
            for h in range(2):
                act.activation(csq[:, h * 1024:(h + 1) * 1024], G[h], ACT.Square).then_inc(ctx_sq, 1)
            for h in range(2):
                act.copy(cxT[:, h * 1024:(h + 1) * 1024], G[h]).then_inc(ctx_sq, 1)
            act_stats(act, "rms1")
            act.wait_ge(ctx_st, 1)
            act.activation(csd[:, :], cvar[:, :], ACT.Sqrt).then_inc(ctx_sd, 1)
            mod = lambda n, who: mods[:, 2 * n + who:2 * n + who + 1]
            act.wait_ge(gains_ready, 3)
            act_rms(act, "rms1", gahi, TOK, CTX, lambda k: gains[:, k:k + 1], lambda k: mod(k, 0), ga_lo, 0)
            for k in range(KC):
                u = k % 2
                act.wait_ge(cc_mul, k + 1)
                if k >= 2:
                    act.wait_ge(ga_lo, KC + k - 1 + 2)
                act.activation(caff[:, u * CTX:(u + 1) * CTX], ccent[:, u * CTX:(u + 1) * CTX], ACT.Identity,
                               scale=gains[:, 8 + k:9 + k], bias=mod(k, 1)).then_inc(cc_aff, 1)
                act.wait_ge(cc_aff, k + 1)
                act.copy(gahi[:, k * TOK:k * TOK + CTX], caff[:, u * CTX:(u + 1) * CTX]).then_inc(ga_hi, 1)
            act.wait_ge(wa1_loaded, 32)
            act.copy(wa1hi[:, :], wa1raw[:, :]).then_inc(wa1_hi, 1)
            act.wait_ge(low_full, 1)
            act.wait_ge(x2_spilled, 16)
            act.copy(gT[0:64, :], GS[0][0:64, 0:TOK]).then_inc(low_out, 1)
            act.sem_inc(o_act, 2)
            with act.Fori(0, GH) as i:
                for d in range(2):
                    act.wait_ge(z_full, i * 2 + d + 1)
                    bias = vecs[:, ds(i + 3 * 96 + 48 + d * GH, 1)]
                    if d == 1:
                        act.wait_ge(z_dve, i * 8 + 2)
                    act.activation(gex[:, 0:TOK], GS[d][:, 0:TOK], ACT.Abs, bias=bias).then_inc(z_act, 1)
                    act.wait_ge(z_act, i * 6 + d * 3 + 1)
                    act.activation(gex[:, 0:TOK], gex[:, 0:TOK], ACT.Exp, scale=-1.0).then_inc(z_act, 1)
                    act.wait_ge(z_act, i * 6 + d * 3 + 2)
                    act.activation(gex[:, 0:TOK], gex[:, 0:TOK], ACT.Ln, bias=1.0).then_inc(z_act, 1)

                def decay(e):
                    d, sign, full, after = DECAYS[e]
                    n0, w = (0, TOK) if full else (CTX, SEQ)
                    act.wait_ge(z_dve, i * 8 + after)
                    if e >= 2:
                        act.wait_ge(gmul, i * 6 + e - 1)
                    act.activation(gex[:, (e % 2) * TOK + n0:(e % 2) * TOK + n0 + w],
                                   gcum[:, d * TOK + n0:d * TOK + n0 + w], ACT.Exp, scale=sign / TAU
                                   ).then_inc(gexp, 1)

                for j in range(6):
                    u = j % 2
                    n = i * 6 + C_GLA + j
                    split_hi(n + 1, (1 - u, i * 48 + (C_GLA // 2 + 1 + (j + 1) // 2) * 16))
                    act.wait_ge(gemm_done, n + 3)
                    if j == 0:
                        act.mul(qT[:, :], GS[u][:, 0:SEQ], GDK ** -0.5).then_inc(g_out, 1)
                    elif j == 1:
                        act.copy(kT[:, :], GS[u][:, 0:TOK]).then_inc(g_out, 1)
                    elif j in (2, 3):
                        act.wait_ge(o_left, i + 1)
                        act.activation(rT[:, (j - 2) * SEQ:(j - 1) * SEQ], GS[u][:, 0:SEQ], ACT.Silu).then_inc(g_out, 1)
                    else:
                        if j == 5:
                            act.wait_ge(tr_full, i * 12 + 10)
                        act.copy(vst[:, :], GS[u][:, 0:TOK]).then_inc(g_out, 1)
                    act.wait_ge(g_out, i * 6 + j + 1)
                    act.sem_inc(act_read, 1)
                    if j == 1:
                        act.wait_ge(tots, i * 2 + 2)
                        act.activation(etot[:, :], tot[:, :], ACT.Exp, scale=1.0 / TAU).then_inc(gexp, 1)
                        act.wait_ge(gcum_ex, i + 1)
                        for e in range(3):
                            decay(e)
                    if j == 2:
                        for e in range(3, 6):
                            decay(e)
                    if j == 3:
                        for d in range(2):
                            for q, blks in enumerate(GROUPS):
                                g = d * 3 + q
                                act.wait_ge(tr_full, i * 12 + g + 2)
                                b0, w = blks[0] * P, len(blks) * P
                                act.copy(kdt[:, d * TOK + b0:d * TOK + b0 + w], BANK[6 + g % 2][:, 0:w]
                                         ).then_inc(tr_act, 1)
                for v_no, (j, d, b, v) in enumerate(visits()):
                    if not first_visit(d, b):
                        continue
                    act.wait_ge(o_full, i * 16 + v_no + 1)
                    act.copy(o_tok[:, b * GDV:(b + 1) * GDV], o_bank(d, v)[:, 0:GDV]).then_inc(o_act, 1)
                for q, b in enumerate(SECOND):
                    act.wait_ge(o_dve, i * 8 + q + 3)
                    act.activation(osq[:, :], o_tok[:, b * GDV:(b + 1) * GDV], ACT.Square,
                                   accum_out=ossq[:, b:b + 1]).then_inc(o_sq, 1)
                    act.wait_ge(o_sq, i * 8 + q + 1)
                act.wait_ge(o_stat, i + 1)
                act.activation(ossq[:, TB:2 * TB], ossq[:, TB:2 * TB], ACT.Sqrt).then_inc(o_sd, 1)
            act.wait_ge(oT_loaded, 16)
            for k in range(KC):
                act.copy(ahi[:, k * SEQ:(k + 1) * SEQ], xres[:, k * SEQ:(k + 1) * SEQ]).then_inc(a_hi, 1)
            with act.Fori(0, KC // 2) as i:
                for u in range(2):
                    j = i * 2 + u
                    split_hi(j + C_WO + 1, (1 - u, i * 16 + (C_WO // 2 + 1 + u) * 16))
                    act.wait_ge(x_out, j + 33)
                    act_square(act, j, 24, xres[:, ds(j * SEQ, SEQ)])
                    act.sem_inc(act_read, 1)
            act_stats(act, "rms2")
            act_rms(act, "rms2", ahi, SEQ, 0, lambda k: gains[:, 16 + k:17 + k], lambda k: mod(24 + k, 0), a_lo, 32)
            n = C_MLP
            for g in range(MLP_GROUPS):
                with act.Fori(0, KC // 2) as i:
                    for u in range(2):
                        j = i * 2 + u
                        split_hi(j + n + 1, (1 - u, i * 16 + (n // 2 + 1 + u) * 16))
                        act.wait_ge(gemm_done, j + n + 3)
                        act.wait_ge(sq_done, j + g * KC + 1)
                        act.activation(relu[:, :], G[u], ACT.Relu).then_inc(relu_done, 1)
                        act.wait_ge(relu_done, j + g * KC + 1)
                        act.sem_inc(act_read, 1)
                        act.wait_ge(sq_done, j + g * KC + 2)
                        act.copy(hhi[:, ds(j * SEQ, SEQ)], sqr[:, :]).then_inc(m_hi, 1)
                n += KC
                def down(i, u):
                    j = i * 2 + u
                    if not (isinstance(i, int) and u == 1):
                        split_hi(j + n + 1, (1 - u, i * 16 + (n // 2 + 1 + u) * 16))
                    if g == MLP_GROUPS - 1:
                        act.wait_ge(x_out, j + 41 + 24)
                        act_square(act, j, 32, xres[:, ds(j * SEQ, SEQ)])
                    act.sem_inc(act_read, 1)

                peeled(act, g == MLP_GROUPS - 1, down)
                n += KC
            act_stats(act, "rmsf")
            for k in range(KC):
                u = k % 2
                act.wait_ge(n_mul, NORMS["rmsf"]["mu"] + k + 1)
                if k >= 2:
                    act.wait_ge(out_T, k - 1)
                act.activation(aff[:, u * SEQ:(u + 1) * SEQ], cent[:, u * SEQ:(u + 1) * SEQ], ACT.Identity,
                               scale=vcol(2, 48 + k)).then_inc(n_aff, 1)

        @block.vector
        def _(dve):
            dve.sem_inc(w_lo, 2)
            dve.sem_inc(dve_read, 2)
            dve.sem_inc(pt_dve, 1)
            for k in range(KC):
                dve.wait_ge(a_hi, k + 1)
                dve.wait_ge(xT_copied, k + 1)
                dve.tensor_tensor(alo[:, k * SEQ:(k + 1) * SEQ], xres[:, k * SEQ:(k + 1) * SEQ],
                                  ahi[:, k * SEQ:(k + 1) * SEQ].bitcast(F32), ALU.subtract).then_inc(a_lo, 1)
            dve.wait_ge(small_loaded, 16 * 3)
            dve.tensor_copy(small[0:NHEAD, 1:2], relx[:, NREL - 1:NREL]).then_inc(rel_ready, 1)
            dve.memset(relx[:, NREL:512], 0.0).then_inc(rel_ready, 1)
            dve.wait_ge(rel_ready, 2)
            dve.tensor_scalar(relx[:, 0:NREL], relx[:, 0:NREL], small[0:NHEAD, 1:2], None,
                              ALU.subtract).then_inc(rel_ready, 1)
            L = lambda s: lf[:, s * SEQ:(s + 1) * SEQ]
            dve.wait_ge(f_full, 1)
            dve.wait_ge(f_act, 1)
            dve.tensor_scalar(L(2), YP[0:NHEAD, :], small[0:NHEAD, 0:1], 0.0, ALU.add, ALU.min).then_inc(f_dve, 1)
            dve.wait_ge(f_act, 3)
            dve.wait_ge(f_dve, 1)
            dve.tensor_tensor(L(3), L(2), L(0), ALU.subtract).then_inc(f_dve, 1)
            dve.memset(L(1), 1.0).then_inc(f_dve, 1)
            dve.wait_ge(f_dve, 3)
            dve.tensor_tensor_scan(L(0), L(1), L(3), 0.0, ALU.mult, ALU.add).then_inc(f_dve, 1)
            dve.wait_ge(f_dve, 4)
            cl = lambda r: cumLs[:, r * SEQ:(r + 1) * SEQ]
            cr = lambda r: cumRs[:, r * SEQ:(r + 1) * SEQ]
            dve.memset(cumLs[:, 0:3 * SEQ], 1.0).then_inc(cum_ready, 1)
            dve.memset(cumRs[:, 3 * SEQ:6 * SEQ], 1.0).then_inc(cum_ready, 1)
            ncum = 2
            src = L(0)
            for r in range(3):
                dve.tensor_copy(cl(3 + r), src).then_inc(cum_ready, 1)
                ncum += 1
                dve.wait_ge(cum_ready, ncum)
                dve.tensor_scalar(cr(r), cl(3 + r), -1.0, None, ALU.mult).then_inc(cum_ready, 1)
                ncum += 1
                if r < 2:
                    dst = L(2 + r)
                    dve.tensor_tensor(dst, src, cl(3 + r), ALU.subtract).then_inc(cum_ready, 1)
                    ncum += 1
                    dve.wait_ge(cum_ready, ncum)
                    src = dst
            dve.wait_ge(rel_done, 2)
            dve.memset(relT[0:64, :].rearrange("p (h n) -> p h n", n=256)[:, :, 192:256], NEG).then_inc(rel_done, 1)

            split_lo(0, 0)
            with dve.Fori(0, PAIRS) as i:
                for half, kind in enumerate("AB"):
                    n = i * 6 + half * 3
                    for j in range(3):
                        c = half * 3 + j
                        u = c % 2
                        split_lo(n + j + 1, (c + 1) % 2)
                        dve.wait_ge(gemm_done, n + j + 3)
                        nq = (i * 2 + half) * 6
                        if j == 0:
                            dve.wait_ge(qk_hi, nq + 2)
                            for e in range(2):
                                last = dve.scalar_tensor_tensor(
                                    out=q2[64:128, e * SEQ:(e + 1) * SEQ], in0=G[u][e * 64:(e + 1) * 64, :],
                                    scalar=QK_SCALE, in1=q2[0:64, e * SEQ:(e + 1) * SEQ].bitcast(F32),
                                    op0=ALU.mult, op1=ALU.subtract).then_inc(qk_lo, 1)
                        elif j == 1:
                            dve.wait_ge(qk_hi, nq + 6)
                            for e in range(2):
                                for r in range(2):
                                    dve.tensor_tensor(
                                        kll[r * 64:(r + 1) * 64, e * SEQ:(e + 1) * SEQ],
                                        G[u][e * 64:(e + 1) * 64, :],
                                        khh[r * 64:(r + 1) * 64, e * SEQ:(e + 1) * SEQ].bitcast(F32),
                                        ALU.subtract).then_inc(qk_lo, 1)
                        if j < 2:
                            dve.wait_ge(qk_lo, nq + (2, 6)[j])
                        dve.sem_inc(dve_read, 1)
                    dve.wait_ge(ada_used, i * ADA_STEP + half * 6 + 10)
                    dve.tensor_tensor(mods[:, ds(i * 2 * ADA_STEP + half * 12, 12)].rearrange("p (n two) -> p n two", two=2),
                                      AUX[0][:, 0:12].rearrange("p (n two) -> p n two", two=2),
                                      vecs[:, ds(i * ADA_STEP + half * 6 + 3 * 96, 6)].unsqueeze(2).broadcast_to([P, 6, 2]),
                                      ALU.add).then_inc(mods_ready, 1)
                    dve_attention(dve, kind, half, i)
            dve.wait_ge(gemm_done, C_WOUT + 2)
            for k in range(KC):
                dve.wait_ge(a_hi, KC + k + 1)
                dve.tensor_tensor(alo[:, k * SEQ:(k + 1) * SEQ], xres[:, k * SEQ:(k + 1) * SEQ],
                                  ahi[:, k * SEQ:(k + 1) * SEQ].bitcast(F32), ALU.subtract).then_inc(a_lo, 1)
            with dve.Fori(0, KC // 2) as i:
                for u in range(2):
                    j = i * 2 + u
                    split_lo(j + C_WOUT + 1, 1 - u)
                    dve.wait_ge(gemm_done, j + C_WOUT + 3)
                    dve.wait_ge(xs_loaded, j * 16 + 16)
                    dve.scalar_tensor_tensor(out=xres[:, ds(j * SEQ, SEQ)], in0=xs[:, :], scalar=ALPHA, in1=G[u],
                                             op0=ALU.mult, op1=ALU.add).then_inc(x_out, 1)
                    dve.wait_ge(x_out, j + 1)
                    dve.sem_inc(dve_read, 1)
            dve_stats(dve, "ln1")
            with dve.Fori(0, KC // 2) as i:
                for u in range(2):
                    dve_scale(dve, "ln1", i * 2 + u, u)
                for u in range(2):
                    k = i * 2 + u
                    dve.wait_ge(a_hi, k + 17)
                    dve.tensor_tensor(alo[:, ds(k * SEQ, SEQ)], xres[:, ds(k * SEQ, SEQ)],
                                      ahi[:, ds(k * SEQ, SEQ)].bitcast(F32), ALU.subtract).then_inc(a_lo, 1)
            n = C_FFN
            for gi, (g0, gc) in enumerate(FFN_GROUPS):
                with dve.Fori(0, gc) as i:
                    for u, cv in enumerate((conv_v, conv_g)):
                        split_lo(i * 2 + n + u + 1, 1 - u)
                        dve.wait_ge(conv_act, i * 2 + g0 * 2 + u + 1)
                        f = i + g0 + u * FCH
                        for back in (1, 2):
                            dve.scalar_tensor_tensor(out=cv[:, back:SEQ], in0=G[u][:, 0:SEQ - back],
                                                     scalar=vcol(0, f + (2 - back) * 44), in1=cv[:, back:SEQ],
                                                     op0=ALU.mult, op1=ALU.add).then_inc(conv_dve, 1)
                            dve.wait_ge(conv_dve, i * 4 + g0 * 4 + u * 2 + back)
                        dve.sem_inc(dve_read, 1)
                    dve.wait_ge(gelu_done, i + g0 + 1)
                    dve.wait_ge(h_hi, i + g0 + 1)
                    dve.tensor_tensor(hidden[:, :], conv_v[:, :], gelu_g[:, :], ALU.mult).then_inc(h_mul, 1)
                    dve.wait_ge(h_hi, i + g0 + 2)
                    dve.tensor_tensor(hlo[:, ds(i * SEQ, SEQ)], hidden[:, :], hhi[:, ds(i * SEQ, SEQ)].bitcast(F32),
                                      ALU.subtract).then_inc(h_lo, 1)
                    dve.wait_ge(h_lo, i + g0 + 1)
                n += 2 * gc
                with dve.Fori(0, KC // 2) as i:
                    for u in range(2):
                        j = i * 2 + u
                        split_lo(j + n + 1, 1 - u)
                        dve.wait_ge(gemm_done, j + n + 3)
                        xr = xres[:, ds(j * SEQ, SEQ)]
                        if gi == 0:
                            dve.scalar_tensor_tensor(out=xr, in0=xr, scalar=ALPHA, in1=G[u], op0=ALU.mult,
                                                     op1=ALU.add).then_inc(x_out, 1)
                        else:
                            dve.tensor_tensor(xr, xr, G[u], ALU.add).then_inc(x_out, 1)
                        dve.wait_ge(x_out, j + 8 * gi + 9)
                        dve.sem_inc(dve_read, 1)
                n += KC
            dve_stats(dve, "ln2")
            with dve.Fori(0, KC // 2) as i:
                for u in range(2):
                    dve_scale(dve, "ln2", i * 2 + u, u)
            mv = mods[:, :].rearrange("p (n two) -> p two n", two=2)
            for t, (who, n0, row) in enumerate(((0, 8, 32), (1, 8, 32), (0, 32, 40))):
                dve.scalar_tensor_tensor(out=gains[:, t * 8:(t + 1) * 8], in0=mv[:, who, n0:n0 + 8], scalar=1.0,
                                         in1=vecs[:, 2 * 96 + row:2 * 96 + row + 8], op0=ALU.add, op1=ALU.mult
                                         ).then_inc(gains_ready, 1)
            dve.sem_inc(ga_lo, 2)
            dve_stats(dve, "rms1")
            dve.wait_ge(ctx_full, 1)
            dve.tensor_scalar(cvar[:, :], BANK[6][:, 0:CTX], RMS_EPS, None, ALU.add).then_inc(ctx_st, 1)
            dve.wait_ge(ctx_sd, 1)
            dve.reciprocal(crs[:, :], csd[:, :]).then_inc(ctx_st, 1)
            dve_rms(dve, "rms1", gahi, galo, TOK, CTX, ga_hi, 0, ga_lo)
            dve.wait_ge(ctx_st, 2)
            dve.wait_ge(ctx_sq, 4)
            for k in range(KC + 1):
                if k < KC:
                    if k >= 2:
                        dve.wait_ge(cc_aff, k - 1)
                    dve.tensor_tensor(ccent[:, (k % 2) * CTX:(k % 2 + 1) * CTX], cxT[:, k * CTX:(k + 1) * CTX],
                                      crs[:, :], ALU.mult).then_inc(cc_mul, 1)
                if k >= 1:
                    q = k - 1
                    dve.wait_ge(ga_hi, KC + q + 1)
                    dve.tensor_tensor(galo[:, q * TOK:q * TOK + CTX], caff[:, (q % 2) * CTX:(q % 2 + 1) * CTX],
                                      gahi[:, q * TOK:q * TOK + CTX].bitcast(F32), ALU.subtract).then_inc(ga_lo, 1)
            dve.wait_ge(wa1_hi, 1)
            dve.tensor_tensor(wa1lo[:, :], wa1raw[:, :], wa1hi[:, :].bitcast(F32), ALU.subtract).then_inc(wa1_lo, 1)
            dve.sem_inc(o_gated, 2)
            dve.sem_inc(o_dve, 2)
            dve.wait_ge(masks_ready, 1)
            with dve.Fori(0, GH) as i:
                nz = i * 8
                for d in range(2):
                    bias = vecs[:, ds(i + 3 * 96 + 48 + d * GH, 1)]
                    cu = gcum[:, d * TOK:(d + 1) * TOK]
                    t1 = gex[:, TOK:2 * TOK]
                    o = d * 4
                    dve.wait_ge(z_act, i * 6 + d * 3 + 1)
                    dve.wait_ge(o_gated, i * 2 + 2)
                    dve.tensor_scalar(cu, GS[d][:, 0:TOK], bias, 0.0, ALU.add, ALU.min).then_inc(z_dve, 1)
                    Z1 = (1, 4)[d]
                    dve.wait_ge(z_act, i * 6 + d * 3 + 3)
                    dve.wait_ge(z_dve, nz + Z1)
                    dve.tensor_tensor(t1, cu, gex[:, 0:TOK], ALU.subtract).then_inc(z_dve, 1)
                    dve.wait_ge(z_dve, nz + Z1 + 1)
                    dve.tensor_tensor_scan(cu, restart[:, :], t1, 0.0, ALU.mult, ALU.add).then_inc(z_dve, 1)
                    dve.wait_ge(z_dve, nz + Z1 + 2)
                    dve.tensor_copy(tot[:, d * NCH:(d + 1) * NCH],
                                    cu.rearrange("p (c t) -> p c t", t=GCH)[:, :, GCH - 1]).then_inc(tots, 1)
                    if d == 1:
                        dve.wait_ge(tots, i * 2 + 2)
                        dve.tensor_tensor(cu, cu, t1, ALU.subtract).then_inc(gcum_ex, 1)
                        dve.wait_ge(gcum_ex, i + 1)

                def rest(d):
                    c3 = gcum[:, d * TOK:(d + 1) * TOK].rearrange("p (c t) -> p c t", t=GCH)
                    dve.tensor_tensor(c3, tot[:, d * NCH:(d + 1) * NCH].unsqueeze(2).broadcast_to([P, NCH, GCH]), c3,
                                      ALU.subtract).then_inc(z_dve, 1)

                def mul(e):
                    dst, src = (
                        (qd[:, 0:SEQ], qT[:, :]), (kn[:, 0:SEQ], kT[:, CTX:TOK]), (kd[:, 0:TOK], kT[:, :]),
                        (kd[:, TOK:2 * TOK], kT[:, :]), (qd[:, SEQ:2 * SEQ], qT[:, :]),
                        (kn[:, SEQ:2 * SEQ], kT[:, CTX:TOK]))[e]
                    w0 = 0 if e in (2, 3) else CTX
                    dve.wait_ge(gexp, i * 7 + e + 2)
                    dve.wait_ge(g_out, i * 6 + 2)
                    dve.tensor_tensor(dst, src, gex[:, (e % 2) * TOK + w0:(e % 2 + 1) * TOK], ALU.mult
                                      ).then_inc(gmul, 1)

                for j in range(6):
                    u = j % 2
                    n = i * 6 + C_GLA + j
                    split_lo(n + 1, 1 - u)
                    dve.sem_inc(dve_read, 1)
                    if j == 1:
                        mul(0)
                        mul(1)
                        rest(0)
                        mul(2)
                    if j == 2:
                        mul(3)
                        rest(1)
                        mul(4)
                        mul(5)
                    if j == 5:
                        dve.wait_ge(gmul, i * 6 + 6)
                        dve.memset(att_f[:, :], 0.0).then_inc(att_zero, 1)
                        dve.memset(att_b[:, :], 0.0).then_inc(att_zero, 1)
                        for f in range(2):
                            for q, blks in enumerate(GROUPS):
                                g = 6 + f * 3 + q
                                dve.wait_ge(tr_full, i * 12 + g + 2)
                                dve.tensor_copy(
                                    g_v[:, :].rearrange("p (b v) -> p b v", v=GDV)[
                                        :, blks[0]:blks[0] + len(blks), f * P:(f + 1) * P],
                                    BANK[6 + g % 2][:, 0:len(blks) * P].rearrange("p (b v) -> p b v", v=P)
                                ).then_inc(tr_dve, 1)
                for h in range(2):
                    dve.wait_ge(att_zero, i * 2 + 2)
                    dve.wait_ge(att_full, i * 2 + h + 1)
                    dve.memset(small[:, 2:3], 0.0)
                    for d, (a, m) in enumerate(((att_f, mask_f), (att_b, mask_b))):
                        dve.copy_predicated(a[:, h * 512:(h + 1) * 512], m[:, :], BANK[d][:, 0:512]).then_inc(att_set, 1)
                dve.wait_ge(att_set, i * 4 + 4)
                dve.tensor_tensor(att_f[:, :], att_f[:, :], att_b[:, :], ALU.add).then_inc(att_sum, 1)
                dve.wait_ge(gexp, i * 7 + 1)
                late = []
                for j in range(STEPS):
                    for d in range(2):
                        if j < STEPS - 1:
                            c = chunk_of(d, j)
                            dve.wait_ge(u_full, i * 38 + 2 * j + d + 1)
                            new = state[:, (d * 2 + (j + 1) % 2) * GDV:(d * 2 + (j + 1) % 2 + 1) * GDV]
                            old = state[:, (d * 2 + j % 2) * GDV:(d * 2 + j % 2 + 1) * GDV]
                            up = BANK[2 + 2 * d + j % 2][:, 0:GDV]
                            if j == 0:
                                dve.tensor_copy(new, up).then_inc(s_new, 1)
                            else:
                                dve.wait_ge(s_new, i * 38 + 2 * (j - 1) + d + 1)
                                dve.scalar_tensor_tensor(out=new, in0=old, scalar=etot[:, d * NCH + c:d * NCH + c + 1],
                                                         in1=up, op0=ALU.mult, op1=ALU.add).then_inc(s_new, 1)
                        for v_no, (jj, dd, b, v) in enumerate(visits()):
                            if (jj, dd) == (j - 1, d) and not first_visit(dd, b):
                                late.append((v_no, dd, b, v))
                        while late:
                            v_no, dd, b, v = late.pop(0)
                            dve_second(dve, i, v_no, dd, b, v)
                for v_no, (jj, dd, b, v) in enumerate(visits()):
                    if jj == STEPS - 1 and not first_visit(dd, b):
                        dve_second(dve, i, v_no, dd, b, v)
                dve.wait_ge(o_sq, i * 8 + 8)
                m = ossq[:, TB:2 * TB]
                dve.tensor_scalar(m, ossq[:, 0:TB], 1.0 / GDV, RMS_EPS, ALU.mult, ALU.add).then_inc(o_stat, 1)
                dve.wait_ge(o_sd, i + 1)
                dve.reciprocal(ossq[:, 2 * TB:3 * TB], m).then_inc(o_rec, 1)
                dve.wait_ge(o_rec, i + 1)
                for b in range(TB):
                    ob = o_tok[:, b * GDV:(b + 1) * GDV]
                    last = dve.tensor_scalar(ob, ob, ossq[:, 2 * TB + b:2 * TB + b + 1], None, ALU.mult)
                last.then_inc(o_norm, 1)
                for f in range(2):
                    dve.wait_ge(oT_full, i * 2 + f + 1)
                    rr = rT[:, f * SEQ:(f + 1) * SEQ]
                    dve.scalar_tensor_tensor(out=rr, in0=psum[:, f * SEQ:(f + 1) * SEQ],
                                             scalar=vecs[:, ds(i * 2 + 2 * 96 + 56 + f, 1)], in1=rr,
                                             op0=ALU.mult, op1=ALU.mult).then_inc(o_gated, 1)
            for k in range(KC):
                dve.wait_ge(a_hi, 3 * KC + k + 1)
                dve.tensor_tensor(alo[:, k * SEQ:(k + 1) * SEQ], xres[:, k * SEQ:(k + 1) * SEQ],
                                  ahi[:, k * SEQ:(k + 1) * SEQ].bitcast(F32), ALU.subtract).then_inc(a_lo, 1)
            with dve.Fori(0, KC // 2) as i:
                for u in range(2):
                    j = i * 2 + u
                    split_lo(j + C_WO + 1, 1 - u)
                    dve.wait_ge(gemm_done, j + C_WO + 3)
                    dve.wait_ge(xs_loaded, j * 16 + 16 * (KC + 1))
                    dve.scalar_tensor_tensor(out=xres[:, ds(j * SEQ, SEQ)], in0=G[u],
                                             scalar=mods[:, ds(j * 2 + 32, 1)], in1=xs[:, :],
                                             op0=ALU.mult, op1=ALU.add).then_inc(x_out, 1)
                    dve.wait_ge(x_out, j + 33)
                    dve.sem_inc(dve_read, 1)
            dve_stats(dve, "rms2")
            dve.sem_inc(a_lo, 2)
            dve_rms(dve, "rms2", ahi, alo, SEQ, 0, a_hi, 32, a_lo)
            n = C_MLP
            dve.sem_inc(sq_done, 1)
            dve.sem_inc(m_lo, 1)
            for g in range(MLP_GROUPS):
                with dve.Fori(0, KC // 2) as i:
                    for u in range(2):
                        j = i * 2 + u
                        split_lo(j + n + 1, 1 - u)
                        dve.wait_ge(relu_done, j + g * KC + 1)
                        dve.sem_inc(dve_read, 1)
                        dve.wait_ge(m_lo, j + g * KC + 1)
                        dve.tensor_tensor(sqr[:, :], relu[:, :], relu[:, :], ALU.mult).then_inc(sq_done, 1)
                        dve.wait_ge(m_hi, j + g * KC + 1)
                        dve.tensor_tensor(hlo[:, ds(j * SEQ, SEQ)], sqr[:, :], hhi[:, ds(j * SEQ, SEQ)].bitcast(F32),
                                          ALU.subtract).then_inc(m_lo, 1)
                n += KC
                def down(i, u):
                    j = i * 2 + u
                    if not (isinstance(i, int) and u == 1):
                        split_lo(j + n + 1, 1 - u)
                    dve.wait_ge(gemm_done, j + n + 3)
                    xr = xres[:, ds(j * SEQ, SEQ)]
                    dve.scalar_tensor_tensor(out=xr, in0=G[u], scalar=mods[:, ds(j * 2 + 80, 1)], in1=xr,
                                             op0=ALU.mult, op1=ALU.add).then_inc(x_out, 1)
                    dve.wait_ge(x_out, j + 41 + 8 * g)
                    dve.sem_inc(dve_read, 1)

                peeled(dve, g == MLP_GROUPS - 1, down)
                n += KC
            dve_stats(dve, "rmsf")
            for k in range(KC + 1):
                if k < KC:
                    dve_scale(dve, "rmsf", k, k % 2)
                if k >= 1:
                    q = k - 1
                    dve.wait_ge(out_T, q + 1)
                    if q >= 2:
                        dve.wait_ge(out_stored[q % 2], 16 * (q // 2))
                    dve.tensor_copy(ostage[:, (q % 2) * SEQ:(q % 2 + 1) * SEQ], G[q % 2]).then_inc(out_copied, 1)


_INS = ["x", "w_in", "b_forget", "rel_bias", "w_out", "ln1_g", "ln1_b", "w_up", "conv_w", "conv_b", "w_down", "ln2_g",
        "ln2_b", "c_2", "ctx_2", "c_ctx_2", "ada_w_2", "ada_b_2", "norm1_g_2", "norm2_g_2", "mlp_w1_2", "mlp_w2_2",
        "gla_w_in_2", "gla_w_a1_2", "gla_w_a2_2", "gla_b_a_2", "gla_g_head_2", "gla_w_o_2", "final_g_2"]


def kernel(**inputs):
    import numpy as _np
    import concourse.bacc as _bacc
    from concourse import mybir as _mybir
    from concourse.bass_utils import run_bass_kernel_spmd as _run

    nc = _bacc.Bacc("TRN2", target_bir_lowering=False, num_devices=1)
    arrays, args = {}, []
    for name in _INS:
        a = _np.ascontiguousarray(inputs[name])
        arrays[f"in_{name}_dram"] = a
        args.append(nc.dram_tensor(f"in_{name}_dram", a.shape, _mybir.dt.from_np(a.dtype), kind="ExternalInput").ap())
    args.append(nc.dram_tensor("out_0_dram", (1, SEQ, D), _mybir.dt.float32, kind="ExternalOutput").ap())
    program(nc, *args)
    r = _run(nc, [arrays], core_ids=[0])
    return r.results[0]["out_0_dram"]
```

```python
from contextlib import ExitStack

import concourse.bass as bass
from concourse import mybir

F32 = mybir.dt.float32
F32R = mybir.dt.float32r
BF16 = mybir.dt.bfloat16
U8 = mybir.dt.uint8
ALU = mybir.AluOpType
ACT = mybir.ActivationFunctionType
AX_X = mybir.AxisListType.X
ds = bass.ds

P = 128
SEQ = 1024
CTX = 256
TOK = SEQ + CTX
D = 1024
KC = D // P
TB = SEQ // P
HD = 64
NHEAD = 8
PAIRS = NHEAD // 2
D_A = NHEAD * HD
DFF = 2816
FCH = DFF // P
FFN_GROUPS = [(0, 8), (8, 8), (16, 6)]
REL = 128
NREL = 2 * REL + 1
LEFT = 4
ALPHA = 2.0 ** 0.25
LN_EPS = 1e-5
RMS_EPS = 1e-6
NEG = -1.0e30
QK_SCALE = HD ** -0.5

ADA_STEP = 12

GH = 4
GDK = 128
GDV = 256
GCH = 64
NCH_CTX = CTX // GCH
NCH = TOK // GCH
NPAIR = TOK // P
LPAIR0 = CTX // P
RANK = 16
TAU = 16.0
MLP_GROUPS = 4

C_ATT = 0
C_WOUT = C_ATT + 6 * PAIRS
C_FFN = C_WOUT + KC
C_GLA = C_FFN + sum(2 * g for _, g in FFN_GROUPS) + KC * len(FFN_GROUPS)
C_WO = C_GLA + 6 * GH
C_MLP = C_WO + KC
C_END = C_MLP + 2 * KC * MLP_GROUPS


def program(nc, x, w_in, b_forget, rel_bias, w_out, ln1_g, ln1_b, w_up, conv_w, conv_b, w_down, ln2_g, ln2_b,
            c_2, ctx_2, c_ctx_2, ada_w, ada_b, norm1_g, norm2_g, mlp_w1, mlp_w2, gla_w_in, gla_w_a1, gla_w_a2,
            gla_b_a, gla_g_head, gla_w_o, final_g, out):
    with ExitStack() as ctx:
        sem = lambda name: ctx.enter_context(nc.semaphore(name))
        base0 = (nc.sbuf_base + 31) // 32 * 32

        def at(name, kb, shape, dt):
            return nc.alloc_sbuf_tensor_at(name, shape, dt, offset=base0 + int(kb * 1024))

        whi = at("whi", 0, [P, 2, KC * P], F32R)
        wlo = at("wlo", 8, [P, 2, KC * P], F32R)
        wraw = at("wraw", 16, [P, 2, KC * P], F32)
        const0 = 24
        ident = at("ident", const0, [P, P], F32)
        ones = at("ones", const0 + .5, [P, P], F32)
        vecs = at("vecs", const0 + 1, [P, 4 * 96], F32)
        mods = at("mods", const0 + 2.5, [P, 96], F32)
        small = at("small", const0 + 2.875, [P, 32], F32)
        x0 = 27
        xres = at("xres", x0, [P, KC * SEQ], F32)
        a0 = x0 + 32
        ahi = at("ahi", a0, [P, KC * SEQ], F32R)
        alo = at("alo", a0 + 32, [P, KC * SEQ], F32R)
        r0 = a0 + 64

        set0 = (x0, r0)
        q2 = [at(f"q2_{h}", set0[h], [P, 2 * SEQ], F32R) for h in range(2)]
        khh = [at(f"khh_{h}", set0[h] + 8, [P, 2 * SEQ], F32R) for h in range(2)]
        kll = [at(f"kll_{h}", set0[h] + 16, [P, 2 * SEQ], F32R) for h in range(2)]
        stage = at("stage", r0 + 24, [P, SEQ], F32)
        vtok = [at(f"vtok_{h}", (x0 + 24, r0 + 28)[h], [P, TB * P], F32) for h in range(2)]
        ystage = xres[:, (KC - 1) * SEQ:KC * SEQ]
        prob = at("prob", r0 + 32, [P, 2 * SEQ], F32)
        probT = at("probT", r0 + 40, [P, 2 * SEQ], F32)
        relT = at("relT", r0 + 48, [P, NHEAD * 256], F32)
        cumL = at("cumL", r0 + 56, [6, 2 * SEQ], BF16)
        cumR = at("cumR", r0 + 60, [6, 2 * SEQ], BF16)
        identb = at("identb", r0 + 64, [P, P], BF16)
        maskb = at("maskb", r0 + 64.25, [P, P], BF16)
        mstat = at("mstat", r0 + 64.5, [P, 64], F32)
        rdiag = at("rdiag", r0 + 82, [P, 2 * P], F32)
        xin = at("xin", r0, [P, TB * D], F32)
        vrow = at("vrow", r0 + 32, [P, 4 * P], F32)
        wf = at("wf", r0 + 34, [P, KC * NHEAD], F32)
        flip = at("flip", r0 + 34.5, [P, P], F32)
        adaring = at("adaring", r0 + 65, [P, 4 * KC * P], F32)
        csil = at("csil", r0 + 81, [P, 2 * KC], F32)
        lf = at("lf", r0, [NHEAD, 4 * SEQ], F32)
        cumLs = at("cumLs", r0 + 48, [NHEAD, 6 * SEQ], BF16)
        cumRs = at("cumRs", r0 + 36, [NHEAD, 6 * SEQ], BF16)
        relx = at("relx", r0 + 28, [NHEAD, 512], F32)
        hank = at("hank", r0 + 16, [P, NHEAD * 256], F32)

        hhi = at("hhi", r0, [P, 8 * SEQ], F32R)
        hlo = at("hlo", r0 + 32, [P, 8 * SEQ], F32R)
        conv_v = at("conv_v", r0 + 64, [P, SEQ], F32)
        conv_g = at("conv_g", r0 + 68, [P, SEQ], F32)
        gelu_g = at("gelu_g", r0 + 72, [P, SEQ], F32)
        hidden = at("hidden", r0 + 76, [P, SEQ], F32)
        xs = at("xs", r0 + 64, [P, SEQ], F32)
        sums = at("sums", r0 + 72, [P, SEQ], F32)
        sumq = at("sumq", r0 + 76, [P, SEQ], F32)
        sqt = at("sqt", r0 + 80, [P, SEQ], F32)
        mean = at("mean", r0 + 16, [P, SEQ], F32)
        tstat = at("tstat", r0 + 20, [P, 5 * TB], F32)
        rdiag8 = at("rdiag8", r0 + 24, [P, SEQ], F32)
        cent = at("cent", r0 + 32, [P, 2 * SEQ], F32)
        aff = at("aff", r0 + 40, [P, 2 * SEQ], F32)
        gahi = at("gahi", a0, [P, KC * TOK], F32R)
        galo = at("galo", a0 + 40, [P, KC * TOK], F32R)
        cin = at("cin", r0 + 48, [P, 2 * D], F32)
        cxT = at("cxT", r0 + 56, [P, KC * CTX], F32)
        csq = at("csq", r0 + 64, [P, KC * CTX], F32)
        crs = at("crs", r0 + 16, [P, CTX], F32)
        cvar = at("cvar", r0 + 17, [P, CTX], F32)
        csd = at("csd", r0 + 18, [P, CTX], F32)
        ccent = at("ccent", r0 + 48, [P, 2 * CTX], F32)
        caff = at("caff", r0 + 50, [P, 2 * CTX], F32)
        gains = small[:, 8:32]
        gT = at("gT", x0, [P, TOK], F32)
        qT = at("qT", x0 + 5, [P, SEQ], F32)
        kT = at("kT", x0 + 9, [P, TOK], F32)
        vst = at("vst", x0 + 14, [P, TOK], F32)
        rT = at("rT", x0 + 19, [P, 2 * SEQ], F32)
        state = at("state", x0 + 27, [P, 4 * GDV], F32)
        tot = at("tot", x0 + 31, [P, 2 * NCH], F32)
        etot = at("etot", x0 + 31.25, [P, 2 * NCH], F32)
        ossq = at("ossq", x0 + 31.5, [P, 3 * TB], F32)
        wa2 = at("wa2", x0 + 14, [P, P], F32)
        g0_ = r0 + 16
        g_v = at("g_v", g0_, [P, NPAIR * GDV], F32)
        gcum = at("gcum", g0_ + 10, [P, 2 * TOK], F32)
        gex = at("gex", g0_ + 20, [P, 2 * TOK], F32)
        qd = at("qd", g0_ + 30, [P, 2 * SEQ], F32)
        kn = at("kn", g0_ + 38, [P, 2 * SEQ], F32)
        kd = at("kd", g0_ + 46, [P, 2 * TOK], F32)
        kdt = at("kdt", g0_ + 56, [P, 2 * TOK], F32)
        mask_f = at("mask_f", g0_ + 66, [P, 512], U8)
        mask_b = at("mask_b", g0_ + 66.5, [P, 512], U8)
        restart = at("restart", g0_ + 67, [P, TOK], U8)
        o_tok = at("o_tok", g0_ + 10, [P, TB * GDV], F32)
        att_f = at("att_f", g0_ + 20, [P, TB * P], F32)
        att_b = at("att_b", g0_ + 24, [P, TB * P], F32)
        osq = at("osq", g0_ + 28, [P, GDV], F32)
        wa1raw = at("wa1raw", r0 + 52, [P, KC * P], F32)
        wa1hi = at("wa1hi", r0 + 64, [P, KC * P], F32R)
        wa1lo = at("wa1lo", r0 + 68, [P, KC * P], F32R)
        mtmp = at("mtmp", g0_ + 12, [P, TOK], F32)
        relu = at("relu", r0 + 64, [P, SEQ], F32)
        sqr = at("sqr", r0 + 68, [P, SEQ], F32)
        ostage = at("ostage", r0 + 48, [P, 2 * SEQ], F32)

        psum = ctx.enter_context(nc.psum_tensor("ps", [P, 8 * 512], F32))
        G = [psum[:, 0:1024], psum[:, 1024:2048]]
        AUX = [psum[:, 2048:2560], psum[:, 2560:3072]]
        YP = psum[:, 3072:4096]
        YB, HB = psum[:, 3072:3584], psum[:, 3584:4096]
        AUXW = psum[:, 2048:3072]
        GS = [psum[:, 0:1536], psum[:, 1536:3072]]
        BANK = [psum[:, b * 512:(b + 1) * 512] for b in range(8)]

        xT_d = nc.dram_tensor("xT_scratch", [P, KC * SEQ], F32, kind="Internal").ap()
        cumL_d = nc.dram_tensor("cumL_scratch", [NHEAD, 6 * SEQ], BF16, kind="Internal").ap()
        cumR_d = nc.dram_tensor("cumR_scratch", [NHEAD, 6 * SEQ], BF16, kind="Internal").ap()
        y_d = nc.dram_tensor("y_scratch", [P, KC * SEQ], F32, kind="Internal").ap()
        x2_d = nc.dram_tensor("x2_scratch", [P, KC * SEQ], F32, kind="Internal").ap()
        oT_d = nc.dram_tensor("oT_scratch", [P, KC * SEQ], F32, kind="Internal").ap()
        rel_d = nc.dram_tensor("rel_scratch", [NHEAD, 512], F32, kind="Internal").ap()

        raw_loaded = [sem("raw_loaded0"), sem("raw_loaded1")]
        w_hi, w_lo = sem("w_hi"), sem("w_lo")
        gemm_done = sem("gemm_done")
        act_read, dve_read = sem("act_read"), sem("dve_read")
        a_hi, a_lo = sem("a_hi"), sem("a_lo")
        x_loaded = sem("x_loaded")
        consts_ready = sem("consts_ready")
        vec_loaded, vec_zero, vec_T, vec_cols = sem("vec_loaded"), sem("vec_zero"), sem("vec_T"), sem("vec_cols")
        xT_full = sem("xT_full")
        xT_copied, xT_spilled = sem("xT_copied"), sem("xT_spilled")
        small_loaded = sem("small_loaded")
        f_full, f_act, f_dve = sem("f_full"), sem("f_act"), sem("f_dve")
        cum_ready, cum_stored = sem("cum_ready"), sem("cum_stored")
        rel_ready, rel_stored, hank_loaded, rel_full, rel_done = (
            sem("rel_ready"), sem("rel_stored"), sem("hank_loaded"), sem("rel_full"), sem("rel_done"))
        cum_loaded = sem("cum_loaded")
        c_silu, ada_used = sem("c_silu"), sem("ada_used")
        ada_loaded = [sem(f"ada_loaded{i}") for i in range(4)]
        side_full, side_act, side_dve, side_hi, side_lo = (
            sem("side_full"), sem("side_act"), sem("side_dve"), sem("side_hi"), sem("side_lo"))
        y_stored, y_left, y_loaded = sem("y_stored"), sem("y_left"), sem("y_loaded")
        s_full, max_ready, exp_done, p_ready = sem("s_full"), sem("max_ready"), sem("exp_done"), sem("p_ready")
        bias_in = sem("bias_in")
        rinv_ready = sem("rinv_ready")
        pt_full, pt_act, pt_dve = sem("pt_full"), sem("pt_act"), sem("pt_dve")
        pv_done, y_out = sem("pv_done"), sem("y_out")
        xs_loaded = sem("xs_loaded")
        x_out, sq_ready, s_added, q_added, sums_zero = (
            sem("x_out"), sem("sq_ready"), sem("s_added"), sem("q_added"), sem("sums_zero"))
        tok_stat, spread_ready, rstd_full, mean_full = (
            sem("tok_stat"), sem("spread_ready"), sem("rstd_full"), sem("mean_full"))
        stat_full, stat_act, stat_dve = sem("stat_full"), sem("stat_act"), sem("stat_dve")
        n_cent, n_mul, n_aff = sem("n_cent"), sem("n_mul"), sem("n_aff")
        h_hi, h_lo = sem("h_hi"), sem("h_lo")
        ga_hi, ga_lo = sem("ga_hi"), sem("ga_lo")
        conv_act, conv_dve, gelu_done, h_mul = sem("conv_act"), sem("conv_dve"), sem("gelu_done"), sem("h_mul")
        gains_ready = sem("gains_ready")
        x2_spilled, ctx_loaded, wa1_loaded, wa1_zero = (
            sem("x2_spilled"), sem("ctx_loaded"), sem("wa1_loaded"), sem("wa1_zero"))
        ctx_T, ctx_sq, ctx_full, ctx_st, ctx_sd = (
            sem("ctx_T"), sem("ctx_sq"), sem("ctx_full"), sem("ctx_st"), sem("ctx_sd"))
        cc_mul, cc_aff = sem("cc_mul"), sem("cc_aff")
        masks_ready, mask_step = sem("masks_ready"), sem("mask_step")
        wa1_hi, wa1_lo, low_full, low_out = sem("wa1_hi"), sem("wa1_lo"), sem("low_full"), sem("low_out")
        wa2_loaded, z_full, z_act, z_dve = sem("wa2_loaded"), sem("z_full"), sem("z_act"), sem("z_dve")
        g_out, gexp, gmul, tots = sem("g_out"), sem("gexp"), sem("gmul"), sem("tots")
        tr_full, tr_act, tr_dve = sem("tr_full"), sem("tr_act"), sem("tr_dve")
        att_zero, att_full, att_set, att_sum = sem("att_zero"), sem("att_full"), sem("att_set"), sem("att_sum")
        u_full, s_new, o_full, o_act, o_dve = sem("u_full"), sem("s_new"), sem("o_full"), sem("o_act"), sem("o_dve")
        o_sq, o_stat, o_sd, o_norm, oT_full, o_gated, o_spilled = (
            sem("o_sq"), sem("o_stat"), sem("o_sd"), sem("o_norm"), sem("oT_full"), sem("o_gated"), sem("o_spilled"))
        o_left = sem("o_left")
        oT_loaded, gcum_ex, o_rec = sem("oT_loaded"), sem("gcum_ex"), sem("o_rec")
        relu_done, sq_done, m_hi, m_lo = sem("relu_done"), sem("sq_done"), sem("m_hi"), sem("m_lo")
        out_T, out_copied, out_stored = sem("out_T"), sem("out_copied"), [sem("out_stored0"), sem("out_stored1")]

        w_cols = {
            "in": w_in[0].rearrange("(k p) n -> p k n", p=P),
            "out": w_out[0].rearrange("(k p) n -> p k n", p=P),
            "up": w_up[0].rearrange("(k p) n -> p k n", p=P),
            "gla": gla_w_in[0].rearrange("(k p) n -> p k n", p=P),
            "o": gla_w_o[0].rearrange("(k p) n -> p k n", p=P),
            "m1": mlp_w1[0].rearrange("(k p) n -> p k n", p=P),
            "m2": mlp_w2[0].rearrange("(k p) n -> p k n", p=P),
            "down": w_down[0].rearrange("(k p) n -> p k n", p=P),
        }

        def raw3(u):
            return wraw[:, u, :].rearrange("p (k n) -> p k n", n=P)

        QA, KA, VA = 0, D_A, 2 * D_A
        QB, KB, VB = 3 * D_A + NHEAD, 4 * D_A + NHEAD, 5 * D_A + NHEAD
        ATT_COLS = [QA, KA, VA, QB, KB, VB]

        def split_hi(n, half):
            u = half[0]
            act = nc.scalar
            act.wait_ge(raw_loaded[u], half[1])
            act.wait_ge(gemm_done, n + 1)
            act.copy(whi[:, u, :], wraw[:, u, :]).then_inc(w_hi, 1)

        def split_hi_next(i, base, u):
            split_hi(i * 2 + base + u + 2, (u, i * 16 + (base // 2 + 2) * 16))

        def split_lo(n, u, dve=nc.vector):
            dve.wait_ge(w_hi, n + 3)
            dve.tensor_tensor(wlo[:, u, :], wraw[:, u, :], whi[:, u, :].bitcast(F32), ALU.subtract).then_inc(w_lo, 1)

        def load_chunk(n, u, src):
            sp = nc.sync
            sp.wait_ge(w_hi, n + 1)
            sp.wait_ge(w_lo, n + 1)
            k = src.shape[1]
            sp.dma_start(raw3(u)[:, 0:k, :], src).then_inc(raw_loaded[u], 16)

        def product(n, u, kc, hi, lo, width, ready):
            pe = nc.tensor
            pe.wait_ge(w_hi, n + 3)
            pe.wait_ge(w_lo, n + 3)
            pe.wait_ge(act_read, n + 1)
            pe.wait_ge(dve_read, n + 1)
            dst = G[u]
            for k in range(kc):
                if ready is not None:
                    pe.wait_ge(ready[0], ready[2] + k + 1 + (ready[3] if len(ready) > 3 else 0))
                    pe.wait_ge(ready[1], ready[2] + k + 1 + (ready[4] if len(ready) > 4 else 0))
                wh, wl = whi[:, u, k * P:(k + 1) * P], wlo[:, u, k * P:(k + 1) * P]
                for w, a in ((wh, hi), (wh, lo), (wl, hi)):
                    for t in range(0, width, 512):
                        e = min(512, width - t)
                        last = pe.matmul(dst[:, t:t + e], w, a[:, k * width + t:k * width + t + e],
                                         start=(k == 0 and w is wh and a is hi),
                                         stop=(k == kc - 1 and w is wl))
            last.then_inc(gemm_done, 1)

        UNITS = [(e, b) for b in range(TB) for e in range(2)]

        SIDE = [("q", 0, (0, 1)), ("q", 1, (2, 3)), ("ada", 0, (4,)), ("k", 0, (5, 6)), ("k", 1, (7, 8)),
                ("v", 0, (9, 10)), ("v", 1, (11, 12)), ("ada", 1, (13,)), ("turn", 0, (14,)), ("turn", 1, (15,))]
        NS = len(SIDE)
        BY_ACT, BY_DVE = ("q", "k", "v"), ("ada", "turn")
        NA = sum(1 for x in SIDE if x[0] in BY_ACT)
        ND = sum(1 for x in SIDE if x[0] in BY_DVE)

        def taken(by, m):
            return sum(1 for x in SIDE[:m] if x[0] in by)

        def pe_side(pe, i, ofs, m, part, bank):
            kind, t, units = SIDE[m]
            parts = len(units)
            if part == 0 and (ofs or m >= 2):
                back = 1 if ofs == 0 else 0
                if ofs or taken(BY_ACT, m - back):
                    pe.wait_ge(side_act, i * 2 * NA + ofs * NA + taken(BY_ACT, m - back))
                if ofs or taken(BY_DVE, m - back):
                    pe.wait_ge(side_dve, i * 2 * ND + ofs * ND + taken(BY_DVE, m - back))
            if kind in BY_ACT:
                j = "qkv".index(kind)
                u = (3 * ofs + j) % 2
                if part == 0 and t == 0:
                    pe.wait_ge(w_hi, i * 6 + C_ATT + 3 * ofs + j + 3)
                    pe.wait_ge(w_lo, i * 6 + C_ATT + 3 * ofs + j + 3)
                for k in range(part * KC // parts, (part + 1) * KC // parts):
                    if ofs == 0 and m == 0:
                        pe.wait_ge(a_hi, k + 1)
                        pe.wait_ge(a_lo, k + 1)
                    wh, wl = whi[:, u, k * P:(k + 1) * P], wlo[:, u, k * P:(k + 1) * P]
                    for w, a in ((wh, ahi), (wh, alo), (wl, ahi)):
                        last = pe.matmul(bank, w, a[:, k * SEQ + t * 512:k * SEQ + t * 512 + 512],
                                         start=(k == 0 and w is wh and a is ahi), stop=(k == KC - 1 and w is wl))
            elif kind == "ada":
                for q in range(3):
                    c = 6 * ofs + 3 * t + q
                    s = c % 4
                    pe.wait_ge(ada_loaded[s], i * (16 * ADA_STEP // 4) + (c // 4 + 1) * 16)
                    for k in range(KC):
                        last = pe.matmul(bank[:, 2 * q:2 * q + 2], adaring[:, s * D + k * P:s * D + (k + 1) * P],
                                         csil[:, 2 * k:2 * k + 2], start=(k == 0), stop=(k == KC - 1))
                    if q < 2:
                        last.then_inc(ada_used, 1)
                last.then_inc(ada_used, 1)
                pe.wait_ge(ada_used, i * ADA_STEP + 6 * ofs + 3 * t + 3 + 4)
                pe.sem_inc(side_full, 1)
                return
            else:
                for b in range(4):
                    last = pe.transpose(bank[:, b * P:(b + 1) * P], stage[:, (t * 4 + b) * P:(t * 4 + b + 1) * P],
                                        ident[:, :])
            if part == parts - 1:
                last.then_inc(side_full, 1)

        def act_side(act, i, ofs, m, bank):
            kind, t, _ = SIDE[m]
            if kind not in BY_ACT:
                return
            j = "qkv".index(kind)
            h = ofs % 2
            act.wait_ge(side_full, i * 2 * NS + ofs * NS + m + 1)
            st = stage[:, t * 512:(t + 1) * 512]
            if kind != "q":
                act.wait_ge(side_lo, i * 24 + ofs * 12 + (0, 0, 0, 2, 4, 8, 12)[m])
            n_act = i * 2 * NA + ofs * NA + taken(BY_ACT, m + 1)
            if kind == "q":
                act.mul(st, bank, QK_SCALE).then_inc(side_act, 1)
            else:
                act.copy(st, bank).then_inc(side_act, 1)
            act.wait_ge(side_act, n_act)
            for e in range(2):
                rows = slice(e * 64, (e + 1) * 64)
                c = slice(e * SEQ + t * 512, e * SEQ + (t + 1) * 512)
                if kind == "q":
                    act.copy(q2[h][rows, c], st[rows, :]).then_inc(side_hi, 1)
                elif kind == "k":
                    for r in range(2):
                        act.copy(khh[h][r * 64:(r + 1) * 64, c], st[rows, :]).then_inc(side_hi, 1)
            if t == 1:
                act.sem_inc(gemm_done, 1)
            if t == 0:
                c = 3 * ofs + j + 1
                split_hi(i * 6 + C_ATT + c, (c % 2, i * 48 + (c // 2 + 1) * 16))

        def lo_side(eng, i, ofs, m):
            kind, t, _ = SIDE[m]
            h = ofs % 2
            if kind not in BY_ACT:
                return
            if kind != "v":
                eng.wait_ge(side_hi, i * 24 + ofs * 12 + (2, 4, 0, 8, 12)[m])
                st = stage[:, t * 512:(t + 1) * 512]
                done = i * 24 + ofs * 12 + (0, 2, 0, 4, 8)[m]

                def step(ins, n):
                    ins.then_inc(side_lo, 1)
                    eng.wait_ge(side_lo, done + n)

                for e in range(2):
                    rows = slice(e * 64, (e + 1) * 64)
                    c = slice(e * SEQ + t * 512, e * SEQ + (t + 1) * 512)
                    if kind == "q":
                        step(eng.tensor_tensor(q2[h][(1 - e) * 64:(2 - e) * 64, c], st[rows, :],
                                               q2[h][rows, c].bitcast(F32), ALU.subtract), e + 1)
                    else:
                        for r in range(2):
                            step(eng.tensor_tensor(kll[h][r * 64:(r + 1) * 64, c], st[rows, :],
                                                   khh[h][rows, c].bitcast(F32), ALU.subtract), 2 * e + r + 1)
            if t == 0:
                c = 3 * ofs + "qkv".index(kind) + 1
                split_lo(i * 6 + C_ATT + c, c % 2, eng)
                eng.wait_ge(w_lo, i * 6 + C_ATT + c + 3)

        def dve_side(dve, i, ofs, m, bank):
            kind, t, _ = SIDE[m]
            h = ofs % 2
            if kind in BY_ACT:
                return
            dve.wait_ge(side_full, i * 2 * NS + ofs * NS + m + 1)
            if kind == "ada":
                c = 6 * ofs + 3 * t
                dve.tensor_tensor(mods[:, ds(i * 2 * ADA_STEP + 2 * c, 6)].rearrange("p (n two) -> p n two", two=2),
                                  bank[:, 0:6].rearrange("p (n two) -> p n two", two=2),
                                  vecs[:, ds(i * ADA_STEP + 3 * 96 + c, 3)].unsqueeze(2).broadcast_to([P, 3, 2]),
                                  ALU.add).then_inc(side_dve, 1)
            else:
                dve.tensor_copy(vtok[h][:, t * 512:(t + 1) * 512], bank).then_inc(side_dve, 1)

        def blocks(kind, b):
            return list(range(b + 1)) if kind == "A" else list(range(max(0, b - LEFT), b + 1))

        def pe_qk(pe, i, ofs, u):
            half = ofs % 2
            kind = "AB"[half]
            e, b = UNITS[u]
            kb = blocks(kind, b)
            slot = G[u % 2]
            if u == 0:
                pe.wait_ge(side_hi, i * 24 + ofs * 12 + 12)
                pe.wait_ge(side_lo, i * 24 + ofs * 12 + 12)
                if kind == "A":
                    pe.wait_ge(cum_loaded, i * 64 + (1 + ofs // 2) * 64)
            pe.wait_ge(exp_done, i * 32 + ofs * 16 + u + 1)
            n0, n = kb[0] * P, len(kb) * P
            qs = q2[half][:, e * SEQ + b * P:e * SEQ + (b + 1) * P]
            for t in range(0, n, 512):
                w = min(512, n - t)
                o = slot[:, t:t + w]
                c = e * SEQ + n0 + t
                final = kind == "B"
                pe.matmul(o, qs, khh[half][:, c:c + w], start=True, stop=False)
                last = pe.matmul(o, qs, kll[half][:, c:c + w], start=False, stop=final)
                if kind == "A":
                    diag = t + w == n
                    last = pe.matmul(o, cumL[:, e * SEQ + b * P:e * SEQ + (b + 1) * P], cumR[:, c:c + w],
                                     start=False, stop=not diag)
                    if diag:
                        last = pe.matmul(slot[:, n - P:n], identb[:, :], maskb[:, :], start=False, stop=True)
            last.then_inc(s_full, 1)

        def pe_attention(pe, half, i, final):
            kind = "AB"[half]
            un = i * 32 + half * 16
            nv = i * 2 + half

            def turn(u):
                e, b = UNITS[u]
                kb = blocks(kind, b)
                pe.wait_ge(p_ready, un + u + 1)
                for hf in range(2):
                    js = [j for j in range(len(kb)) if j // 4 == hf]
                    pe.wait_ge((pt_act, pt_dve)[hf], un + u + 1)
                    for j in js:
                        last = pe.matmul(AUX[hf][:, (j % 4) * P:(j % 4 + 1) * P],
                                         prob[:, (u % 2) * SEQ + j * P:(u % 2) * SEQ + (j + 1) * P],
                                         rdiag[:, (u % 2) * P:(u % 2 + 1) * P], start=True, stop=True)
                last.then_inc(pt_full, 1)

            def pv(u):
                e, b = UNITS[u]
                kb = blocks(kind, b)
                pe.wait_ge(pt_act, un + u + 2)
                pe.wait_ge(pt_dve, un + u + 2)
                if u == 0:
                    pe.wait_ge(side_dve, nv * ND + ND)
                if u % 8 == 0:
                    pe.wait_ge(y_out, nv * 2 + u // 8 + 1)
                for j, k in enumerate(kb):
                    last = pe.matmul(YB[e * HD:(e + 1) * HD, (b % 4) * P:(b % 4 + 1) * P],
                                     vtok[half][:, k * P + e * HD:k * P + (e + 1) * HD],
                                     probT[:, (u % 2) * SEQ + j * P:(u % 2) * SEQ + (j + 1) * P],
                                     start=(j == 0), stop=(j == len(kb) - 1))
                last.then_inc(pv_done, 1)

            for u in range(16):
                if u + 1 < 16:
                    pe_qk(pe, i, half, u + 1)
                elif not final:
                    pe_qk(pe, i, half + 1, 0)
                if not final:
                    for m, (_, _, units) in enumerate(SIDE):
                        if u in units:
                            pe_side(pe, i, half + 1, m, units.index(u), HB)
                turn(u)
                if u >= 1:
                    pv(u - 1)
            pv(15)

        def act_exp(act, i, ofs, u):
            kind = "AB"[ofs % 2]
            e, b = UNITS[u]
            n = len(blocks(kind, b)) * P
            un = i * 32 + ofs * 16
            act.wait_ge(max_ready, un + u + 1)
            act.wait_ge(pt_full, un + u + 1)
            s = 3 * (u % 2)
            act.activation(prob[:, (u % 2) * SEQ:(u % 2) * SEQ + n], G[u % 2][:, 0:n], ACT.Exp,
                           bias=mstat[:, s:s + 1], accum_out=mstat[:, s + 1:s + 2]).then_inc(exp_done, 1)

        def act_attention(act, half, i, final):
            kind = "AB"[half]
            un = i * 32 + half * 16
            nv = i * 2 + half

            def evac(u):
                e, b = UNITS[u]
                n = min(4, len(blocks(kind, b))) * P
                act.wait_ge(pt_full, un + u + 3)
                act.wait_ge(pv_done, un + u + 1)
                act.copy(probT[:, (u % 2) * SEQ:(u % 2) * SEQ + n], AUX[0][:, 0:n]).then_inc(pt_act, 1)

            def results(t):
                act.wait_ge(pv_done, un + 8 * (t + 1) + 2)
                act.wait_ge(y_left, nv * 2 + t + 1)
                act.copy(ystage[:, t * 512:(t + 1) * 512], YB).then_inc(y_out, 1)

            for u in range(16):
                if u >= 1:
                    evac(u - 1)
                if u + 1 < 16:
                    act_exp(act, i, half, u + 1)
                elif not final:
                    act_exp(act, i, half + 1, 0)
                if u == 9:
                    results(0)
                if not final:
                    for m, (_, _, units) in enumerate(SIDE):
                        if u == units[-1]:
                            act_side(act, i, half + 1, m, HB)
            evac(15)
            results(1)

        def wide(u):
            return len(blocks("B", UNITS[u][1])) == LEFT + 1

        NB_B = sum(2 if wide(u) else 1 for u in range(len(UNITS)))

        def dve_max(dve, i, ofs, u):
            kind = "AB"[ofs % 2]
            e, b = UNITS[u]
            n = len(blocks(kind, b)) * P
            un = i * 32 + ofs * 16
            s = 3 * (u % 2)
            slot = G[u % 2]
            dve.wait_ge(s_full, un + u + 1)
            if kind == "B":
                w = min(n, 256)
                dve.tensor_tensor(slot[:, n - w:n], slot[:, n - w:n],
                                  relT[:, ds(i * 512 + e * 256 + 256 - w, w)], ALU.add).then_inc(bias_in, 1)
                if wide(u):
                    dve.memset(slot[64:128, 0:64], NEG).then_inc(bias_in, 1)
                dve.wait_ge(bias_in, i * NB_B + sum(2 if wide(v) else 1 for v in range(u + 1)))
            dve.wait_ge(exp_done, un + u + 1)
            dve.reduce_max(mstat[:, s:s + 1], slot[:, 0:n], AX_X, negate=True).then_inc(max_ready, 1)

        def dve_attention(dve, half, i, final):
            kind = "AB"[half]
            un = i * 32 + half * 16

            def norm(u):
                s = 3 * (u % 2)
                dve.wait_ge(exp_done, un + u + 3)
                dve.reciprocal(mstat[:, s + 2:s + 3], mstat[:, s + 1:s + 2]).then_inc(rinv_ready, 1)
                dve.wait_ge(rinv_ready, un + u + 1)
                dve.tensor_scalar(rdiag[:, (u % 2) * P:(u % 2 + 1) * P], ident[:, :], mstat[:, s + 2:s + 3], None,
                                  ALU.mult).then_inc(p_ready, 1)

            def evac(u):
                e, b = UNITS[u]
                n = max(0, len(blocks(kind, b)) - 4) * P
                dve.wait_ge(pt_full, un + u + 3)
                if n == 0:
                    dve.wait_ge(pt_dve, un + u + 1)
                    dve.sem_inc(pt_dve, 1)
                    return
                dve.wait_ge(pv_done, un + u + 1)
                dve.tensor_copy(probT[:, (u % 2) * SEQ + 512:(u % 2) * SEQ + 512 + n], AUX[1][:, 0:n]
                                ).then_inc(pt_dve, 1)

            for u in range(16):
                norm(u)
                if u >= 1:
                    evac(u - 1)
                if u + 1 < 16:
                    dve_max(dve, i, half, u + 1)
                elif not final:
                    dve_max(dve, i, half + 1, 0)
                if not final:
                    for m, (_, _, units) in enumerate(SIDE):
                        if u == units[-1]:
                            dve_side(dve, i, half + 1, m, HB)
            evac(15)

        SETUP_BANKS = (HB, YB)


        NORMS = {
            "ln1": dict(sq=0, s=0, st=0, sa=0, sd=0, ce=0, mu=0, af=0),
            "ln2": dict(sq=8, s=8, st=1, sa=2, sd=2, ce=8, mu=8, af=8),
            "rms1": dict(sq=16, st=2, sa=4, sd=4, mu=16, af=16),
            "rms2": dict(sq=24, st=3, sa=5, sd=6, mu=24, af=24),
            "rmsf": dict(sq=32, st=4, sa=6, sd=8, mu=32, af=32),
        }
        LNV = {"ln1": 0, "ln2": 16}

        def vcol(t, row):
            return vecs[:, ds(row + t * 96, 1)]

        def act_square(act, j, sq, src):
            act.wait_ge(q_added, j + sq + 1)
            act.activation(sqt[:, :], src, ACT.Square).then_inc(sq_ready, 1)

        zeroed = [0]

        def pool_zero(pool):
            pool.memset(sums[:, :], 0.0).then_inc(sums_zero, 1)
            pool.memset(sumq[:, :], 0.0).then_inc(sums_zero, 1)
            zeroed[0] += 2
            pool.wait_ge(sums_zero, zeroed[0])

        SQUARES = (sqt, sums)

        def pool_sum(pool, j, xo, s, sq, square=sqt):
            if s is not None:
                pool.wait_ge(x_out, j + xo + 1)
                pool.tensor_tensor(sums[:, :], sums[:, :], xres[:, ds(j * SEQ, SEQ)], ALU.add).then_inc(s_added, 1)
                pool.wait_ge(s_added, j + s + 1)
            pool.wait_ge(sq_ready, j + sq + 1)
            pool.tensor_tensor(sumq[:, :], sumq[:, :], square[:, :], ALU.add).then_inc(q_added, 1)
            pool.wait_ge(q_added, j + sq + 2)

        def pe_stats(pe, name):
            c = NORMS[name]
            pe.wait_ge(q_added, c["sq"] + KC + 1)
            if "ce" in c:
                for b in range(TB):
                    pe.matmul(AUX[0][:, TB + b:TB + b + 1], sums[:, b * P:(b + 1) * P], ones[:, 0:1],
                              start=True, stop=True)
            for b in range(TB):
                last = pe.matmul(AUX[0][:, b:b + 1], sumq[:, b * P:(b + 1) * P], ones[:, 0:1], start=True, stop=True)
            last.then_inc(stat_full, 1)
            if "ce" in c:
                for t in range(0, SEQ, 512):
                    last = pe.matmul(YP[:, t:t + 512], ones[:, :], sums[:, t:t + 512], start=True, stop=True)
                last.then_inc(mean_full, 1)
            pe.wait_ge(spread_ready, c["st"] + 1)
            for t in range(0, SEQ, 512):
                last = pe.matmul(AUXW[:, t:t + 512], ones[:, :], rdiag8[:, t:t + 512], start=True, stop=True)
            last.then_inc(rstd_full, 1)

        def act_stats(act, name):
            c = NORMS[name]
            act.wait_ge(stat_dve, c["sd"] + 1)
            act.activation(tstat[:, 3 * TB:4 * TB], tstat[:, 2 * TB:3 * TB], ACT.Sqrt, scale=1.0 / (D * D)
                           ).then_inc(stat_act, 1)
            if "ce" in c:
                act.wait_ge(mean_full, c["st"] + 1)
                act.copy(mean[:, :], YP).then_inc(stat_act, 1)

        def dve_stats(dve, name):
            c = NORMS[name]
            dve.wait_ge(stat_full, c["st"] + 1)
            tv = tstat[:, 2 * TB:3 * TB]
            if "ce" in c:
                dve.tensor_copy(tstat[:, 0:TB], AUX[0][:, TB:2 * TB]).then_inc(tok_stat, 1)
                dve.wait_ge(tok_stat, 2 * c["st"] + 1)
                dve.tensor_tensor(tstat[:, TB:2 * TB], tstat[:, 0:TB], tstat[:, 0:TB], ALU.mult).then_inc(tok_stat, 1)
                dve.wait_ge(tok_stat, 2 * c["st"] + 2)
                dve.scalar_tensor_tensor(out=tv, in0=AUX[0][:, 0:TB], scalar=LN_EPS, in1=tstat[:, TB:2 * TB],
                                         op0=ALU.add, op1=ALU.subtract).then_inc(stat_dve, 1)
            else:
                dve.tensor_scalar(tv, AUX[0][:, 0:TB], RMS_EPS, None, ALU.add).then_inc(stat_dve, 1)
            dve.wait_ge(stat_act, c["sa"] + 1)
            dve.reciprocal(tstat[:, 4 * TB:5 * TB], tstat[:, 3 * TB:4 * TB]).then_inc(stat_dve, 1)
            dve.wait_ge(stat_dve, c["sd"] + 2)
            dve.tensor_tensor(rdiag8[:, :].rearrange("p (b t) -> p b t", t=P),
                              ident[:, :].unsqueeze(1).broadcast_to([P, TB, P]),
                              tstat[:, 4 * TB:5 * TB].unsqueeze(2).broadcast_to([P, TB, P]), ALU.mult
                              ).then_inc(spread_ready, 1)
            dve.wait_ge(rstd_full, c["st"] + 1)

        def pool_centre(pool, name):
            c = NORMS[name]
            pool.wait_ge(stat_act, c["sa"] + 2)
            with pool.Fori(0, KC // 2) as i:
                for u in range(2):
                    pool_centre_one(pool, name, i * 2 + u, u)

        def pool_centre_one(pool, name, k, u):
            pool.wait_ge(n_aff, k + NORMS[name]["af"] + 1)
            pool.tensor_tensor(cent[:, u * SEQ:(u + 1) * SEQ], xres[:, ds(k * SEQ, SEQ)], mean[:, :],
                               ALU.subtract).then_inc(n_cent, 1)

        def dve_scale(dve, name, k, u):
            c = NORMS[name]
            cu = cent[:, u * SEQ:(u + 1) * SEQ]
            if "ce" in c:
                dve.wait_ge(n_cent, k + c["ce"] + 1)
                src = cu
            else:
                dve.wait_ge(n_aff, k + c["af"] + 1)
                src = xres[:, ds(k * SEQ, SEQ)]
            dve.tensor_tensor(cu, src, AUXW, ALU.mult).then_inc(n_mul, 1)

        def act_layer_norm(act, name, k, u):
            c = NORMS[name]
            act.wait_ge(n_mul, k + c["mu"] + 1)
            act.activation(xres[:, ds(k * SEQ, SEQ)], cent[:, u * SEQ:(u + 1) * SEQ], ACT.Identity,
                           scale=vcol(2, k + LNV[name]), bias=vcol(2, k + LNV[name] + KC)).then_inc(n_aff, 1)
            act.wait_ge(n_aff, k + c["af"] + 3)

        GLA_COLS = [(0, P), (GH * GDK, P), (2048, GDV), (2048 + P, GDV), (1024, GDV), (1024 + P, GDV)]
        STEPS = NCH

        def chunk_of(d, j):
            return j if d == 0 else (NCH_CTX - 1 - j if j < NCH_CTX else NCH + NCH_CTX - 1 - j)

        def first_visit(d, b):
            return (b < TB // 2) == (d == 0)

        GROUPS = [range(0, 4), range(4, 8), range(8, 10)]

        def act_rms(act, name, dst, w, off, gain, shift, done, base):
            c = NORMS[name]
            for k in range(KC):
                u = k % 2
                act.wait_ge(n_mul, c["mu"] + k + 1)
                act.wait_ge(done, base + k - 1 + 2)
                act.activation(aff[:, u * SEQ:(u + 1) * SEQ], cent[:, u * SEQ:(u + 1) * SEQ], ACT.Identity,
                               scale=gain(k), bias=shift(k)).then_inc(n_aff, 1)
                act.wait_ge(n_aff, c["af"] + k + 3)
                act.copy(dst[:, k * w + off:k * w + off + SEQ], aff[:, u * SEQ:(u + 1) * SEQ]).then_inc(
                    {"rms1": ga_hi, "rms2": a_hi}[name], 1)

        def dve_rms(dve, name, dhi, dlo, w, off, hi_sem, hi_base, lo_sem):
            for k in range(KC + 1):
                if k < KC:
                    dve_scale(dve, name, k, k % 2)
                if k >= 1:
                    q = k - 1
                    dve.wait_ge(hi_sem, hi_base + q + 1)
                    dve.tensor_tensor(dlo[:, q * w + off:q * w + off + SEQ], aff[:, (q % 2) * SEQ:(q % 2 + 1) * SEQ],
                                      dhi[:, q * w + off:q * w + off + SEQ].bitcast(F32), ALU.subtract
                                      ).then_inc(lo_sem, 1)

        def gla_product(n, u, lat_only):
            pe = nc.tensor
            pe.wait_ge(w_hi, n + 3)
            pe.wait_ge(w_lo, n + 3)
            pe.wait_ge(act_read, n + 1)
            pe.wait_ge(dve_read, n + 1)
            t0, width = (CTX, SEQ) if lat_only else (0, TOK)
            for k in range(KC):
                wh, wl = whi[:, u, k * P:(k + 1) * P], wlo[:, u, k * P:(k + 1) * P]
                for w, a in ((wh, gahi), (wh, galo), (wl, gahi)):
                    for t in range(0, width, 512):
                        e = min(512, width - t)
                        c = k * TOK + t0 + t
                        last = pe.matmul(GS[u][:, t:t + e], w, a[:, c:c + e],
                                         start=(k == 0 and w is wh and a is gahi), stop=(k == KC - 1 and w is wl))
            last.then_inc(gemm_done, 1)

        def pe_turn(pe, i, g0, src, ready):
            pe.wait_ge(*ready)
            for q, blks in enumerate(GROUPS):
                g = g0 + q
                if g < 2:
                    pe.wait_ge(o_dve, i * 8 + 2)
                    pe.wait_ge(o_act, i * 8 + 2)
                elif g - 2 < 6:
                    pe.wait_ge(tr_act, i * 6 + g - 1)
                else:
                    pe.wait_ge(tr_dve, i * 6 + g - 7)
                for y, b in enumerate(blks):
                    last = pe.transpose(BANK[6 + g % 2][:, y * P:(y + 1) * P], src[:, b * P:(b + 1) * P], ident[:, :])
                last.then_inc(tr_full, 1)

        def o_bank(d, v):
            return BANK[(6, 0)[v % 2] + d]

        def visits():
            return [(j, d, (chunk_of(d, j) - NCH_CTX) // 2, (j - NCH_CTX) // 2)
                    for j in range(NCH_CTX + 1, STEPS, 2) for d in range(2)]

        def evac_count(d, v):
            seen = {True: 0, False: 0}
            for _, dd, b, vv in visits():
                fv = first_visit(dd, b)
                seen[fv] += 1
                if (dd, vv) == (d, v):
                    return fv, seen[fv]

        def pe_gla_core(pe, i):
            pe.wait_ge(tr_act, i * 6 + 6)
            pe.wait_ge(tr_dve, i * 6 + 6)
            pe.wait_ge(gmul, i * 6 + 6)
            pe.wait_ge(act_read, i * 6 + C_GLA + 8)
            for h in range(2):
                if h == 1:
                    pe.wait_ge(att_set, i * 4 + 2)
                for d in range(2):
                    for y in range(4):
                        b = h * 4 + y
                        last = pe.matmul(BANK[d][:, y * P:(y + 1) * P], kn[:, d * SEQ + b * P:d * SEQ + (b + 1) * P],
                                         qd[:, d * SEQ + b * P:d * SEQ + (b + 1) * P], start=True, stop=True)
                last.then_inc(att_full, 1)
            for j in range(STEPS):
                for d in range(2):
                    c = chunk_of(d, j)
                    b, r = c // 2, (c % 2) * 64
                    if j < STEPS - 1:
                        if j >= 2:
                            pe.wait_ge(s_new, i * 38 + 2 * (j - 2) + d + 1)
                        pe.matmul(BANK[2 + 2 * d + j % 2][:, 0:GDV], kdt[r:r + 64, d * TOK + b * P:d * TOK + (b + 1) * P],
                                  g_v[r:r + 64, b * GDV:(b + 1) * GDV], start=True, stop=True).then_inc(u_full, 1)
                    if j >= NCH_CTX:
                        v = (j - NCH_CTX) // 2
                        lb = b - LPAIR0
                        bank = o_bank(d, v)[:, 0:GDV]
                        if (j - NCH_CTX) % 2 == 0:
                            if v >= 2:
                                fv, cnt = evac_count(d, v - 2)
                                pe.wait_ge(o_act if fv else o_dve, i * 8 + cnt + 2)
                            if v == 1:
                                pe.wait_ge(att_set, i * 4 + 4)
                            if d == 0:
                                if v == 0:
                                    pe.wait_ge(att_sum, i + 1)
                                pe.matmul(bank, att_f[:, lb * P:(lb + 1) * P], g_v[:, b * GDV:(b + 1) * GDV],
                                          start=True, stop=False, skip_group_check=True)
                        pe.wait_ge(s_new, i * 38 + 2 * (j - 1) + d + 1)
                        qo = d * SEQ + (c - NCH_CTX) * GCH
                        last = pe.matmul(bank[r:r + 64, :], qd[:, qo:qo + GCH],
                                         state[:, (d * 2 + j % 2) * GDV:(d * 2 + j % 2 + 1) * GDV],
                                         start=(d == 1), stop=True, skip_group_check=True)
                        if (j - NCH_CTX) % 2 == 1:
                            last.then_inc(o_full, 1)
            pe.wait_ge(o_norm, i + 1)
            for f in range(2):
                for b in range(TB):
                    last = pe.transpose(psum[:, f * SEQ + b * P:f * SEQ + (b + 1) * P],
                                        o_tok[:, b * GDV + f * P:b * GDV + (f + 1) * P], ident[:, :])
                last.then_inc(oT_full, 1)

        def dve_second(dve, i, v_no, d, b, v):
            dve.wait_ge(o_full, i * 16 + v_no + 1)
            fv, cnt = evac_count(1 - d, [w for _, dd, bb, w in visits() if dd == 1 - d and bb == b][0])
            dve.wait_ge(o_act, i * 8 + cnt + 2)
            ob = o_tok[:, b * GDV:(b + 1) * GDV]
            dve.tensor_tensor(ob, ob, o_bank(d, v)[:, 0:GDV], ALU.add).then_inc(o_dve, 1)

        DECAYS = [(0, 1, False, 3), (0, -1, False, 3), (0, 1, True, 7),
                  (1, 1, True, 6), (1, 1, False, 8), (1, -1, False, 8)]
        SECOND = [b for _, d, b, _ in visits() if not first_visit(d, b)]

        def peeled(eng, last, body):
            with eng.Fori(0, KC // 2 - (1 if last else 0)) as i:
                for u in range(2):
                    body(i, u)
            if last:
                for u in range(2):
                    body(KC // 2 - 1, u)

        block = ctx.enter_context(nc.Block())

        @block.sync
        def _(sp):
            xv = x[0].rearrange("(b p) d -> b p d", p=P)
            for b in range(TB):
                sp.dma_start(xin[:, b * D:(b + 1) * D], xv[b]).then_inc(x_loaded, 16)
            ada_v = ada_w[0].rearrange("(k p) n -> p k n", p=P)
            with sp.Fori(0, PAIRS) as i:
                def ada(c):
                    s = c % 4
                    sp.wait_ge(ada_used, i * ADA_STEP + c + 1)
                    sp.dma_start(adaring[:, s * D:(s + 1) * D].rearrange("p (k n) -> p k n", n=P),
                                 ada_v[:, :, ds(i * ADA_STEP * P + c * P, P)]).then_inc(ada_loaded[s], 16)

                for half in range(2):
                    for j in range(3):
                        c = half * 3 + j
                        load_chunk(i * 6 + C_ATT + c, c % 2, w_cols["in"][:, :, ds(i * P + ATT_COLS[c], P)])
                        if j != 1:
                            for q in range(3):
                                ada(half * 6 + 3 * (j // 2) + q)
            with sp.Fori(0, KC // 2) as i:
                for u in range(2):
                    load_chunk(i * 2 + C_WOUT + u, u, w_cols["out"][:, :, ds(i * 2 * P + u * P, P)])
            n = C_FFN
            for g0, gc in FFN_GROUPS:
                with sp.Fori(0, gc) as i:
                    load_chunk(i * 2 + n, 0, w_cols["up"][:, :, ds(i * P + g0 * P, P)])
                    load_chunk(i * 2 + n + 1, 1, w_cols["up"][:, :, ds(i * P + (g0 + FCH) * P, P)])
                n += 2 * gc
                with sp.Fori(0, KC // 2) as i:
                    for u in range(2):
                        load_chunk(i * 2 + n + u, u, w_cols["down"][:, g0:g0 + gc, ds(i * 2 * P + u * P, P)])
                n += KC
            with sp.Fori(0, GH) as i:
                for j, (c0, step) in enumerate(GLA_COLS):
                    load_chunk(i * 6 + C_GLA + j, j % 2, w_cols["gla"][:, :, ds(i * step + c0, P)])
            with sp.Fori(0, KC // 2) as i:
                for u in range(2):
                    load_chunk(i * 2 + C_WO + u, u, w_cols["o"][:, :, ds(i * 2 * P + u * P, P)])
            n = C_MLP
            for g in range(MLP_GROUPS):
                with sp.Fori(0, KC // 2) as i:
                    for u in range(2):
                        load_chunk(i * 2 + n + u, u, w_cols["m1"][:, :, ds(i * 2 * P + (g * KC + u) * P, P)])
                n += KC
                with sp.Fori(0, KC // 2) as i:
                    for u in range(2):
                        load_chunk(i * 2 + n + u, u, w_cols["m2"][:, g * KC:(g + 1) * KC, ds(i * 2 * P + u * P, P)])
                n += KC

        @block.gpsimd
        def _(pool):
            pool.memset(ident[:, :], 0.0).then_inc(vec_zero, 1)
            pool.memset(flip[:, :], 0.0).then_inc(vec_zero, 1)
            pool.memset(maskb[:, :], 0.0).then_inc(vec_zero, 1)
            pool.memset(vrow[:, :], 0.0).then_inc(vec_zero, 1)
            pool.memset(ones[:, :], 1.0 / D).then_inc(consts_ready, 1)
            pool.wait_ge(vec_zero, 4)
            pool.affine_select(out=ident[:, :], in_=ident[:, :], compare_op=ALU.not_equal, fill=1.0, base=0,
                               pattern=[[-1, P]], channel_multiplier=1).then_inc(consts_ready, 1)
            pool.affine_select(out=flip[:, :], in_=flip[:, :], compare_op=ALU.not_equal, fill=1.0, base=1 - P,
                               pattern=[[1, P]], channel_multiplier=1).then_inc(consts_ready, 1)
            pool.affine_select(out=maskb[:, :], in_=maskb[:, :], compare_op=ALU.is_ge, fill=NEG, base=0,
                               pattern=[[-1, P]], channel_multiplier=1).then_inc(consts_ready, 1)
            pool.wait_ge(consts_ready, 4)
            pool.tensor_copy(identb[:, :], ident[:, :]).then_inc(consts_ready, 1)
            rows = [
                [conv_w[0, 0:2].rearrange("j (n p) -> (j n) p", p=P)],
                [conv_w[0, 2:3].rearrange("j (n p) -> (j n) p", p=P), conv_b.rearrange("j (n p) -> (j n) p", p=P)],
                [v.rearrange("j (n p) -> (j n) p", p=P) for v in (ln1_g, ln1_b, ln2_g, ln2_b, norm1_g, norm2_g)]
                + [final_g.rearrange("(n p) -> n p", p=P), gla_g_head[0].rearrange("h (n p) -> (h n) p", p=P),
                   c_2.rearrange("j (n p) -> (j n) p", p=P), c_ctx_2.rearrange("(n p) -> n p", p=P)],
                [ada_b.rearrange("j (n p) -> (j n) p", p=P), gla_b_a[0].rearrange("d (n p) -> (d n) p", p=P)],
            ]
            for t, vs in enumerate(rows):
                r = 0
                for v in vs:
                    pool.dma_start(vrow[r:r + v.shape[0], t * P:(t + 1) * P], v).then_inc(vec_loaded, 16)
                    r += v.shape[0]
            pool.dma_start(wf[:, :].rearrange("p (k n) -> p k n", n=NHEAD),
                           w_cols["in"][:, :, 3 * D_A:3 * D_A + NHEAD]).then_inc(small_loaded, 16)
            pool.dma_start(small[0:NHEAD, 0:1], b_forget.rearrange("j h -> h j")).then_inc(small_loaded, 16)
            pool.wait_ge(xT_full, KC)
            pool.dma_start(relx[:, 0:NREL], rel_bias[0]).then_inc(small_loaded, 16)
            pool.wait_ge(xT_copied, KC)
            pool.dma_start(xT_d, xres[:, :]).then_inc(xT_spilled, 16)
            pool.wait_ge(rel_ready, 3)
            pool.dma_start(rel_d, relx[:, :]).then_inc(rel_stored, 16)
            pool.wait_ge(cum_ready, 10)
            pool.dma_start(cumL_d, cumLs[:, :]).then_inc(cum_stored, 16)
            pool.dma_start(cumR_d, cumRs[:, :]).then_inc(cum_stored, 16)
            pool.wait_ge(rel_stored, 16)
            for h in range(NHEAD):
                for jj in range(2):
                    src = bass.AP(tensor=rel_d.tensor, offset=h * 512 + 129 - 128 * jj, ap=[[1, P], [1, P]])
                    pool.dma_start(hank[:, h * 256 + jj * P:h * 256 + (jj + 1) * P], src).then_inc(hank_loaded, 16)
            pool.wait_ge(cum_stored, 32)
            def load_gate(i, pair):
                for e in range(2):
                    for dst, src in ((cumL, cumL_d), (cumR, cumR_d)):
                        pool.dma_start(dst[:, e * SEQ:(e + 1) * SEQ],
                                       src[ds(i * 2 + 2 * pair + e, 1), :].rearrange("h (r t) -> (h r) t", r=6)
                                       ).then_inc(cum_loaded, 16)

            def store_result(i, half, t):
                pool.wait_ge(y_out, i * 4 + half * 2 + t + 2)
                pool.dma_start(y_d[:, ds(i * SEQ + half * PAIRS * SEQ + t * 512, 512)],
                               ystage[:, t * 512:(t + 1) * 512]).then_inc(y_stored, 16)
                pool.wait_ge(y_stored, i * 64 + half * 32 + t * 16 + 16)
                pool.sem_inc(y_left, 1)

            pool.sem_inc(y_left, 2)
            load_gate(0, 0)

            def pool_attention(i, half):
                for m in range(NS):
                    lo_side(pool, i, half + 1, m)
                    if m == 5:
                        store_result(i, half, 0)
                        if half == 1:
                            pool.wait_ge(exp_done, i * 32 + 18)
                            load_gate(i, 1)
                store_result(i, half, 1)

            with pool.Fori(0, PAIRS - 1) as i:
                for half in range(2):
                    pool_attention(i, half)
            pool_attention(PAIRS - 1, 0)
            pool.wait_ge(cum_loaded, 16 * 4 * PAIRS)
            pool.wait_ge(pv_done, (PAIRS - 1) * 32 + 18)
            pool.dma_start(xres[:, 0:(KC - 1) * SEQ], y_d[:, 0:(KC - 1) * SEQ]).then_inc(y_loaded, 16)
            pool.wait_ge(y_out, 4 * PAIRS + 1)
            pool_zero(pool)
            pool.sem_inc(q_added, 1)
            pool.wait_ge(xT_spilled, 16)
            with pool.Fori(0, KC) as j:
                pool.dma_start(xs[:, :], xT_d[:, ds(j * SEQ, SEQ)]).then_inc(xs_loaded, 16)
                pool_sum(pool, j, 0, 0, 0)
            pool_centre(pool, "ln1")
            pool.wait_ge(h_lo, FCH)
            pool_zero(pool)
            with pool.Fori(0, KC) as j:
                pool_sum(pool, j, 24, 8, 8)
            pool.wait_ge(stat_full, 2)
            pool.memset(sumq[:, :], 0.0).then_inc(sums_zero, 1)
            zeroed[0] += 1
            pool.wait_ge(sums_zero, zeroed[0])
            pool.dma_start(cin[:, :].rearrange("p (b d) -> p b d", d=D), ctx_2[0].rearrange("(b p) d -> p b d", p=P)
                           ).then_inc(ctx_loaded, 16)
            for k in range(KC):
                pool_sum(pool, k, 0, None, 16, SQUARES[k % 2])
            pool.wait_ge(ctx_T, 1)
            pool.memset(wa1raw[:, :], 0.0).then_inc(wa1_zero, 1)
            pool.wait_ge(wa1_zero, 1)
            for d in range(2):
                pool.dma_start(wa1raw[:, :].rearrange("p (k n) -> p k n", n=P)[:, :, 32 * d:32 * d + RANK],
                               gla_w_a1[0, d].rearrange("(k p) n -> p k n", p=P)).then_inc(wa1_loaded, 16)
            pool.dma_start(x2_d, xres[:, :]).then_inc(x2_spilled, 16)
            pool.wait_ge(q_added, 25)
            pool.wait_ge(ga_lo, 2 * KC + 2)
            pool.wait_ge(x2_spilled, 16)
            def load_wa2(i, more):
                for d in range(2):
                    pool.dma_start(wa2[32 * d:32 * d + RANK, :], gla_w_a2[0, d][:, ds(i * P + more * P, P)]
                                   ).then_inc(wa2_loaded, 16)

            load_wa2(0, 0)
            ms = 0

            def step(ins):
                ins.then_inc(mask_step, 1)
                pool.wait_ge(mask_step, ms + 1)
                return ms + 1

            m3 = mtmp[:, 0:512].rearrange("p (b t) -> p b t", t=P)
            for mask, sign, rows, cols in ((mask_f, 1, slice(0, 64), slice(64, 128)),
                                           (mask_b, -1, slice(64, 128), slice(0, 64))):
                ms = step(pool.memset(mtmp[:, 0:512], 1.0))
                ms = step(pool.affine_select(out=m3, in_=m3, compare_op=ALU.is_ge, fill=0.0, base=0,
                                             pattern=[[0, 4], [sign, P]], channel_multiplier=-sign))
                ms = step(pool.memset(m3[rows, :, cols], 0.0))
                ms = step(pool.tensor_copy(mask[:, :], mtmp[:, 0:512]))
            ms = step(pool.memset(mtmp[:, :], 1.0))
            ms = step(pool.memset(mtmp[:, :].rearrange("p (c t) -> p c t", t=GCH)[:, :, 0:1], 0.0))
            ms = step(pool.tensor_copy(restart[:, :], mtmp[:, :]))
            pool.sem_inc(masks_ready, 1)
            pool.wait_ge(x2_spilled, 16)
            pool.wait_ge(low_out, 1)
            pool.sem_inc(o_left, 1)

            def spill_head(i):
                pool.wait_ge(o_gated, i * 2 + 4)
                pool.dma_start(oT_d[:, ds(i * 2 * SEQ, 2 * SEQ)], rT[:, :]).then_inc(o_spilled, 16)
                pool.wait_ge(o_spilled, i * 16 + 16)
                pool.sem_inc(o_left, 1)

            with pool.Fori(0, GH - 1) as i:
                pool.wait_ge(tr_full, i * 12 + 13)
                load_wa2(i, 1)
                spill_head(i)
            pool.wait_ge(tr_full, GH * 12 + 1)
            pool.wait_ge(gmul, GH * 6)
            pool.dma_start(xres[:, 0:4 * SEQ], oT_d[:, 0:4 * SEQ]).then_inc(oT_loaded, 16)
            spill_head(GH - 1)
            pool.wait_ge(oT_loaded, 16)
            pool.dma_start(xres[:, 4 * SEQ:8 * SEQ], oT_d[:, 4 * SEQ:8 * SEQ]).then_inc(oT_loaded, 16)
            pool_zero(pool)
            with pool.Fori(0, KC) as j:
                pool.dma_start(xs[:, :], x2_d[:, ds(j * SEQ, SEQ)]).then_inc(xs_loaded, 16)
                pool.wait_ge(x_out, j + 33)
                pool_sum(pool, j, 0, None, 24)
            pool.wait_ge(m_lo, 4 * KC + 1)
            pool_zero(pool)
            with pool.Fori(0, KC) as j:
                pool_sum(pool, j, 0, None, 32)
            ov = out[0].rearrange("(b t) f -> t b f", t=P)
            with pool.Fori(0, KC // 2) as i:
                for u in range(2):
                    pool.wait_ge(out_copied, i * 2 + u + 1)
                    pool.dma_start(ov[:, :, ds(i * 2 * P + u * P, P)],
                                   ostage[:, u * SEQ:(u + 1) * SEQ].rearrange("p (b f) -> p b f", f=P)
                                   ).then_inc(out_stored[u], 16)
            for u in range(2):
                pool.wait_ge(out_stored[u], 16 * KC // 2)

        @block.tensor
        def _(pe):
            pe.sem_inc(ada_used, 4)
            pe.sem_inc(pv_done, 2)
            pe.sem_inc(pt_full, 2)
            pe.wait_ge(consts_ready, 5)
            pe.wait_ge(vec_loaded, 16 * 15)
            for t in range(4):
                last = pe.transpose(AUX[0][:, t * P:(t + 1) * P], vrow[:, t * P:(t + 1) * P], ident[:, :])
            last.then_inc(vec_T, 1)
            for k in range(KC):
                if k >= 2:
                    pe.wait_ge(xT_copied, k - 1)
                for b in range(TB):
                    if k == 0:
                        pe.wait_ge(x_loaded, 16 * TB)
                    last = pe.transpose(G[k % 2][:, b * P:(b + 1) * P], xin[:, b * D + k * P:b * D + (k + 1) * P],
                                        ident[:, :])
                last.then_inc(xT_full, 1)
            pe.wait_ge(small_loaded, 16 * 3)
            pe.wait_ge(xT_copied, KC)
            for t in range(2):
                for k in range(KC):
                    last = pe.matmul(YP[0:NHEAD, t * 512:(t + 1) * 512], wf[:, k * NHEAD:(k + 1) * NHEAD],
                                     xres[:, k * SEQ + t * 512:k * SEQ + (t + 1) * 512],
                                     start=(k == 0), stop=(k == KC - 1))
            last.then_inc(f_full, 1)
            pe.wait_ge(c_silu, 2)
            pe.wait_ge(vec_cols, 1)
            pe.wait_ge(f_act, 1)
            pe.wait_ge(f_dve, 1)
            for m, (_, _, units) in enumerate(SIDE):
                for part in range(len(units)):
                    if SIDE[m][0] == "turn" and part == 0:
                        pe.wait_ge(side_act, NA)
                    pe_side(pe, 0, 0, m, part, SETUP_BANKS[m % 2])
            pe.wait_ge(hank_loaded, 16 * 16)
            pe.wait_ge(xT_copied, KC)
            for h in range(NHEAD):
                slot = G[h // 4][:, (h % 4) * 256:(h % 4 + 1) * 256]
                for jj in range(2):
                    last = pe.matmul(slot[:, jj * P:(jj + 1) * P],
                                     hank[:, h * 256 + jj * P:h * 256 + (jj + 1) * P], flip[:, :], start=True, stop=True)
            last.then_inc(rel_full, 1)
            pe.wait_ge(rel_done, 3)
            pe.wait_ge(side_dve, ND)
            pe_qk(pe, 0, 0, 0)
            with pe.Fori(0, PAIRS - 1) as i:
                for half in range(2):
                    pe_attention(pe, half, i, False)
            pe_attention(pe, 0, PAIRS - 1, False)
            pe_attention(pe, 1, PAIRS - 1, True)
            pe.wait_ge(exp_done, PAIRS * 32 + 2)
            with pe.Fori(0, KC // 2) as i:
                for u in range(2):
                    product(i * 2 + C_WOUT + u, u, KC, ahi, alo, SEQ, (a_hi, a_lo, 8))
            pe_stats(pe, "ln1")
            n = C_FFN
            for g0, gc in FFN_GROUPS:
                with pe.Fori(0, gc) as i:
                    for u in range(2):
                        product(i * 2 + n + u, u, KC, ahi, alo, SEQ, (a_hi, a_lo, 16))
                n += 2 * gc
                with pe.Fori(0, KC // 2) as i:
                    for u in range(2):
                        product(i * 2 + n + u, u, gc, hhi, hlo, SEQ, (h_hi, h_lo, g0, 1))
                n += KC
            pe_stats(pe, "ln2")
            pe.wait_ge(ctx_loaded, 16)
            for k in range(KC):
                for b in range(2):
                    last = pe.transpose(G[k // 4][:, (k % 4) * CTX + b * P:(k % 4) * CTX + (b + 1) * P],
                                        cin[:, b * D + k * P:b * D + (k + 1) * P], ident[:, :])
            last.then_inc(ctx_T, 1)
            pe.wait_ge(ctx_sq, 2)
            for k in range(KC):
                last = pe.matmul(BANK[6][:, 0:CTX], ones[:, :], csq[:, k * CTX:(k + 1) * CTX],
                                 start=(k == 0), stop=(k == KC - 1))
            last.then_inc(ctx_full, 1)
            pe_stats(pe, "rms1")
            pe.wait_ge(wa1_hi, 1)
            pe.wait_ge(wa1_lo, 1)
            for k in range(KC):
                pe.wait_ge(ga_lo, KC + k + 1 + 2)
                wh, wl = wa1hi[:, k * P:(k + 1) * P], wa1lo[:, k * P:(k + 1) * P]
                for w, a in ((wh, gahi), (wh, galo), (wl, gahi)):
                    for t in range(0, TOK, 512):
                        e = min(512, TOK - t)
                        last = pe.matmul(GS[0][:, t:t + e], w, a[:, k * TOK + t:k * TOK + t + e],
                                         start=(k == 0 and w is wh and a is gahi), stop=(k == KC - 1 and w is wl))
            last.then_inc(low_full, 1)
            pe.sem_inc(tr_full, 1)
            with pe.Fori(0, GH) as i:
                pe.wait_ge(wa2_loaded, i * 32 + 32)
                pe.wait_ge(low_out, 1)
                pe.wait_ge(o_gated, i * 2 + 2)
                for d in range(2):
                    for t in range(0, TOK, 512):
                        e = min(512, TOK - t)
                        last = pe.matmul(GS[d][:, t:t + e], wa2[32 * d:32 * d + RANK, :],
                                         gT[32 * d:32 * d + RANK, t:t + e], start=True, stop=True)
                    last.then_inc(z_full, 1)
                for j in range(6):
                    n = i * 6 + C_GLA + j
                    if j < 2:
                        pe.wait_ge(z_dve, i * 8 + j * 3 + 1)
                    lat_only = j in (0, 2, 3)
                    gla_product(n, j % 2, lat_only)
                    if j == 3:
                        for d in range(2):
                            pe_turn(pe, i, d * 3, kd[:, d * TOK:(d + 1) * TOK], (gmul, i * 6 + (3, 4)[d]))
                pe_turn(pe, i, 6, vst[:, :], (g_out, i * 6 + 5))
                pe_turn(pe, i, 9, vst[:, :], (g_out, i * 6 + 6))
                pe_gla_core(pe, i)
            pe.wait_ge(o_gated, GH * 2 + 2)
            with pe.Fori(0, KC // 2) as i:
                for u in range(2):
                    product(i * 2 + C_WO + u, u, KC, ahi, alo, SEQ, (a_hi, a_lo, 24))
            pe_stats(pe, "rms2")
            n = C_MLP
            for g in range(MLP_GROUPS):
                with pe.Fori(0, KC // 2) as i:
                    for u in range(2):
                        product(i * 2 + n + u, u, KC, ahi, alo, SEQ, (a_hi, a_lo, 32, 0, 2))
                n += KC
                with pe.Fori(0, KC // 2) as i:
                    for u in range(2):
                        product(i * 2 + n + u, u, KC, hhi, hlo, SEQ, (m_hi, m_lo, g * KC, 0, 1))
                n += KC
            pe_stats(pe, "rmsf")
            pe.wait_ge(act_read, C_END + 2)
            pe.wait_ge(dve_read, C_END + 2)
            for k in range(KC):
                pe.wait_ge(n_aff, NORMS["rmsf"]["af"] + k + 3)
                if k >= 2:
                    pe.wait_ge(out_copied, k - 1)
                for b in range(TB):
                    last = pe.transpose(G[k % 2][:, b * P:(b + 1) * P],
                                        aff[:, (k % 2) * SEQ + b * P:(k % 2) * SEQ + (b + 1) * P], ident[:, :])
                last.then_inc(out_T, 1)

        @block.scalar
        def _(act):
            act.sem_inc(w_hi, 2)
            act.sem_inc(gemm_done, 2)
            act.sem_inc(act_read, 2)
            act.sem_inc(exp_done, 2)
            act.sem_inc(y_out, 1)
            act.sem_inc(pt_act, 1)
            act.wait_ge(vec_T, 1)
            act.copy(vecs[:, :].rearrange("p (t n) -> p t n", n=96),
                     AUX[0].rearrange("p (t n) -> p t n", n=P)[:, :, 0:96]).then_inc(vec_cols, 1)
            for k in range(KC):
                act.wait_ge(xT_full, k + 1)
                act.copy(ahi[:, k * SEQ:(k + 1) * SEQ], G[k % 2]).then_inc(a_hi, 1)
                act.copy(xres[:, k * SEQ:(k + 1) * SEQ], G[k % 2]).then_inc(xT_copied, 1)
            act.wait_ge(vec_cols, 1)
            cs = csil[:, :].rearrange("p (k two) -> p two k", two=2)
            act.activation(cs[:, 0, :], vecs[:, 2 * 96 + 64:2 * 96 + 72], ACT.Silu).then_inc(c_silu, 1)
            act.activation(cs[:, 1, :], vecs[:, 2 * 96 + 72:2 * 96 + 80], ACT.Silu).then_inc(c_silu, 1)
            split_hi(0, (0, 16))
            act.wait_ge(f_full, 1)
            L = lambda s: lf[:, s * SEQ:(s + 1) * SEQ]
            act.activation(L(0), YP[0:NHEAD, :], ACT.Abs, bias=small[0:NHEAD, 0:1]).then_inc(f_act, 1)
            act.wait_ge(f_act, 1)
            act.activation(L(1), L(0), ACT.Exp, scale=-1.0).then_inc(f_act, 1)
            act.wait_ge(f_act, 2)
            act.activation(L(0), L(1), ACT.Ln, bias=1.0).then_inc(f_act, 1)
            act.wait_ge(xT_spilled, 16)
            for m in range(NS):
                act_side(act, 0, 0, m, SETUP_BANKS[m % 2])
            act.wait_ge(rel_full, 1)
            act.wait_ge(cum_stored, 32)
            act.copy(relT[:, 0:1024], G[0]).then_inc(rel_done, 1)
            act.copy(relT[:, 1024:2048], G[1]).then_inc(rel_done, 1)
            act_exp(act, 0, 0, 0)
            with act.Fori(0, PAIRS - 1) as i:
                for half in range(2):
                    act_attention(act, half, i, False)
            act_attention(act, 0, PAIRS - 1, False)
            act_attention(act, 1, PAIRS - 1, True)
            act.sem_inc(act_read, C_WOUT)
            act.wait_ge(gemm_done, C_WOUT + 2)
            split_hi(C_WOUT + 1, (1, (C_WOUT // 2 + 1) * 16))
            for k in range(KC):
                if k == 0:
                    act.wait_ge(y_loaded, 16)
                if k == KC - 1:
                    act.wait_ge(y_out, 4 * PAIRS + 1)
                act.copy(ahi[:, k * SEQ:(k + 1) * SEQ], xres[:, k * SEQ:(k + 1) * SEQ]).then_inc(a_hi, 1)
            act.sem_inc(n_aff, 2)
            with act.Fori(0, KC // 2) as i:
                for u in range(2):
                    j = i * 2 + u
                    act.wait_ge(gemm_done, j + C_WOUT + 3)
                    act.sem_inc(act_read, 1)
                    split_hi_next(i, C_WOUT, u)
                    act.wait_ge(x_out, j + 1)
                    act_square(act, j, 0, xres[:, ds(j * SEQ, SEQ)])
            act_stats(act, "ln1")
            with act.Fori(0, KC // 2) as i:
                for u in range(2):
                    k = i * 2 + u
                    act_layer_norm(act, "ln1", k, u)
                    act.copy(ahi[:, ds(k * SEQ, SEQ)], xres[:, ds(k * SEQ, SEQ)]).then_inc(a_hi, 1)
            n = C_FFN
            act.sem_inc(h_mul, 1)
            act.sem_inc(h_hi, 1)
            for gi, (g0, gc) in enumerate(FFN_GROUPS):
                with act.Fori(0, gc) as i:
                    for u, cv in enumerate((conv_v, conv_g)):
                        act.wait_ge(gemm_done, i * 2 + n + u + 3)
                        act.wait_ge(h_mul, i + g0 + 1)
                        f = i + g0 + u * FCH
                        act.activation(cv[:, :], G[u], ACT.Identity, scale=vcol(1, f), bias=vcol(1, f + 44)
                                       ).then_inc(conv_act, 1)
                        act.wait_ge(conv_act, i * 2 + g0 * 2 + u + 1)
                        act.sem_inc(act_read, 1)
                        split_hi_next(i, n, u)
                    act.wait_ge(conv_dve, i * 4 + g0 * 4 + 4)
                    act.activation(gelu_g[:, :], conv_g[:, :], ACT.Gelu_apprx_tanh).then_inc(gelu_done, 1)
                    act.wait_ge(h_mul, i + g0 + 2)
                    act.copy(hhi[:, ds(i * SEQ, SEQ)], hidden[:, :]).then_inc(h_hi, 1)
                n += 2 * gc
                with act.Fori(0, KC // 2) as i:
                    for u in range(2):
                        j = i * 2 + u
                        act.wait_ge(gemm_done, j + n + 3)
                        act.sem_inc(act_read, 1)
                        split_hi_next(i, n, u)
                        if gi == len(FFN_GROUPS) - 1:
                            act.wait_ge(x_out, j + 25)
                            act_square(act, j, 8, xres[:, ds(j * SEQ, SEQ)])
                n += KC
            act_stats(act, "ln2")
            for k in range(KC):
                act_layer_norm(act, "ln2", k, k % 2)
                act.wait_ge(q_added, k + 16)
                act.activation(SQUARES[k % 2][:, :], xres[:, k * SEQ:(k + 1) * SEQ], ACT.Square).then_inc(sq_ready, 1)
            act.wait_ge(ctx_T, 1)
            for h in range(2):
                act.activation(csq[:, h * 1024:(h + 1) * 1024], G[h], ACT.Square).then_inc(ctx_sq, 1)
            for h in range(2):
                act.copy(cxT[:, h * 1024:(h + 1) * 1024], G[h]).then_inc(ctx_sq, 1)
            act.wait_ge(ctx_st, 1)
            act.activation(csd[:, :], cvar[:, :], ACT.Sqrt).then_inc(ctx_sd, 1)
            mod = lambda n, who: mods[:, 2 * n + who:2 * n + who + 1]
            act.wait_ge(gains_ready, 3)
            for k in range(KC):
                u = k % 2
                act.wait_ge(cc_mul, k + 1)
                if k >= 2:
                    act.wait_ge(ga_lo, k - 1 + 2)
                act.activation(caff[:, u * CTX:(u + 1) * CTX], ccent[:, u * CTX:(u + 1) * CTX], ACT.Identity,
                               scale=gains[:, 8 + k:9 + k], bias=mod(k, 1)).then_inc(cc_aff, 1)
                act.wait_ge(cc_aff, k + 1)
                act.copy(gahi[:, k * TOK:k * TOK + CTX], caff[:, u * CTX:(u + 1) * CTX]).then_inc(ga_hi, 1)
            act.wait_ge(wa1_loaded, 32)
            act.copy(wa1hi[:, :], wa1raw[:, :]).then_inc(wa1_hi, 1)
            act_stats(act, "rms1")
            act_rms(act, "rms1", gahi, TOK, CTX, lambda k: gains[:, k:k + 1], lambda k: mod(k, 0), ga_lo, KC)
            act.wait_ge(low_full, 1)
            act.wait_ge(x2_spilled, 16)
            act.copy(gT[0:64, :], GS[0][0:64, 0:TOK]).then_inc(low_out, 1)
            act.sem_inc(o_act, 2)
            with act.Fori(0, GH) as i:
                for d in range(2):
                    act.wait_ge(z_full, i * 2 + d + 1)
                    bias = vecs[:, ds(i + 3 * 96 + 48 + d * GH, 1)]
                    if d == 1:
                        act.wait_ge(z_dve, i * 8 + 2)
                    act.activation(gex[:, 0:TOK], GS[d][:, 0:TOK], ACT.Abs, bias=bias).then_inc(z_act, 1)
                    act.wait_ge(z_act, i * 6 + d * 3 + 1)
                    act.activation(gex[:, 0:TOK], gex[:, 0:TOK], ACT.Exp, scale=-1.0).then_inc(z_act, 1)
                    act.wait_ge(z_act, i * 6 + d * 3 + 2)
                    act.activation(gex[:, 0:TOK], gex[:, 0:TOK], ACT.Ln, bias=1.0).then_inc(z_act, 1)

                def decay(e):
                    d, sign, full, after = DECAYS[e]
                    n0, w = (0, TOK) if full else (CTX, SEQ)
                    act.wait_ge(z_dve, i * 8 + after)
                    if e >= 2:
                        act.wait_ge(gmul, i * 6 + e - 1)
                    act.activation(gex[:, (e % 2) * TOK + n0:(e % 2) * TOK + n0 + w],
                                   gcum[:, d * TOK + n0:d * TOK + n0 + w], ACT.Exp, scale=sign / TAU
                                   ).then_inc(gexp, 1)

                for j in range(6):
                    u = j % 2
                    n = i * 6 + C_GLA + j
                    act.wait_ge(gemm_done, n + 3)
                    if j == 0:
                        act.mul(qT[:, :], GS[u][:, 0:SEQ], GDK ** -0.5).then_inc(g_out, 1)
                    elif j == 1:
                        act.copy(kT[:, :], GS[u][:, 0:TOK]).then_inc(g_out, 1)
                    elif j in (2, 3):
                        act.wait_ge(o_left, i + 1)
                        act.activation(rT[:, (j - 2) * SEQ:(j - 1) * SEQ], GS[u][:, 0:SEQ], ACT.Silu).then_inc(g_out, 1)
                    else:
                        if j == 5:
                            act.wait_ge(tr_full, i * 12 + 10)
                        act.copy(vst[:, :], GS[u][:, 0:TOK]).then_inc(g_out, 1)
                    act.wait_ge(g_out, i * 6 + j + 1)
                    act.sem_inc(act_read, 1)
                    split_hi(n + 2, (u, i * 48 + (C_GLA // 2 + 2 + j // 2) * 16))
                    if j == 1:
                        act.wait_ge(tots, i * 2 + 2)
                        act.activation(etot[:, :], tot[:, :], ACT.Exp, scale=1.0 / TAU).then_inc(gexp, 1)
                        act.wait_ge(gcum_ex, i + 1)
                        for e in range(3):
                            decay(e)
                    if j == 2:
                        for e in range(3, 6):
                            decay(e)
                    if j == 3:
                        for d in range(2):
                            for q, blks in enumerate(GROUPS):
                                g = d * 3 + q
                                act.wait_ge(tr_full, i * 12 + g + 2)
                                b0, w = blks[0] * P, len(blks) * P
                                act.copy(kdt[:, d * TOK + b0:d * TOK + b0 + w], BANK[6 + g % 2][:, 0:w]
                                         ).then_inc(tr_act, 1)
                for v_no, (j, d, b, v) in enumerate(visits()):
                    if not first_visit(d, b):
                        continue
                    act.wait_ge(o_full, i * 16 + v_no + 1)
                    act.copy(o_tok[:, b * GDV:(b + 1) * GDV], o_bank(d, v)[:, 0:GDV]).then_inc(o_act, 1)
                for q, b in enumerate(SECOND):
                    act.wait_ge(o_dve, i * 8 + q + 3)
                    act.activation(osq[:, :], o_tok[:, b * GDV:(b + 1) * GDV], ACT.Square,
                                   accum_out=ossq[:, b:b + 1]).then_inc(o_sq, 1)
                    act.wait_ge(o_sq, i * 8 + q + 1)
                act.wait_ge(o_stat, i + 1)
                act.activation(ossq[:, TB:2 * TB], ossq[:, TB:2 * TB], ACT.Sqrt).then_inc(o_sd, 1)
            for k in range(KC):
                act.wait_ge(oT_loaded, 16 if k < 4 else 32)
                act.copy(ahi[:, k * SEQ:(k + 1) * SEQ], xres[:, k * SEQ:(k + 1) * SEQ]).then_inc(a_hi, 1)
            with act.Fori(0, KC // 2) as i:
                for u in range(2):
                    j = i * 2 + u
                    act.wait_ge(gemm_done, j + C_WO + 3)
                    act.sem_inc(act_read, 1)
                    split_hi_next(i, C_WO, u)
                    act.wait_ge(x_out, j + 33)
                    act_square(act, j, 24, xres[:, ds(j * SEQ, SEQ)])
            act_stats(act, "rms2")
            act_rms(act, "rms2", ahi, SEQ, 0, lambda k: gains[:, 16 + k:17 + k], lambda k: mod(24 + k, 0), a_lo, 32)
            n = C_MLP
            for g in range(MLP_GROUPS):
                with act.Fori(0, KC // 2) as i:
                    for u in range(2):
                        j = i * 2 + u
                        act.wait_ge(gemm_done, j + n + 3)
                        act.wait_ge(sq_done, j + g * KC + 1)
                        act.activation(relu[:, :], G[u], ACT.Relu).then_inc(relu_done, 1)
                        act.wait_ge(relu_done, j + g * KC + 1)
                        act.sem_inc(act_read, 1)
                        split_hi_next(i, n, u)
                        act.wait_ge(sq_done, j + g * KC + 2)
                        act.copy(hhi[:, ds(j * SEQ, SEQ)], sqr[:, :]).then_inc(m_hi, 1)
                n += KC
                def down(i, u):
                    j = i * 2 + u
                    act.wait_ge(gemm_done, j + n + 3)
                    act.sem_inc(act_read, 1)
                    if not isinstance(i, int):
                        split_hi_next(i, n, u)
                    if g == MLP_GROUPS - 1:
                        act.wait_ge(x_out, j + 41 + 24)
                        act_square(act, j, 32, xres[:, ds(j * SEQ, SEQ)])

                peeled(act, g == MLP_GROUPS - 1, down)
                n += KC
            act_stats(act, "rmsf")
            for k in range(KC):
                u = k % 2
                act.wait_ge(n_mul, NORMS["rmsf"]["mu"] + k + 1)
                if k >= 2:
                    act.wait_ge(out_T, k - 1)
                act.activation(aff[:, u * SEQ:(u + 1) * SEQ], cent[:, u * SEQ:(u + 1) * SEQ], ACT.Identity,
                               scale=vcol(2, 48 + k)).then_inc(n_aff, 1)

        @block.vector
        def _(dve):
            dve.sem_inc(w_lo, 2)
            dve.sem_inc(dve_read, 2)
            dve.sem_inc(pt_dve, 1)
            for k in range(KC):
                dve.wait_ge(a_hi, k + 1)
                dve.wait_ge(xT_copied, k + 1)
                dve.tensor_tensor(alo[:, k * SEQ:(k + 1) * SEQ], xres[:, k * SEQ:(k + 1) * SEQ],
                                  ahi[:, k * SEQ:(k + 1) * SEQ].bitcast(F32), ALU.subtract).then_inc(a_lo, 1)
            dve.wait_ge(small_loaded, 16 * 3)
            dve.tensor_copy(small[0:NHEAD, 1:2], relx[:, NREL - 1:NREL]).then_inc(rel_ready, 1)
            dve.memset(relx[:, NREL:512], 0.0).then_inc(rel_ready, 1)
            dve.wait_ge(rel_ready, 2)
            dve.tensor_scalar(relx[:, 0:NREL], relx[:, 0:NREL], small[0:NHEAD, 1:2], None,
                              ALU.subtract).then_inc(rel_ready, 1)
            split_lo(0, 0)
            L = lambda s: lf[:, s * SEQ:(s + 1) * SEQ]
            dve.wait_ge(f_full, 1)
            dve.wait_ge(f_act, 1)
            dve.tensor_scalar(L(2), YP[0:NHEAD, :], small[0:NHEAD, 0:1], 0.0, ALU.add, ALU.min).then_inc(f_dve, 1)
            dve.wait_ge(f_act, 3)
            dve.wait_ge(f_dve, 1)
            dve.tensor_tensor(L(3), L(2), L(0), ALU.subtract).then_inc(f_dve, 1)
            dve.memset(L(1), 1.0).then_inc(f_dve, 1)
            dve.wait_ge(f_dve, 3)
            dve.tensor_tensor_scan(L(0), L(1), L(3), 0.0, ALU.mult, ALU.add).then_inc(f_dve, 1)
            dve.wait_ge(f_dve, 4)
            cl = lambda r: cumLs[:, r * SEQ:(r + 1) * SEQ]
            cr = lambda r: cumRs[:, r * SEQ:(r + 1) * SEQ]
            dve.memset(cumLs[:, 0:3 * SEQ], 1.0).then_inc(cum_ready, 1)
            dve.memset(cumRs[:, 3 * SEQ:6 * SEQ], 1.0).then_inc(cum_ready, 1)
            ncum = 2
            src = L(0)
            for r in range(3):
                dve.tensor_copy(cl(3 + r), src).then_inc(cum_ready, 1)
                ncum += 1
                dve.wait_ge(cum_ready, ncum)
                dve.tensor_scalar(cr(r), cl(3 + r), -1.0, None, ALU.mult).then_inc(cum_ready, 1)
                ncum += 1
                if r < 2:
                    dst = L(2 + r)
                    dve.tensor_tensor(dst, src, cl(3 + r), ALU.subtract).then_inc(cum_ready, 1)
                    ncum += 1
                    dve.wait_ge(cum_ready, ncum)
                    src = dst
            for m in range(NS):
                lo_side(dve, 0, 0, m)
                dve_side(dve, 0, 0, m, SETUP_BANKS[m % 2])
            dve.wait_ge(rel_done, 2)
            dve.memset(relT[0:64, :].rearrange("p (h n) -> p h n", n=256)[:, :, 192:256], NEG).then_inc(rel_done, 1)
            dve_max(dve, 0, 0, 0)
            with dve.Fori(0, PAIRS - 1) as i:
                for half in range(2):
                    dve_attention(dve, half, i, False)
            dve_attention(dve, 0, PAIRS - 1, False)
            dve_attention(dve, 1, PAIRS - 1, True)
            dve.sem_inc(dve_read, C_WOUT)
            dve.wait_ge(gemm_done, C_WOUT + 2)
            split_lo(C_WOUT + 1, 1)
            for k in range(KC):
                dve.wait_ge(a_hi, KC + k + 1)
                dve.tensor_tensor(alo[:, k * SEQ:(k + 1) * SEQ], xres[:, k * SEQ:(k + 1) * SEQ],
                                  ahi[:, k * SEQ:(k + 1) * SEQ].bitcast(F32), ALU.subtract).then_inc(a_lo, 1)
            with dve.Fori(0, KC // 2) as i:
                for u in range(2):
                    j = i * 2 + u
                    dve.wait_ge(gemm_done, j + C_WOUT + 3)
                    dve.wait_ge(xs_loaded, j * 16 + 16)
                    dve.scalar_tensor_tensor(out=xres[:, ds(j * SEQ, SEQ)], in0=xs[:, :], scalar=ALPHA, in1=G[u],
                                             op0=ALU.mult, op1=ALU.add).then_inc(x_out, 1)
                    dve.wait_ge(x_out, j + 1)
                    dve.sem_inc(dve_read, 1)
                    split_lo(j + C_WOUT + 2, u)
            dve_stats(dve, "ln1")
            with dve.Fori(0, KC // 2) as i:
                for u in range(2):
                    dve_scale(dve, "ln1", i * 2 + u, u)
                for u in range(2):
                    k = i * 2 + u
                    dve.wait_ge(a_hi, k + 17)
                    dve.tensor_tensor(alo[:, ds(k * SEQ, SEQ)], xres[:, ds(k * SEQ, SEQ)],
                                      ahi[:, ds(k * SEQ, SEQ)].bitcast(F32), ALU.subtract).then_inc(a_lo, 1)
            n = C_FFN
            for gi, (g0, gc) in enumerate(FFN_GROUPS):
                with dve.Fori(0, gc) as i:
                    for u, cv in enumerate((conv_v, conv_g)):
                        dve.wait_ge(conv_act, i * 2 + g0 * 2 + u + 1)
                        f = i + g0 + u * FCH
                        for back in (1, 2):
                            dve.scalar_tensor_tensor(out=cv[:, back:SEQ], in0=G[u][:, 0:SEQ - back],
                                                     scalar=vcol(0, f + (2 - back) * 44), in1=cv[:, back:SEQ],
                                                     op0=ALU.mult, op1=ALU.add).then_inc(conv_dve, 1)
                            dve.wait_ge(conv_dve, i * 4 + g0 * 4 + u * 2 + back)
                        dve.sem_inc(dve_read, 1)
                        split_lo(i * 2 + n + u + 2, u)
                    dve.wait_ge(gelu_done, i + g0 + 1)
                    dve.wait_ge(h_hi, i + g0 + 1)
                    dve.tensor_tensor(hidden[:, :], conv_v[:, :], gelu_g[:, :], ALU.mult).then_inc(h_mul, 1)
                    dve.wait_ge(h_hi, i + g0 + 2)
                    dve.tensor_tensor(hlo[:, ds(i * SEQ, SEQ)], hidden[:, :], hhi[:, ds(i * SEQ, SEQ)].bitcast(F32),
                                      ALU.subtract).then_inc(h_lo, 1)
                    dve.wait_ge(h_lo, i + g0 + 1)
                n += 2 * gc
                with dve.Fori(0, KC // 2) as i:
                    for u in range(2):
                        j = i * 2 + u
                        dve.wait_ge(gemm_done, j + n + 3)
                        xr = xres[:, ds(j * SEQ, SEQ)]
                        if gi == 0:
                            dve.scalar_tensor_tensor(out=xr, in0=xr, scalar=ALPHA, in1=G[u], op0=ALU.mult,
                                                     op1=ALU.add).then_inc(x_out, 1)
                        else:
                            dve.tensor_tensor(xr, xr, G[u], ALU.add).then_inc(x_out, 1)
                        dve.wait_ge(x_out, j + 8 * gi + 9)
                        dve.sem_inc(dve_read, 1)
                        split_lo(j + n + 2, u)
                n += KC
            dve_stats(dve, "ln2")
            dve.wait_ge(stat_act, NORMS["ln2"]["sa"] + 2)
            with dve.Fori(0, KC // 2) as i:
                for u in range(2):
                    k = i * 2 + u
                    dve.wait_ge(n_aff, k + NORMS["ln2"]["af"] + 1)
                    dve.tensor_tensor(cent[:, u * SEQ:(u + 1) * SEQ], xres[:, ds(k * SEQ, SEQ)], mean[:, :],
                                      ALU.subtract).then_inc(n_cent, 1)
                    dve_scale(dve, "ln2", k, u)
            mv = mods[:, :].rearrange("p (n two) -> p two n", two=2)
            for t, (who, n0, row) in enumerate(((0, 8, 32), (1, 8, 32), (0, 32, 40))):
                dve.scalar_tensor_tensor(out=gains[:, t * 8:(t + 1) * 8], in0=mv[:, who, n0:n0 + 8], scalar=1.0,
                                         in1=vecs[:, 2 * 96 + row:2 * 96 + row + 8], op0=ALU.add, op1=ALU.mult
                                         ).then_inc(gains_ready, 1)
            dve.sem_inc(ga_lo, 2)
            dve.wait_ge(ctx_full, 1)
            dve.tensor_scalar(cvar[:, :], BANK[6][:, 0:CTX], RMS_EPS, None, ALU.add).then_inc(ctx_st, 1)
            dve.wait_ge(ctx_sd, 1)
            dve.reciprocal(crs[:, :], csd[:, :]).then_inc(ctx_st, 1)
            dve.wait_ge(ctx_st, 2)
            dve.wait_ge(ctx_sq, 4)
            for k in range(KC + 1):
                if k < KC:
                    if k >= 2:
                        dve.wait_ge(cc_aff, k - 1)
                    dve.tensor_tensor(ccent[:, (k % 2) * CTX:(k % 2 + 1) * CTX], cxT[:, k * CTX:(k + 1) * CTX],
                                      crs[:, :], ALU.mult).then_inc(cc_mul, 1)
                if k >= 1:
                    q = k - 1
                    dve.wait_ge(ga_hi, q + 1)
                    dve.tensor_tensor(galo[:, q * TOK:q * TOK + CTX], caff[:, (q % 2) * CTX:(q % 2 + 1) * CTX],
                                      gahi[:, q * TOK:q * TOK + CTX].bitcast(F32), ALU.subtract).then_inc(ga_lo, 1)
            dve.wait_ge(wa1_hi, 1)
            dve.tensor_tensor(wa1lo[:, :], wa1raw[:, :], wa1hi[:, :].bitcast(F32), ALU.subtract).then_inc(wa1_lo, 1)
            dve_stats(dve, "rms1")
            dve_rms(dve, "rms1", gahi, galo, TOK, CTX, ga_hi, KC, ga_lo)
            dve.sem_inc(o_gated, 2)
            dve.sem_inc(o_dve, 2)
            dve.wait_ge(masks_ready, 1)
            with dve.Fori(0, GH) as i:
                nz = i * 8
                for d in range(2):
                    bias = vecs[:, ds(i + 3 * 96 + 48 + d * GH, 1)]
                    cu = gcum[:, d * TOK:(d + 1) * TOK]
                    t1 = gex[:, TOK:2 * TOK]
                    o = d * 4
                    dve.wait_ge(z_act, i * 6 + d * 3 + 1)
                    dve.wait_ge(o_gated, i * 2 + 2)
                    dve.tensor_scalar(cu, GS[d][:, 0:TOK], bias, 0.0, ALU.add, ALU.min).then_inc(z_dve, 1)
                    Z1 = (1, 4)[d]
                    dve.wait_ge(z_act, i * 6 + d * 3 + 3)
                    dve.wait_ge(z_dve, nz + Z1)
                    dve.tensor_tensor(t1, cu, gex[:, 0:TOK], ALU.subtract).then_inc(z_dve, 1)
                    dve.wait_ge(z_dve, nz + Z1 + 1)
                    dve.tensor_tensor_scan(cu, restart[:, :], t1, 0.0, ALU.mult, ALU.add).then_inc(z_dve, 1)
                    dve.wait_ge(z_dve, nz + Z1 + 2)
                    dve.tensor_copy(tot[:, d * NCH:(d + 1) * NCH],
                                    cu.rearrange("p (c t) -> p c t", t=GCH)[:, :, GCH - 1]).then_inc(tots, 1)
                    if d == 1:
                        dve.wait_ge(tots, i * 2 + 2)
                        dve.tensor_tensor(cu, cu, t1, ALU.subtract).then_inc(gcum_ex, 1)
                        dve.wait_ge(gcum_ex, i + 1)

                def rest(d):
                    c3 = gcum[:, d * TOK:(d + 1) * TOK].rearrange("p (c t) -> p c t", t=GCH)
                    dve.tensor_tensor(c3, tot[:, d * NCH:(d + 1) * NCH].unsqueeze(2).broadcast_to([P, NCH, GCH]), c3,
                                      ALU.subtract).then_inc(z_dve, 1)

                def mul(e):
                    dst, src = (
                        (qd[:, 0:SEQ], qT[:, :]), (kn[:, 0:SEQ], kT[:, CTX:TOK]), (kd[:, 0:TOK], kT[:, :]),
                        (kd[:, TOK:2 * TOK], kT[:, :]), (qd[:, SEQ:2 * SEQ], qT[:, :]),
                        (kn[:, SEQ:2 * SEQ], kT[:, CTX:TOK]))[e]
                    w0 = 0 if e in (2, 3) else CTX
                    dve.wait_ge(gexp, i * 7 + e + 2)
                    dve.wait_ge(g_out, i * 6 + 2)
                    dve.tensor_tensor(dst, src, gex[:, (e % 2) * TOK + w0:(e % 2 + 1) * TOK], ALU.mult
                                      ).then_inc(gmul, 1)

                for j in range(6):
                    u = j % 2
                    n = i * 6 + C_GLA + j
                    dve.sem_inc(dve_read, 1)
                    if j < 5:
                        split_lo(n + 2, u)
                    if j == 1:
                        mul(0)
                        mul(1)
                        rest(0)
                        mul(2)
                    if j == 2:
                        mul(3)
                        rest(1)
                        mul(4)
                        mul(5)
                    if j == 5:
                        dve.wait_ge(gmul, i * 6 + 6)
                        dve.memset(att_f[:, :], 0.0).then_inc(att_zero, 1)
                        dve.memset(att_b[:, :], 0.0).then_inc(att_zero, 1)
                        for f in range(2):
                            for q, blks in enumerate(GROUPS):
                                g = 6 + f * 3 + q
                                dve.wait_ge(tr_full, i * 12 + g + 2)
                                dve.tensor_copy(
                                    g_v[:, :].rearrange("p (b v) -> p b v", v=GDV)[
                                        :, blks[0]:blks[0] + len(blks), f * P:(f + 1) * P],
                                    BANK[6 + g % 2][:, 0:len(blks) * P].rearrange("p (b v) -> p b v", v=P)
                                ).then_inc(tr_dve, 1)
                        split_lo(n + 2, u)
                for h in range(2):
                    dve.wait_ge(att_zero, i * 2 + 2)
                    dve.wait_ge(att_full, i * 2 + h + 1)
                    dve.memset(small[:, 2:3], 0.0)
                    for d, (a, m) in enumerate(((att_f, mask_f), (att_b, mask_b))):
                        dve.copy_predicated(a[:, h * 512:(h + 1) * 512], m[:, :], BANK[d][:, 0:512]).then_inc(att_set, 1)
                dve.wait_ge(att_set, i * 4 + 4)
                dve.tensor_tensor(att_f[:, :], att_f[:, :], att_b[:, :], ALU.add).then_inc(att_sum, 1)
                dve.wait_ge(gexp, i * 7 + 1)
                late = []
                for j in range(STEPS):
                    for d in range(2):
                        if j < STEPS - 1:
                            c = chunk_of(d, j)
                            dve.wait_ge(u_full, i * 38 + 2 * j + d + 1)
                            new = state[:, (d * 2 + (j + 1) % 2) * GDV:(d * 2 + (j + 1) % 2 + 1) * GDV]
                            old = state[:, (d * 2 + j % 2) * GDV:(d * 2 + j % 2 + 1) * GDV]
                            up = BANK[2 + 2 * d + j % 2][:, 0:GDV]
                            if j == 0:
                                dve.tensor_copy(new, up).then_inc(s_new, 1)
                            else:
                                dve.wait_ge(s_new, i * 38 + 2 * (j - 1) + d + 1)
                                dve.scalar_tensor_tensor(out=new, in0=old, scalar=etot[:, d * NCH + c:d * NCH + c + 1],
                                                         in1=up, op0=ALU.mult, op1=ALU.add).then_inc(s_new, 1)
                        for v_no, (jj, dd, b, v) in enumerate(visits()):
                            if (jj, dd) == (j - 1, d) and not first_visit(dd, b):
                                late.append((v_no, dd, b, v))
                        while late:
                            v_no, dd, b, v = late.pop(0)
                            dve_second(dve, i, v_no, dd, b, v)
                for v_no, (jj, dd, b, v) in enumerate(visits()):
                    if jj == STEPS - 1 and not first_visit(dd, b):
                        dve_second(dve, i, v_no, dd, b, v)
                dve.wait_ge(o_sq, i * 8 + 8)
                m = ossq[:, TB:2 * TB]
                dve.tensor_scalar(m, ossq[:, 0:TB], 1.0 / GDV, RMS_EPS, ALU.mult, ALU.add).then_inc(o_stat, 1)
                dve.wait_ge(o_sd, i + 1)
                dve.reciprocal(ossq[:, 2 * TB:3 * TB], m).then_inc(o_rec, 1)
                dve.wait_ge(o_rec, i + 1)
                for b in range(TB):
                    ob = o_tok[:, b * GDV:(b + 1) * GDV]
                    last = dve.tensor_scalar(ob, ob, ossq[:, 2 * TB + b:2 * TB + b + 1], None, ALU.mult)
                last.then_inc(o_norm, 1)
                for f in range(2):
                    dve.wait_ge(oT_full, i * 2 + f + 1)
                    rr = rT[:, f * SEQ:(f + 1) * SEQ]
                    dve.scalar_tensor_tensor(out=rr, in0=psum[:, f * SEQ:(f + 1) * SEQ],
                                             scalar=vecs[:, ds(i * 2 + 2 * 96 + 56 + f, 1)], in1=rr,
                                             op0=ALU.mult, op1=ALU.mult).then_inc(o_gated, 1)
            for k in range(KC):
                dve.wait_ge(a_hi, 3 * KC + k + 1)
                dve.tensor_tensor(alo[:, k * SEQ:(k + 1) * SEQ], xres[:, k * SEQ:(k + 1) * SEQ],
                                  ahi[:, k * SEQ:(k + 1) * SEQ].bitcast(F32), ALU.subtract).then_inc(a_lo, 1)
            with dve.Fori(0, KC // 2) as i:
                for u in range(2):
                    j = i * 2 + u
                    dve.wait_ge(gemm_done, j + C_WO + 3)
                    dve.wait_ge(xs_loaded, j * 16 + 16 * (KC + 1))
                    dve.scalar_tensor_tensor(out=xres[:, ds(j * SEQ, SEQ)], in0=G[u],
                                             scalar=mods[:, ds(j * 2 + 32, 1)], in1=xs[:, :],
                                             op0=ALU.mult, op1=ALU.add).then_inc(x_out, 1)
                    dve.wait_ge(x_out, j + 33)
                    dve.sem_inc(dve_read, 1)
                    split_lo(j + C_WO + 2, u)
            dve_stats(dve, "rms2")
            dve.sem_inc(a_lo, 2)
            dve_rms(dve, "rms2", ahi, alo, SEQ, 0, a_hi, 32, a_lo)
            n = C_MLP
            dve.sem_inc(sq_done, 1)
            dve.sem_inc(m_lo, 1)
            for g in range(MLP_GROUPS):
                with dve.Fori(0, KC // 2) as i:
                    for u in range(2):
                        j = i * 2 + u
                        dve.wait_ge(relu_done, j + g * KC + 1)
                        dve.sem_inc(dve_read, 1)
                        dve.wait_ge(m_lo, j + g * KC + 1)
                        dve.tensor_tensor(sqr[:, :], relu[:, :], relu[:, :], ALU.mult).then_inc(sq_done, 1)
                        split_lo(j + n + 2, u)
                        dve.wait_ge(m_hi, j + g * KC + 1)
                        dve.tensor_tensor(hlo[:, ds(j * SEQ, SEQ)], sqr[:, :], hhi[:, ds(j * SEQ, SEQ)].bitcast(F32),
                                          ALU.subtract).then_inc(m_lo, 1)
                n += KC
                def down(i, u):
                    j = i * 2 + u
                    dve.wait_ge(gemm_done, j + n + 3)
                    xr = xres[:, ds(j * SEQ, SEQ)]
                    dve.scalar_tensor_tensor(out=xr, in0=G[u], scalar=mods[:, ds(j * 2 + 80, 1)], in1=xr,
                                             op0=ALU.mult, op1=ALU.add).then_inc(x_out, 1)
                    dve.wait_ge(x_out, j + 41 + 8 * g)
                    dve.sem_inc(dve_read, 1)
                    if not isinstance(i, int):
                        split_lo(j + n + 2, u)

                peeled(dve, g == MLP_GROUPS - 1, down)
                n += KC
            dve_stats(dve, "rmsf")
            for k in range(KC + 1):
                if k < KC:
                    dve_scale(dve, "rmsf", k, k % 2)
                if k >= 1:
                    q = k - 1
                    dve.wait_ge(out_T, q + 1)
                    if q >= 2:
                        dve.wait_ge(out_stored[q % 2], 16 * (q // 2))
                    dve.tensor_copy(ostage[:, (q % 2) * SEQ:(q % 2 + 1) * SEQ], G[q % 2]).then_inc(out_copied, 1)


_INS = ["x", "w_in", "b_forget", "rel_bias", "w_out", "ln1_g", "ln1_b", "w_up", "conv_w", "conv_b", "w_down", "ln2_g",
        "ln2_b", "c_2", "ctx_2", "c_ctx_2", "ada_w_2", "ada_b_2", "norm1_g_2", "norm2_g_2", "mlp_w1_2", "mlp_w2_2",
        "gla_w_in_2", "gla_w_a1_2", "gla_w_a2_2", "gla_b_a_2", "gla_g_head_2", "gla_w_o_2", "final_g_2"]


def kernel(**inputs):
    import numpy as _np
    import concourse.bacc as _bacc
    from concourse import mybir as _mybir
    from concourse.bass_utils import run_bass_kernel_spmd as _run

    nc = _bacc.Bacc("TRN2", target_bir_lowering=False, num_devices=1)
    arrays, args = {}, []
    for name in _INS:
        a = _np.ascontiguousarray(inputs[name])
        arrays[f"in_{name}_dram"] = a
        args.append(nc.dram_tensor(f"in_{name}_dram", a.shape, _mybir.dt.from_np(a.dtype), kind="ExternalInput").ap())
    args.append(nc.dram_tensor("out_0_dram", (1, SEQ, D), _mybir.dt.float32, kind="ExternalOutput").ap())
    program(nc, *args)
    r = _run(nc, [arrays], core_ids=[0])
    return r.results[0]["out_0_dram"]
```
